# Optimizing a Trainium2 kernel written in Bass

```python
import jax, jax.numpy as jnp
from jax import lax
import numpy as np

D_MODEL = 1024
BATCH = 1
SEQ = 256
DEPTH = 2
DEC_BATCH = 1
DEC_SEQ = 2048
PAST_LEN = 256

GRID_W = 64
HEAD_DIM = 64
N_GROUPS = 4
GROUP_W = D_MODEL // N_GROUPS
A_HEADS = GROUP_W // HEAD_DIM
A_KV = max(1, A_HEADS // 2)
B_HEADS = GROUP_W // HEAD_DIM
C_HEADS = GROUP_W // HEAD_DIM
D_HEADS = GROUP_W // HEAD_DIM
WINDOW = 128
QBLK = 128
NA_ROWS = 8
NA_COLS = 16
NA_QCOLS = 16
NA_KCOLS = 32
NCB = GRID_W // NA_QCOLS
CHUNK = 64
ROPE_BASE = 10000.0
EPS = 1e-6
NEG = -1e30
LB_FLOOR = 1e-30
IN_WIDTHS = (GROUP_W, A_KV * HEAD_DIM, A_KV * HEAD_DIM, GROUP_W,
             GROUP_W, GROUP_W, GROUP_W, GROUP_W,
             GROUP_W, GROUP_W, GROUP_W, GROUP_W,
             GROUP_W, GROUP_W, GROUP_W, GROUP_W, GROUP_W)
IN_WIDTH = sum(IN_WIDTHS)

kernel_name = 'hybrid_diffusion_parallel_heads_step'

def rmsnorm(x, g):
    x32 = x.astype(jnp.float32)
    y = x32 * lax.rsqrt(jnp.mean(x32 * x32, axis=-1, keepdims=True) + EPS)
    return (y * g.astype(jnp.float32)).astype(x.dtype)

def adaln(cvec, w, b):
    m = jax.nn.silu(cvec) @ w + b
    return jnp.split(m, 3, axis=-1)

def rope_2d(x):
    bsz, slen, nh, hd = x.shape
    t = jnp.arange(slen)
    half = hd // 2
    nf = half // 2
    freqs = ROPE_BASE ** (-jnp.arange(nf, dtype=jnp.float32) / nf)

    def rot(xa, pos):
        ang = pos.astype(jnp.float32)[:, None] * freqs[None, :]
        cos = jnp.cos(ang)[None, :, None, :]
        sin = jnp.sin(ang)[None, :, None, :]
        x1, x2 = xa[..., :nf], xa[..., nf:]
        return jnp.concatenate([x1 * cos - x2 * sin, x2 * cos + x1 * sin], axis=-1)

    x32 = x.astype(jnp.float32)
    out = jnp.concatenate([rot(x32[..., :half], t // GRID_W), rot(x32[..., half:], t % GRID_W)], axis=-1)
    return out.astype(x.dtype)

def split_branches(h, w_in):
    bsz, slen = h.shape[:2]
    parts = jnp.split(h @ w_in, np.cumsum(IN_WIDTHS)[:-1].tolist(), axis=-1)
    return [p.reshape(bsz, slen, -1, HEAD_DIM) for p in parts]

def finish(x, outs, gates, w_out, g_post, gate_mod):
    bsz, slen = x.shape[:2]
    mixed = jnp.concatenate(
        [(o.astype(x.dtype) * jax.nn.silu(g)).reshape(bsz, slen, GROUP_W) for o, g in zip(outs, gates)], axis=-1)
    return x + gate_mod * rmsnorm(mixed @ w_out, g_post)

def dense_attn(q, k, v, sink):
    bsz, slen, nh, hd = q.shape
    nkv = k.shape[2]
    grp = nh // nkv
    nb = slen // QBLK
    nk = k.shape[1]
    qb = jnp.moveaxis(q.reshape(bsz, nb, QBLK, nkv, grp, hd), 1, 0)

    def block(qi):
        s = jnp.einsum('bqkgd,bskd->bkgqs', qi, k, preferred_element_type=jnp.float32) * hd ** -0.5
        if sink is not None:
            sk = jnp.broadcast_to(sink.astype(jnp.float32).reshape(1, nkv, grp, 1, 1), s.shape[:-1] + (1,))
            s = jnp.concatenate([s, sk], axis=-1)
        p = jax.nn.softmax(s, axis=-1)[..., :nk].astype(v.dtype)
        return jnp.einsum('bkgqs,bskd->bqkgd', p, v)

    o = lax.map(block, qb)
    return jnp.moveaxis(o, 0, 1).reshape(bsz, slen, nh, hd)

def window_attn(q, k, v, k_ctx, v_ctx, sink):
    bsz, slen, nh, hd = q.shape
    nkv = k.shape[2]
    grp = nh // nkv
    nb = slen // QBLK
    qb = q.reshape(bsz, nb, QBLK, nkv, grp, hd)

    def band(t):
        tp = jnp.pad(t, ((0, 0), (QBLK, QBLK), (0, 0), (0, 0))).reshape(bsz, nb + 2, QBLK, nkv, hd)
        return jnp.concatenate([tp[:, :-2], tp[:, 1:-1], tp[:, 2:]], axis=2)

    kb, vb = band(k), band(v)
    blk = np.arange(nb)[:, None]
    qpos = blk * QBLK + np.arange(QBLK)[None, :]
    kpos = (blk - 1) * QBLK + np.arange(3 * QBLK)[None, :]
    mask = ((kpos[:, None, :] >= 0) & (kpos[:, None, :] < slen)
            & (np.abs(qpos[:, :, None] - kpos[:, None, :]) <= WINDOW))
    scale = hd ** -0.5
    s_loc = jnp.einsum('bnqkgd,bnskd->bnkgqs', qb, kb, preferred_element_type=jnp.float32) * scale
    s_loc = jnp.where(mask[None, :, None, None], s_loc, NEG)
    s_ctx = jnp.einsum('bnqkgd,bskd->bnkgqs', qb, k_ctx, preferred_element_type=jnp.float32) * scale
    sk = jnp.broadcast_to(sink.astype(jnp.float32).reshape(1, 1, nkv, grp, 1, 1), s_loc.shape[:-1] + (1,))
    p = jax.nn.softmax(jnp.concatenate([s_loc, s_ctx, sk], axis=-1), axis=-1).astype(v.dtype)
    nloc = 3 * QBLK
    nctx = k_ctx.shape[1]
    o = (jnp.einsum('bnkgqs,bnskd->bnqkgd', p[..., :nloc], vb)
         + jnp.einsum('bnkgqs,bskd->bnqkgd', p[..., nloc:nloc + nctx], v_ctx))
    return o.reshape(bsz, slen, nh, hd)

def neighborhood_attn(q, k, v, k_ctx, v_ctx, rpb):
    bsz, slen, nh, hd = q.shape
    rows = slen // GRID_W
    wr = min(NA_ROWS, rows)
    r = np.arange(rows)
    row_idx = np.clip(r - wr // 2, 0, rows - wr)[:, None] + np.arange(wr)[None, :]
    kcol0 = np.clip(np.arange(NCB) * NA_QCOLS - (NA_KCOLS - NA_QCOLS) // 2, 0, GRID_W - NA_KCOLS)
    col_idx = kcol0[:, None] + np.arange(NA_KCOLS)[None, :]
    qcol = np.arange(NCB)[:, None] * NA_QCOLS + np.arange(NA_QCOLS)[None, :]
    qws = np.clip(qcol - NA_COLS // 2, 0, GRID_W - NA_COLS)
    col_ok = ((col_idx[:, None, :] >= qws[:, :, None])
              & (col_idx[:, None, :] < qws[:, :, None] + NA_COLS))
    nkeys = wr * NA_KCOLS
    mask = np.broadcast_to(col_ok[:, :, None, :], (NCB, NA_QCOLS, wr, NA_KCOLS)).reshape(NCB, NA_QCOLS, nkeys)
    ri = (row_idx - r[:, None]) + NA_ROWS - 1
    ci = np.clip(col_idx[:, None, :] - qcol[:, :, None], -(NA_COLS - 1), NA_COLS - 1) + NA_COLS - 1
    bias = rpb.astype(jnp.float32)[:, ri[:, None, None, :, None], ci[None, :, :, None, :]]
    bias = jnp.transpose(bias.reshape(nh, rows, NCB, NA_QCOLS, nkeys), (1, 2, 0, 3, 4))

    def gather(t):
        t5 = t.reshape(bsz, rows, GRID_W, nh, hd)
        g = t5[:, row_idx[:, None, :, None], col_idx[None, :, None, :]]
        return g.reshape(bsz, rows, NCB, nkeys, nh, hd)

    kb, vb = gather(k), gather(v)
    qb = q.reshape(bsz, rows, NCB, NA_QCOLS, nh, hd)
    scale = hd ** -0.5
    s_loc = jnp.einsum('brcqhd,brckhd->brchqk', qb, kb, preferred_element_type=jnp.float32) * scale + bias[None]
    s_loc = jnp.where(mask[None, None, :, None], s_loc, NEG)
    s_ctx = jnp.einsum('brcqhd,bshd->brchqs', qb, k_ctx, preferred_element_type=jnp.float32) * scale
    p = jax.nn.softmax(jnp.concatenate([s_loc, s_ctx], axis=-1), axis=-1).astype(v.dtype)
    o = (jnp.einsum('brchqk,brckhd->brcqhd', p[..., :nkeys], vb)
         + jnp.einsum('brchqs,bshd->brcqhd', p[..., nkeys:], v_ctx))
    return o.reshape(bsz, slen, nh, hd)

def _chunks(t, nc):
    bsz, slen, nh, d = t.shape
    return jnp.moveaxis(t.astype(jnp.float32).reshape(bsz, nc, CHUNK, nh, d), 1, 0)

def retention_scan(q, k, v, log_gamma, s0):
    bsz, slen, nh, _ = q.shape
    nc = slen // CHUNK
    lg = log_gamma.astype(jnp.float32)
    idx = jnp.arange(CHUNK, dtype=jnp.float32)
    dist = idx[:, None] - idx[None, :]
    decay = jnp.where(dist >= 0, jnp.exp(jnp.maximum(dist, 0.0)[None] * lg[:, None, None]), 0.0)
    q_decay = jnp.exp((idx[:, None] + 1.0) * lg[None, :])
    k_decay = jnp.exp((CHUNK - 1.0 - idx)[:, None] * lg[None, :])
    chunk_decay = jnp.exp(CHUNK * lg)

    def step(state, inp):
        qc, kc, vc = inp
        scores = jnp.einsum('bqhd,bkhd->bhqk', qc, kc) * decay
        intra = jnp.einsum('bhqk,bkhe->bqhe', scores, vc)
        cross = jnp.einsum('bqhd,bhde->bqhe', qc, state) * q_decay[None, :, :, None]
        new = (state * chunk_decay[None, :, None, None]
               + jnp.einsum('bkhd,bkhe->bhde', kc * k_decay[None, :, :, None], vc))
        return new, intra + cross

    s_fin, o = lax.scan(step, s0.astype(jnp.float32), (_chunks(q, nc), _chunks(k, nc), _chunks(v, nc)))
    return jnp.moveaxis(o, 0, 1).reshape(bsz, slen, nh, v.shape[-1]), s_fin

def hgrn2_scan(q, log_f, k, v, s0):
    bsz, slen, nh, _ = q.shape
    nc = slen // CHUNK
    causal = jnp.tril(jnp.ones((CHUNK, CHUNK), dtype=bool))

    def step(state, inp):
        qc, lfc, kc, vc = inp
        b = jnp.cumsum(lfc, axis=1)
        diff = b[:, :, None] - b[:, None, :]
        w = jnp.where(causal[None, :, :, None, None], jnp.exp(jnp.minimum(diff, 0.0)), 0.0)
        attn = jnp.einsum('bihd,bjhd,bijhd->bhij', qc, kc, w)
        intra = jnp.einsum('bhij,bjhe->bihe', attn, vc)
        cross = jnp.einsum('bihd,bhde->bihe', qc * jnp.exp(b), state)
        b_last = b[:, -1]
        new = (state * jnp.exp(b_last)[..., None]
               + jnp.einsum('bjhd,bjhe->bhde', kc * jnp.exp(b_last[:, None] - b), vc))
        return new, intra + cross

    xs = (_chunks(q, nc), _chunks(log_f, nc), _chunks(k, nc), _chunks(v, nc))
    s_fin, o = lax.scan(step, s0.astype(jnp.float32), xs)
    return jnp.moveaxis(o, 0, 1).reshape(bsz, slen, nh, v.shape[-1]), s_fin

def retention_branch(q, k, v, log_gamma, s0_f, s0_b):
    k = k * HEAD_DIM ** -0.5
    o_f, s_f = retention_scan(q, k, v, log_gamma[0], s0_f)
    o_b, s_b = retention_scan(q[:, ::-1], k[:, ::-1], v[:, ::-1], log_gamma[1], s0_b)
    o = o_f + o_b[:, ::-1]
    mu = jnp.mean(o, axis=-1, keepdims=True)
    var = jnp.mean(jnp.square(o - mu), axis=-1, keepdims=True)
    o = (o - mu) * lax.rsqrt(var + EPS)
    return o, jnp.stack([s_f, s_b], axis=1)

def hgrn2_branch(q, z_f, z_b, v, lb, s0_f, s0_b):
    q = jax.nn.silu(q)

    def forget(z, lbd):
        lbd = jnp.maximum(lbd, LB_FLOOR)
        log_f = jnp.logaddexp(jnp.log(lbd), jnp.log1p(-lbd) + jax.nn.log_sigmoid(z.astype(jnp.float32)))
        return log_f, 1.0 - jnp.exp(log_f)

    lf_f, k_f = forget(z_f, lb[0])
    o_f, s_f = hgrn2_scan(q, lf_f, k_f, v, s0_f)
    lf_b, k_b = forget(z_b[:, ::-1], lb[1])
    o_b, s_b = hgrn2_scan(q[:, ::-1], lf_b, k_b, v[:, ::-1], s0_b)
    o = o_f + o_b[:, ::-1]
    o = o * lax.rsqrt(jnp.mean(o * o, axis=-1, keepdims=True) + EPS)
    return o, jnp.stack([s_f, s_b], axis=1)

def context_layer(x, c_ctx, w_ada_l, b_ada_l, g_pre_l, g_post_l, w_in_l, w_out_l, sink_l, log_gamma_l, lb_l):
    shift, scale, gate = adaln(c_ctx, w_ada_l, b_ada_l)
    h = rmsnorm(x, g_pre_l) * (1.0 + scale) + shift
    aq, ak, av, ag, bq, bk, bv, bg, cq, ck, cv, cg, dq, dzf, dzb, di, dg = split_branches(h, w_in_l)
    bsz = x.shape[0]
    zc = jnp.zeros((bsz, C_HEADS, HEAD_DIM, HEAD_DIM), jnp.float32)
    zd = jnp.zeros((bsz, D_HEADS, HEAD_DIM, HEAD_DIM), jnp.float32)
    o_a = dense_attn(aq, ak, av, sink_l)
    o_b = dense_attn(bq, bk, bv, None)
    o_c, s_c = retention_branch(cq, ck, cv, log_gamma_l, zc, zc)
    o_d, s_d = hgrn2_branch(dq, dzf, dzb, di, lb_l, zd, zd)
    x = finish(x, (o_a, o_b, o_c, o_d), (ag, bg, cg, dg), w_out_l, g_post_l, gate)
    return x, (ak, av, bk, bv, s_c, s_d)

def latent_layer(x, c, ca_k, ca_v, cb_k, cb_v, st_c, st_d, w_ada_l, b_ada_l, g_pre_l, g_post_l,
                 w_in_l, w_out_l, sink_l, rpb_l, log_gamma_l, lb_l):
    shift, scale, gate = [m[:, None, :] for m in adaln(c, w_ada_l, b_ada_l)]
    h = rmsnorm(x, g_pre_l) * (1.0 + scale) + shift
    aq, ak, av, ag, bq, bk, bv, bg, cq, ck, cv, cg, dq, dzf, dzb, di, dg = split_branches(h, w_in_l)
    o_a = window_attn(rope_2d(aq), rope_2d(ak), av, ca_k, ca_v, sink_l)
    o_b = neighborhood_attn(bq, bk, bv, cb_k, cb_v, rpb_l)
    o_c, _ = retention_branch(rope_2d(cq), rope_2d(ck), cv, log_gamma_l, st_c[:, 0], st_c[:, 1])
    o_d, _ = hgrn2_branch(dq, dzf, dzb, di, lb_l, st_d[:, 0], st_d[:, 1])
    return finish(x, (o_a, o_b, o_c, o_d), (ag, bg, cg, dg), w_out_l, g_post_l, gate)

def setup_inputs(seed: int = 0) -> dict:
    key = jax.random.key(seed)
    ks = jax.random.split(key, 20)
    nrm = jax.random.normal
    f32 = jnp.float32
    ret_init = jnp.log(2.0 ** (5.0 + jnp.arange(C_HEADS, dtype=f32)) - 1.0)
    return {
        'x_prompt': nrm(ks[0], (BATCH, SEQ, D_MODEL), f32),
        'x_sample': nrm(ks[1], (DEC_BATCH, DEC_SEQ, D_MODEL), f32),
        'c': nrm(ks[2], (DEC_BATCH, D_MODEL), f32),
        'cache_win_k': nrm(ks[3], (DEC_BATCH, DEPTH, PAST_LEN, A_KV, HEAD_DIM), f32),
        'cache_win_v': nrm(ks[4], (DEC_BATCH, DEPTH, PAST_LEN, A_KV, HEAD_DIM), f32),
        'cache_na_k': nrm(ks[5], (DEC_BATCH, DEPTH, PAST_LEN, B_HEADS, HEAD_DIM), f32),
        'cache_na_v': nrm(ks[6], (DEC_BATCH, DEPTH, PAST_LEN, B_HEADS, HEAD_DIM), f32),
        'state_ret': nrm(ks[7], (DEC_BATCH, DEPTH, 2, C_HEADS, HEAD_DIM, HEAD_DIM), f32),
        'state_hgrn': nrm(ks[8], (DEC_BATCH, DEPTH, 2, D_HEADS, HEAD_DIM, HEAD_DIM), f32),
        'c_ctx': nrm(ks[9], (D_MODEL,), f32),
        'w_ada': nrm(ks[10], (DEPTH, D_MODEL, 3 * D_MODEL), f32) * D_MODEL ** -0.5,
        'b_ada': nrm(ks[11], (DEPTH, 3 * D_MODEL), f32) * 0.02,
        'g_pre': 1.0 + 0.02 * nrm(ks[12], (DEPTH, D_MODEL), f32),
        'g_post': 1.0 + 0.02 * nrm(ks[13], (DEPTH, D_MODEL), f32),
        'w_in': nrm(ks[14], (DEPTH, D_MODEL, IN_WIDTH), f32) * D_MODEL ** -0.5,
        'w_out': nrm(ks[15], (DEPTH, D_MODEL, D_MODEL), f32) * D_MODEL ** -0.5,
        'attn_sink': nrm(ks[16], (DEPTH, A_HEADS), f32) * 0.5,
        'na_rpb': nrm(ks[17], (DEPTH, B_HEADS, 2 * NA_ROWS - 1, 2 * NA_COLS - 1), f32) * 0.1,
        'ret_decay_logit': ret_init[None, None, :] + 0.1 * nrm(ks[18], (DEPTH, 2, C_HEADS), f32),
        'hgrn_lb_logit': nrm(ks[19], (DEPTH, 2, D_HEADS * HEAD_DIM), f32) * 0.5,
    }

def reference(x_prompt, x_sample, c, cache_win_k, cache_win_v, cache_na_k, cache_na_v, state_ret, state_hgrn,
              c_ctx, w_ada, b_ada, g_pre, g_post, w_in, w_out, attn_sink, na_rpb, ret_decay_logit, hgrn_lb_logit):
    p_lb = jax.nn.softmax(hgrn_lb_logit.astype(jnp.float32), axis=0)
    lower_bounds = (jnp.cumsum(p_lb, axis=0) - p_lb[0:1]).reshape(DEPTH, 2, D_HEADS, HEAD_DIM)
    log_gammas = jax.nn.log_sigmoid(ret_decay_logit.astype(jnp.float32))

    x = x_prompt
    win_k, win_v, na_k, na_v, st_ret, st_hgrn = [], [], [], [], [], []
    for l in range(DEPTH):
        x, (ak, av, bk, bv, s_c, s_d) = context_layer(
            x, c_ctx, w_ada[l], b_ada[l], g_pre[l], g_post[l], w_in[l], w_out[l],
            attn_sink[l], log_gammas[l], lower_bounds[l])
        win_k.append(ak)
        win_v.append(av)
        na_k.append(bk)
        na_v.append(bv)
        st_ret.append(s_c)
        st_hgrn.append(s_d)
    y_prompt = x
    new_win_k = jnp.stack(win_k, axis=1)
    new_win_v = jnp.stack(win_v, axis=1)
    new_na_k = jnp.stack(na_k, axis=1)
    new_na_v = jnp.stack(na_v, axis=1)
    new_state_ret = jnp.stack(st_ret, axis=1)
    new_state_hgrn = jnp.stack(st_hgrn, axis=1)

    x = x_sample
    for l in range(DEPTH):
        x = latent_layer(
            x, c, cache_win_k[:, l], cache_win_v[:, l], cache_na_k[:, l], cache_na_v[:, l],
            state_ret[:, l], state_hgrn[:, l], w_ada[l], b_ada[l], g_pre[l], g_post[l], w_in[l], w_out[l],
            attn_sink[l], na_rpb[l], log_gammas[l], lower_bounds[l])
    y_sample = x
    return (y_prompt, y_sample, new_win_k, new_win_v, new_na_k, new_na_v, new_state_ret, new_state_hgrn)


_drawn_inputs = setup_inputs


def setup_inputs(seed=0):
    import zlib

    import numpy as np

    out = dict(_drawn_inputs(seed))
    spreads = {}
    factors = {'state_hgrn': 8.0, 'g_post': 3.558, 'attn_sink': 8.0, 'na_rpb': 8.0}
    for name, (base, spread) in spreads.items():
        noise = np.random.default_rng([zlib.crc32(name.encode()), seed]).standard_normal(out[name].shape)
        drawn = base * np.exp(spread * noise) if base else spread * noise
        out[name] = __import__('jax').numpy.asarray(drawn.astype(out[name].dtype))
    for name, factor in factors.items():
        out[name] = (out[name] * factor).astype(out[name].dtype)
    return out
```

```python
from contextlib import ExitStack

import numpy as np

import concourse.bass as bass
from concourse import mybir

F32 = mybir.dt.float32
BF16 = mybir.dt.bfloat16
ALU = mybir.AluOpType
ACT = mybir.ActivationFunctionType
AX_X = mybir.AxisListType.X

P = 128
D_MODEL = 1024
KC = D_MODEL // P
DEPTH = 2
CTX, LAT, PAST = 256, 2048, 256
CT = CTX // P
NT = (CTX + LAT) // P
HD = 64
HEADS = 4
GW = HEADS * HD
IN_W = 4096
GRP = 512
NG = IN_W // GRP
ROW_W = IN_W + 2 * GW
NP = NT // 2
GRID_W = 64
WINDOW = 128
NA_ROWS, NA_COLS = 8, 16
EPS = 1e-6
NEG = -1e30
LB_FLOOR = 1e-30
LN_SPLIT = 2.0 ** -50
LEVELS = 7
SLOTS = LEVELS - 1
AHEAD = 2

KV_AT = 384
SLOT_N = NT + PAST // P
MX, M2, NM, ES, D1, D2, DN, RD = range(8)
BIAS_PARTS = ([(0, r, 7 - r, 0) for r in range(2)] + [(1, r, 5 - r, 0) for r in range(2)]
              + [(2, r, 3, r) for r in range(2)] + [(3, r, 3 - r, 2) for r in range(2)]
              + [(4, r, 1 - r, 2) for r in range(2)])

C_AQ, C_AK, C_AV, C_AG = 0, 256, 384, 512
C_BQ, C_BK, C_BV, C_BG = 768, 1024, 1280, 1536
C_CQ, C_CK, C_CV, C_CG = 1792, 2048, 2304, 2560
C_DQ, C_LF, C_DG, C_DI, C_KD = 2816, 3072, 3584, 3840, 4096


def shape_constants():
    t = np.arange(P)
    low = (t[:, None] >= 0)
    before = t[:, None] < t[None, :]
    cols = {"ident": np.eye(P)}
    window = np.zeros((P, 3, 3 * P))
    for kind, off in enumerate((0, P, 2 * P)):
        dist = np.abs(t[:, None] + off - np.arange(3 * P)[None, :])
        window[:, kind] = np.where(dist <= WINDOW, 0.0, NEG)
    cols["window"] = window.reshape(P, -1)
    ahead = t[None, :] - t[:, None]
    cols["dist_f"] = np.maximum(ahead, 0)
    cols["dist_b"] = np.maximum(-ahead, 0)
    cols["keep_f"] = (ahead >= 0) * HD ** -0.5
    cols["keep_b"] = (ahead <= 0) * HD ** -0.5
    cols["row_f"] = np.broadcast_to(t[None, :] + 1.0, (P, P))
    cols["row_b"] = np.broadcast_to(P - t[None, :], (P, P))
    cols["col_f"] = (P - 1.0 - t)[:, None]
    cols["col_b"] = (t * 1.0)[:, None]
    sums_f, sums_b = np.zeros((P, 8, P)), np.zeros((P, 8, P))
    for lv in range(LEVELS):
        s = 2 ** lv
        for i in range(P):
            m = i // (2 * s) * 2 * s + s
            if i >= m:
                sums_f[m:i + 1, lv, i] = 1
                sums_b[m:i, lv, i] = 1
            else:
                sums_f[i + 1:m, lv, i] = 1
                sums_b[i:m, lv, i] = 1
    sums_f[:, 7] = t[:, None] <= t[None, :]
    sums_b[:, 7] = t[:, None] >= t[None, :]
    cols["sums_f"], cols["sums_b"] = sums_f.reshape(P, -1), sums_b.reshape(P, -1)
    cols["after"] = (t[:, None] > t[None, :])
    cols["before"] = before
    keep = np.zeros((P, 2 * SLOTS + 1, 64))
    j, i = t % 64, np.arange(64)
    for lv in range(SLOTS):
        s = 2 ** lv
        same = (j[:, None] // (2 * s)) == (i[None, :] // (2 * s))
        jh, ih = (j[:, None] // s) % 2, (i[None, :] // s) % 2
        keep[:, lv] = same & (jh == 0) & (ih == 1)
        keep[:, SLOTS + lv] = same & (jh == 1) & (ih == 0)
    keep[:, 2 * SLOTS] = j[:, None] == i[None, :]
    cols["keep"] = keep.reshape(P, -1)
    cols["ones"] = np.ones((P, 1))
    at, parts = {}, []
    n = 0
    for name, a in cols.items():
        a = np.asarray(a, np.float32)
        at[name] = (n, n + a.shape[1])
        n += a.shape[1]
        parts.append(a)
    table = np.ascontiguousarray(np.concatenate(parts, axis=1))
    nf = HD // 4
    freq = (np.float32(10000.0) ** (-np.arange(nf, dtype=np.float32) / np.float32(nf))).astype(np.float32)
    pos = np.arange(LAT)
    rope = np.zeros((CTX + LAT + PAST, 2, HD), np.float32)
    rope[:, 0] = 1.0
    for half, place in enumerate((pos // GRID_W, pos % GRID_W)):
        ang = (place.astype(np.float32)[:, None] * freq[None, :]).astype(np.float32)
        c, s = np.cos(ang), np.sin(ang)
        o = half * 2 * nf
        rope[CTX:CTX + LAT, 0, o:o + nf] = c
        rope[CTX:CTX + LAT, 0, o + nf:o + 2 * nf] = c
        rope[CTX:CTX + LAT, 1, o:o + nf] = -s
        rope[CTX:CTX + LAT, 1, o + nf:o + 2 * nf] = s
    return at, table, rope.reshape(-1, 2 * HD)


AT, TABLE, ROPE = shape_constants()


def made(n, units=0):
    return n * (units + AHEAD)


class Steps:

    def __init__(self, eng, sem, base):
        self.eng, self.sem, self.base, self.n = eng, sem, base, 0

    def mark(self, ins):
        ins.then_inc(self.sem, 1)
        self.n += 1

    def wait(self):
        self.eng.wait_ge(self.sem, self.base + self.n)


def build(nc, ins, outs):
    (x_all, cond_in, cwk, cwv, cnk, cnv, st_ret, st_hgrn, w_ada, b_ada, g_pre, g_post, w_in, w_out,
     sink_in, rpb_in, decay_in, lb_in, table_in, rope_in) = ins
    streams, out_wk, out_wv, out_nk, out_nv, out_ret, out_hgrn = outs

    rows = nc.dram_tensor("projected", (NT * P, ROW_W), F32, kind="Internal").ap()
    mixed = nc.dram_tensor("mixed", (NT * P, D_MODEL), F32, kind="Internal").ap()
    gate_row = nc.dram_tensor("gate_row", (2, D_MODEL), F32, kind="Internal").ap()
    skew = nc.dram_tensor("skew", (HEADS * 15 * 64 * 128,), F32, kind="Internal").ap()

    nc.disable_value_cache = True
    arena = ExitStack()
    arena.enter_context(nc.allow_non_contiguous_dma(reason="vectors of the model, a few thousand elements"))

    def sb(stack, name, shape, dt=F32):
        return stack.enter_context(nc.sbuf_tensor(name, shape, dt))

    def sem(name):
        return arena.enter_context(nc.semaphore(name))

    def pair(name):
        return [sem(f"{name}{b}") for b in range(2)]

    def skew_ap(offset, pattern):
        return bass.AP(tensor=skew.tensor, offset=offset, ap=pattern)

    ident = sb(arena, "ident", [P, P])
    eps = sb(arena, "eps", [P, 1])
    ones = sb(arena, "ones", [P, 1])
    lbd = sb(arena, "lbd", [P, DEPTH, 2 * GW])
    oml = sb(arena, "oml", [P, DEPTH, 2 * GW])
    cond = sb(arena, "cond", [P, KC, 2])
    cond_e = sb(arena, "cond_e", [P, KC, 2])
    mod = sb(arena, "mod", [P, 3 * KC, 2])
    lbd_l = sb(arena, "lbd_l", [P, 2 * GW])
    oml_l = sb(arena, "oml_l", [P, 2 * GW])
    mod_w = sb(arena, "mod_w", [P, 5 * KC])
    stat = sb(arena, "stat", [P, 2, 8])
    ps = arena.enter_context(nc.psum_tensor("ps", [P, 8, GRP], F32))

    STAGES = 7
    (MODULATE, PROJECT, WIN, NEI, RET, HGRN, OUTPUT) = range(STAGES)

    with ExitStack() as s:
        w_sb = sb(s, "w_sb", [P, KC, IN_W])
        with ExitStack() as s2:
            wa = sb(s2, "wa", [P, 2, KC, 3 * P])
            lb_raw = sb(s2, "lb_raw", [P, DEPTH, 2 * GW])
        xt = sb(s, "xt", [P, 2, D_MODEL])
        hT = sb(s, "hT", [P, 2, KC, P])
        row_t = sb(s, "row_t", [P, 2, ROW_W])
        e_t = sb(s, "e_t", [P, 3, GRP])
        sq_junk = sb(s, "sq_junk", [P, D_MODEL], BF16)
    with ExitStack() as s:
        wo_sb = sb(s, "wo_sb", [P, KC, D_MODEL])
        gp_sb = sb(s, "gp_sb", [P, 2, D_MODEL])
        mx_t = sb(s, "mx_t", [P, 2, D_MODEL])
        xo_t = sb(s, "xo_t", [P, 2, D_MODEL])
        mT = sb(s, "mT", [P, 2, KC, P])
        y_t = sb(s, "y_t", [P, 2, D_MODEL])

    class Group:
        pass

    def attention(s, name, near, nkv, cq, ck, cv, cg, cache_k, cache_v, col):
        a = Group()
        a.near, a.nkv, a.cq, a.ck, a.cv, a.cg, a.col = near, nkv, cq, ck, cv, cg, col
        a.cache_k, a.cache_v = cache_k, cache_v
        a.kT = sb(s, f"{name}_kT", [HD, nkv, SLOT_N * P])
        a.v = sb(s, f"{name}_v", [P, SLOT_N, nkv * HD])
        a.k_raw = sb(s, f"{name}_k_raw", [P, 2, nkv * HD])
        a.q_raw = sb(s, f"{name}_q_raw", [P, 2, GW])
        a.gate_t = sb(s, f"{name}_gate_t", [P, 2, GW])
        a.out_t = sb(s, f"{name}_out_t", [P, 2, GW])
        a.qT = sb(s, f"{name}_qT", [HD, 2, HEADS, P])
        a.sl = sb(s, f"{name}_sl", [P, 2, near * P])
        a.e = sb(s, f"{name}_e", [P, 2, (near + CT) * P])
        a.pT = sb(s, f"{name}_pT", [P, 2, near + CT, P])
        a.st = sb(s, f"{name}_st", [P, 2, 8, HEADS])
        return a

    with ExitStack() as s:
        win = attention(s, "win", 3, 2, C_AQ, C_AK, C_AV, C_AG, cwk, cwv, 0)
        win_mask = sb(s, "win_mask", [P, 3, 3 * P])
        sink = sb(s, "sink", [P, HEADS])
        win.k_rope = sb(s, "win_k_rope", [P, 2, 2 * HD])
        win.q_rope = sb(s, "win_q_rope", [P, 2, GW])
        win.rope_t = sb(s, "win_rope_t", [P, 2, 2 * HD])
        win.rope_q = sb(s, "win_rope_q", [P, 2, 2 * HD])
        win.rot_tmp = sb(s, "win_rot_tmp", [P, GW])
    with ExitStack() as s:
        nei = attention(s, "nei", 5, 4, C_BQ, C_BK, C_BV, C_BG, cnk, cnv, GW)
        nei_bias = sb(s, "nei_bias", [P, 5, HEADS, 5 * P])
    def scan(s, name, stage, stream_w, back_w, col):
        a = Group()
        a.name, a.stage, a.col = name, stage, col
        a.raw = sb(s, f"{name}_raw", [P, 2, stream_w])
        a.braw = sb(s, f"{name}_braw", [P, 2, back_w])
        a.kd = sb(s, f"{name}_kd", [P, 2, GW])
        a.sf = sb(s, f"{name}_sf", [P, 2, P])
        a.sb = sb(s, f"{name}_sb", [P, 2, P])
        a.sb_all = sb(s, f"{name}_sb_all", [P, NT, P])
        a.sb_at = sb(s, f"{name}_sb_at", [P, 2, P])
        a.out_t = sb(s, f"{name}_out_t", [P, 2, GW])
        a.o_c = sb(s, f"{name}_o_c", [P, 2, GW])
        a.o_sq = sb(s, f"{name}_o_sq", [P, 2, GW])
        a.st = sb(s, f"{name}_st", [P, 2, 4, HEADS])
        return a

    with ExitStack() as s:
        ret = scan(s, "ret", RET, 4 * GW, 2 * GW, 2 * GW)
        ret.rope_t = sb(s, "ret_rope_t", [P, 2, 2 * HD])
        ret.rope_b = sb(s, "ret_rope_b", [P, 2, 2 * HD])
        ret.tmp = sb(s, "ret_tmp", [P, 2 * GW])
        ret.x = sb(s, "ret_x", [P, 2, 2 * GW])
        ret.xT = sb(s, "ret_xT", [P, 2, 4, P])
        ret.qd = sb(s, "ret_qd", [P, 2, 2, 2, P])
        ret.p = sb(s, "ret_p", [P, 2, 2, 2, P])
        lg = sb(s, "lg", [P, 2 * HEADS])
        lg_t = sb(s, "lg_t", [P, 3, 2 * HEADS])
        lgp = sb(s, "lgp", [P, 2, 2])
        pair_decay = sb(s, "pair_decay", [P, 2, 2])
        key_decay = sb(s, "key_decay", [P, 2, HEADS])
        row_decay = sb(s, "row_decay", [P, 2, 2, P])
        dmat = sb(s, "dmat", [P, 2, 2, P])
        dtab = sb(s, "dtab", [P, 6, P])
        dcol = sb(s, "dcol", [P, 2])
        dtmp = sb(s, "dtmp", [P, 2, P])
    with ExitStack() as s:
        hg = scan(s, "hg", HGRN, 7 * GW, 3 * GW, 3 * GW)
        hg.ed = sb(s, "hg_ed", [P, 2, GW + 2])
        hg.xT = sb(s, "hg_xT", [P, 2, 6, P])
        hg.d = sb(s, "hg_d", [P, 2, 8, P])
        hg.q = sb(s, "hg_q", [P, 2, 2, 8, P])
        hg.k = sb(s, "hg_k", [P, 2, 2, LEVELS, P])
        hg.w = sb(s, "hg_w", [P, 2 * SLOTS + 1, 64])
        hg.tc = sb(s, "hg_tc", [P, 2, 64])
        hg.p = sb(s, "hg_p", [P, 2, P])
        sums = sb(s, "sums", [P, 2, 8, P])
        keep = sb(s, "keep", [P, 2 * SLOTS + 1, 64])
        past = sb(s, "past", [P, 2, P])
    with ExitStack() as s:
        neg_t = sb(s, "neg_t", [P, 15 * HEADS * 64])

    passed = sem("passed")
    consts_in = sem("consts_in")
    lb_loaded = sem("lb_loaded")
    setup = sem("setup")
    setup_act = sem("setup_act")
    x_copied = sem("x_copied")
    stage_done = sem("stage_done")
    wa_in, wa_used = pair("wa_in"), sem("wa_used")
    modw_in = sem("modw_in")
    ada_done = sem("ada_done")
    mod_ready = sem("mod_ready")
    gate_out = sem("gate_out")
    mod_step = sem("mod_step")
    w_loaded = [sem(f"w_loaded{g}") for g in range(NG)]
    x_in, x_normed = pair("x_in"), sem("x_normed")
    act_step, dve_step = sem("act_step"), sem("dve_step")
    rstd_ready = sem("rstd_ready")
    x_turned = sem("x_turned")
    h_act, h_dve = sem("h_act"), sem("h_dve")
    proj_done = sem("proj_done")
    exp_ready = sem("exp_ready")
    ln_in, ln_out = sem("ln_in"), sem("ln_out")
    out_g = [sem(f"out_g{g}") for g in range(NG)]
    bounds_ready = sem("bounds_ready")
    row_stored = pair("row_stored")
    emit_act, emit_dve = sem("emit_act"), sem("emit_dve")
    kv_saved = sem("kv_saved")
    wo_in = sem("wo_in")
    mx_in, xo_in, mx_turned = pair("mx_in"), pair("xo_in"), sem("mx_turned")
    mT_act, mT_dve = sem("mT_act"), sem("mT_dve")
    y_done, yr_ready, y_ready, y_stored = sem("y_done"), sem("yr_ready"), sem("y_ready"), pair("y_stored")
    o_act, o_dve = sem("o_act"), sem("o_dve")

    def gate(eng, l, stage):
        settled(eng)
        eng.drain().then_inc(stage_done, 1)
        eng.wait_ge(stage_done, (l * STAGES + stage + 1) * 5)
        settled(eng)

    def settled(eng):
        eng.sem_inc(passed, 1)

    win.stage, nei.stage = WIN, NEI
    both_v_in, both_stored = pair("v_in"), pair("attention_stored")
    both = [sem(x) for x in ("k_turned", "k_out", "q_turned", "q_ready", "s_done", "nm_ready", "e_ready", "p_turned",
                             "pt_act", "pt_dve", "pv_done", "attention_ready", "s_step")]
    win.lay, nei.lay = (lambda l: 2 * l), (lambda l: 2 * l + 1)
    for name, a in (("win", win), ("nei", nei)):
        a.k_in, a.q_in = pair(f"{name}_k_in"), pair(f"{name}_q_in")
        a.v_in, a.stored = both_v_in, both_stored
        (a.k_turned, a.k_out, a.q_turned, a.q_ready, a.s_done, a.nm_ready, a.e_ready, a.p_turned, a.pt_act, a.pt_dve,
         a.pv_done, a.out_ready, a.s_step) = both
        a.f_step = sem(f"{name}_f_step")
    win.k_rot, win.q_rot, win.k_step, win.q_step = (sem(f"win_{x}") for x in ("k_rot", "q_rot", "k_step", "q_step"))
    ret.lay, hg.lay = win.lay, nei.lay
    SHARED = ("bk_ready", "bkv_done", "bs_ready", "xT_ready", "sb_ready", "kf_ready", "kv_done", "sf_ready",
              "sq_ready", "var_ready", "r_ready", "out_ready", "n_step", "s_in", "s_saved", "ready")
    shared = [sem(f"scan_{x}") for x in SHARED]
    ret.stored = hg.stored = pair("scan_stored")
    for a in (ret, hg):
        (a.bk_ready, a.bkv_done, a.bs_ready, a.xT_ready, a.sb_ready, a.kf_ready, a.kv_done, a.sf_ready,
         a.sq_ready, a.var_ready, a.r_ready, a.out_ready, a.n_step, a.s_in, a.s_saved, a.ready) = shared
        a.b_in, a.raw_in = pair(f"{a.name}_b_in"), pair(f"{a.name}_raw_in")
        a.tab_in, a.turned, a.p_done, a.p_ready, a.o_done, a.x_ready, a.f_step = (
            sem(f"{a.name}_{x}") for x in ("tab_in", "turned", "p_done", "p_ready", "o_done", "x_ready", "f_step"))
    ret.b_step, ret.x_step, ret.qd_ready = sem("ret_b_step"), sem("ret_x_step"), sem("ret_qd_ready")
    hg.b_step = sem("hg_b_step")
    hg.f_turned, hg.f_exp, hg.e_done, hg.d_ready, hg.qk_ready, hg.tc_ready = (
        sem(f"hg_{x}") for x in ("f_turned", "f_exp", "e_done", "d_ready", "qk_ready", "tc_ready"))
    lg_step, lg_act, dm_step, states_clear = (sem(x) for x in ("lg_step", "lg_act", "dm_step", "states_clear"))
    mask_in, skew_in, bias_clear, neg_ready, skew_clear = (
        sem(x) for x in ("mask_in", "skew_in", "bias_clear", "neg_ready", "skew_clear"))

    OUT_BANK = (7, 0)

    def score_banks(p):
        return ps[:, 1 + 2 * p:3 + 2 * p, :].rearrange("p a n -> p (a n)")

    def w_par(b, h):
        return h % 2

    def attend(eng, a, first, score, turn, last):
        def both(i, kinds, base):
            units = [(i, b, h, kinds[b], base[b]) for b in range(2) for h in range(HEADS)]
            for b in range(2):
                first(i, b)
            for n in range(len(units) + 2):
                if n < len(units):
                    score(*units[n])
                if 1 <= n <= len(units):
                    turn(*units[n - 1])
                if n >= 2 and last:
                    last(*units[n - 2])
        edge = a.near // 2
        top = CT + (NT - CT) - a.near
        both(0, (None, None), (0, 0))
        both(1, (0, 1), (CT, CT + max(0, 1 - edge)))
        with eng.Fori(2, NP - 1) as i:
            both(i, (edge, edge), (2 * i - edge, 2 * i + 1 - edge))
        last_kind = 2 * edge
        both(NP - 1, (last_kind - 1, last_kind), (min(top, NT - 2 - edge), top))

    def back_tile(i, b):
        return 1 - b if isinstance(i, int) and i == 0 else NT + 1 - 2 * i - b

    def backward(eng, unit):
        for b in range(2):
            unit(0, b, 0)
        with eng.Fori(1, NP) as i:
            for b in range(2):
                unit(i, b, 1)

    def state_ap(dram, l, direction):
        return [dram[bass.ds(l, 1), direction, 2 * g:2 * g + 2, :, :].rearrange("a h d e -> (a h d) e")
                for g in range(2)]

    def tok(t):
        return bass.ds(t * P, P)

    def tiles(eng, pre, post):
        pre(0, 0, 0)
        pre(0, 1, 0)
        post(0, 0, 0)
        pre(1, 0, 1)
        post(0, 1, 0)
        with eng.Fori(1, NP - 1) as i:
            pre(i, 1, 1)
            post(i, 0, 1)
            pre(i + 1, 0, 1)
            post(i, 1, 1)
        pre(NP - 1, 1, 1)
        post(NP - 1, 0, 1)
        post(NP - 1, 1, 1)

    block = arena.enter_context(nc.Block())

    @block.sync
    def _(sp):
        def cols(name, part=P):
            a, b = AT[name]
            return table_in[0:part, a:b]

        sp.dma_start(ident[:, :], cols("ident")).then_inc(consts_in, 16)
        sp.dma_start(cond[:, :, 0], cond_in[0, :].rearrange("(k p) -> p k", p=P)).then_inc(consts_in, 16)
        sp.dma_start(cond[:, :, 1], cond_in[1, :].rearrange("(k p) -> p k", p=P)).then_inc(consts_in, 16)
        sp.wait_ge(consts_in, 48)
        sp.dma_start(streams[0], x_all).then_inc(x_copied, 16)
        sp.wait_ge(x_copied, 16)
        sp.wait_ge(neg_ready, 1)
        sp.dma_start(skew.rearrange("(p n) -> p n", p=P), neg_t[:, :]).then_inc(skew_clear, 16)
        sp.wait_ge(skew_clear, 16)
        sp.dma_start(lb_raw[:, 0, :], lb_in[0:1, :].broadcast_to([P, 2 * GW])).then_inc(lb_loaded, 16)
        for d in range(1, DEPTH):
            sp.dma_start(lb_raw[:, d, :], lb_in[d:d + 1, :].broadcast_to([P, 2 * GW])).then_inc(lb_loaded, 16)
        with sp.Fori(0, DEPTH) as l:
            for part, at, n in ((b_ada, 0, 3 * KC), (g_pre, 3 * KC, KC), (g_post, 4 * KC, KC)):
                sp.dma_start(mod_w[:, at:at + n], part[bass.ds(l, 1), :].rearrange("a (n p) -> p (a n)", p=P)
                             ).then_inc(modw_in, 16)
            for n in range(KC):
                sp.wait_ge(wa_used, made(1, l * KC + n - 1))
                sp.dma_start(wa[:, n % 2], w_ada[bass.ds(l, 1), :, n * 3 * P:(n + 1) * 3 * P].rearrange(
                    "a (k p) n -> p (a k) n", p=P)).then_inc(wa_in[n % 2], 16)
            for g in range(NG):
                src = w_in[bass.ds(l, 1)].rearrange("a (k p) n -> p (a k) n", p=P)
                if g < NG - 1:
                    sp.dma_start(w_sb[:, :, g * GRP:(g + 1) * GRP], src[:, :, g * GRP:(g + 1) * GRP]
                                 ).then_inc(w_loaded[g], 16)
                else:
                    for at, frm in ((C_DG, IN_W - GW), (C_DI, IN_W - GRP)):
                        sp.dma_start(w_sb[:, :, at:at + GW], src[:, :, frm:frm + GW]).then_inc(w_loaded[g], 16)
            gate(sp, l, MODULATE)

            with sp.Fori(0, NP) as i:
                for b in range(2):
                    t = 2 * i + b
                    sp.wait_ge(x_turned, made(1, l * NT + t - 1))
                    sp.dma_start(xt[:, b], streams[bass.ds(l, 1), tok(t), :].rearrange("a p n -> p (a n)")
                                 ).then_inc(x_in[b], 16)
            gate(sp, l, PROJECT)
            for a in (win, nei):
                if a is win:
                    sp.dma_start(win_mask[:, :, :].rearrange("p a n -> p (a n)"), cols("window")).then_inc(mask_in, 16)
                    sp.dma_start(sink[:, :], sink_in[bass.ds(l, 1), :].broadcast_to([P, HEADS])).then_inc(mask_in, 16)
                    rpb = rpb_in[bass.ds(l, 1)].rearrange("a r c -> (a r) c")
                    inner = NA_COLS // 2
                    for q0, nq in [(q, 1) for q in range(inner)] + [(inner, GRID_W - 2 * inner + 1)] + \
                            [(q, 1) for q in range(GRID_W - inner + 1, GRID_W)]:
                        first = min(max(q0 - inner, 0), GRID_W - NA_COLS)
                        sp.dma_start(skew_ap(q0 * P + first - q0 + 63, [[64 * P, HEADS * 15], [P, nq], [1, NA_COLS]]),
                                     rpb[:, first - q0 + 15:first - q0 + 15 + NA_COLS].unsqueeze(1).broadcast_to(
                                         [HEADS * 15, nq, NA_COLS])).then_inc(skew_in, 16)
                    sp.wait_ge(skew_in, 16 * 2 * inner * (l + 1))
                    settled(sp)
                else:
                    sp.wait_ge(bias_clear, l + 1)
                    for kind, h0, r0, first_row in BIAS_PARTS:
                        for h in range(HEADS):
                            sp.dma_start(nei_bias[64 * h0:64 * h0 + 64, kind, h, first_row * 64:first_row * 64 + 512].rearrange(
                                "p (j n) -> p j n", n=64),
                                skew_ap((h * 15 + r0) * 64 * P + 63, [[P - 1, 64], [64 * P, NA_ROWS], [1, 64]])
                                ).then_inc(mask_in, 16)

                def load_kv(i, b, k_src, v_src, t):
                    sp.wait_ge(a.k_turned, made(1, a.lay(l) * SLOT_N + 2 * i + b - 1))
                    settled(sp)
                    sp.dma_start(a.k_raw[:, b], k_src).then_inc(a.k_in[b], 16)
                    if a is win:
                        sp.dma_start(a.rope_t[:, b], rope_in[tok(t), :]).then_inc(a.k_in[b], 16)
                    sp.dma_start(a.v[:, bass.ds(t, 1), :].rearrange("p a n -> p (a n)"), v_src).then_inc(a.v_in[b], 16)

                with sp.Fori(0, NP) as i:
                    for b in range(2):
                        t = 2 * i + b
                        load_kv(i, b, rows[tok(t), a.ck:a.ck + a.nkv * HD], rows[tok(t), a.cv:a.cv + a.nkv * HD], t)
                for b in range(2):
                    load_kv(NP, b, a.cache_k[bass.ds(l, 1), b * P:(b + 1) * P, :].rearrange("a p n -> p (a n)"),
                            a.cache_v[bass.ds(l, 1), b * P:(b + 1) * P, :].rearrange("a p n -> p (a n)"), NT + b)
                with sp.Fori(0, NP) as i:
                    for b in range(2):
                        t = 2 * i + b
                        sp.wait_ge(a.out_ready, made(1, a.lay(l) * NT + t - 1))
                        settled(sp)
                        sp.dma_start(a.q_raw[:, b], rows[tok(t), a.cq:a.cq + GW]).then_inc(a.q_in[b], 16)
                        sp.dma_start(a.gate_t[:, b], rows[tok(t), a.cg:a.cg + GW]).then_inc(a.q_in[b], 16)
                        if a is win:
                            sp.dma_start(a.rope_q[:, b], rope_in[tok(t), :]).then_inc(a.q_in[b], 16)
                gate(sp, l, a.stage)
            for a in (ret, hg):
                if a is ret:
                    sp.dma_start(lg[:, :], decay_in[bass.ds(l, 1), :].broadcast_to([P, 2 * HEADS])).then_inc(a.tab_in, 16)
                    for k, name in enumerate(("dist_f", "dist_b", "keep_f", "keep_b", "row_f", "row_b")):
                        sp.dma_start(dtab[:, k], cols(name)).then_inc(a.tab_in, 16)
                    for k, name in enumerate(("col_f", "col_b")):
                        sp.dma_start(dcol[:, k:k + 1], cols(name)).then_inc(a.tab_in, 16)
                else:
                    for k, name in enumerate(("sums_f", "sums_b")):
                        sp.dma_start(sums[:, k].rearrange("p s n -> p (s n)"), cols(name)).then_inc(a.tab_in, 16)
                    sp.dma_start(keep[:, :, :].rearrange("p s n -> p (s n)"), cols("keep")).then_inc(a.tab_in, 16)
                    for k, name in enumerate(("after", "before")):
                        sp.dma_start(past[:, k], cols(name)).then_inc(a.tab_in, 16)
                for d, state in enumerate((a.sf, a.sb)):
                    for g, src in enumerate(state_ap(st_ret if a is ret else st_hgrn, l, d)):
                        sp.dma_start(state[:, 1, g * HD:(g + 1) * HD], src).then_inc(a.s_in, 16)

                def load_back(i, b, c):
                    t = back_tile(i, b)
                    u = l * NT + 2 * i + b
                    v = a.lay(l) * NT + 2 * i + b
                    sp.wait_ge(a.bk_ready, made(1, v - 1))
                    sp.wait_ge(a.bkv_done, made(1, v - 1))
                    settled(sp)
                    if a is ret:
                        sp.dma_start(a.braw[:, b], rows[tok(t), C_CK:C_CK + 2 * GW]).then_inc(a.b_in[b], 16)
                        sp.dma_start(a.rope_b[:, b], rope_in[tok(t), :]).then_inc(a.b_in[b], 16)
                    else:
                        sp.dma_start(a.braw[:, b, 0:GW], rows[tok(t), C_LF + GW:C_LF + 2 * GW]).then_inc(a.b_in[b], 16)
                        sp.dma_start(a.braw[:, b, GW:2 * GW], rows[tok(t), C_DI:C_DI + GW]).then_inc(a.b_in[b], 16)
                        sp.dma_start(a.braw[:, b, 2 * GW:3 * GW], rows[tok(t), C_KD + GW:C_KD + 2 * GW]).then_inc(a.b_in[b], 16)

                backward(sp, load_back)
                with sp.Fori(0, NP) as i:
                    for b in range(2):
                        t = 2 * i + b
                        sp.wait_ge(a.out_ready, made(1, a.lay(l) * NT + t - 1))
                        sp.wait_ge(a.kv_done, made(1, a.lay(l) * NT + t - 1))
                        settled(sp)
                        if a is ret:
                            sp.dma_start(a.raw[:, b], rows[tok(t), C_CQ:C_CQ + 4 * GW]).then_inc(a.raw_in[b], 16)
                            sp.dma_start(a.rope_t[:, b], rope_in[tok(t), :]).then_inc(a.raw_in[b], 16)
                        else:
                            sp.dma_start(a.raw[:, b], rows[tok(t), C_DQ:C_DQ + 7 * GW]).then_inc(a.raw_in[b], 16)
                gate(sp, l, a.stage)
            sp.dma_start(wo_sb[:, :, :], w_out[bass.ds(l, 1)].rearrange("a (k p) n -> p (a k) n", p=P)
                         ).then_inc(wo_in, 16)
            for c in range(2):
                sp.dma_start(gp_sb[:, c], gate_row[c:c + 1, :].broadcast_to([P, D_MODEL])).then_inc(wo_in, 16)
            with sp.Fori(0, NP) as i:
                for b in range(2):
                    t = 2 * i + b
                    sp.wait_ge(mx_turned, made(1, l * NT + t - 1))
                    sp.dma_start(mx_t[:, b], mixed[tok(t), :]).then_inc(mx_in[b], 16)
                    sp.wait_ge(y_ready, made(1, l * NT + t - 1))
                    sp.dma_start(xo_t[:, b], streams[bass.ds(l, 1), tok(t), :].rearrange("a p n -> p (a n)")
                                 ).then_inc(xo_in[b], 16)
            gate(sp, l, OUTPUT)

    @block.gpsimd
    def _(pool):
        with pool.Fori(0, DEPTH) as l:
            pool.wait_ge(mod_ready, l + 1)
            settled(pool)
            for c in range(2):
                pool.dma_start(gate_row[c, :].rearrange("(k p) -> p k", p=P), mod[:, 2 * KC:3 * KC, c]
                               ).then_inc(gate_out, 16)
            pool.wait_ge(gate_out, 32 * (l + 1))
            settled(pool)
            gate(pool, l, MODULATE)
            with pool.Fori(0, NP) as i:
                for b in range(2):
                    t = 2 * i + b
                    for g in range(NG):
                        pool.wait_ge(out_g[g], made(1, l * NT + t + 1))
                    settled(pool)
                    pool.dma_start(rows[tok(t), :], row_t[:, b]).then_inc(row_stored[b], 16)
            for b in range(2):
                pool.wait_ge(row_stored[b], 16 * (l + 1) * NP)
            settled(pool)
            for dst, at, n in ((out_wk, C_AK, P), (out_wv, C_AV, P), (out_nk, C_BK, GW), (out_nv, C_BV, GW)):
                pool.dma_start(dst[bass.ds(l, 1)].rearrange("a t n -> t (a n)"), rows[0:CTX, at:at + n]
                               ).then_inc(kv_saved, 16)
            pool.wait_ge(kv_saved, 64 * (l + 1))
            settled(pool)
            gate(pool, l, PROJECT)
            for a in (win, nei):
                if a is nei:
                    nc.gpsimd.memset(nei_bias[:, :, :, :], NEG).then_inc(bias_clear, 1)
                with pool.Fori(0, NP) as i:
                    for b in range(2):
                        t = 2 * i + b
                        pool.wait_ge(a.out_ready, made(1, a.lay(l) * NT + t + 1))
                        settled(pool)
                        pool.dma_start(mixed[tok(t), a.col:a.col + GW], a.out_t[:, b]).then_inc(a.stored[b], 16)
                for b in range(2):
                    pool.wait_ge(a.stored[b], 16 * NP * (a.lay(l) + 1))
                settled(pool)
                gate(pool, l, a.stage)
            for a in (ret, hg):
                with pool.Fori(0, NP) as i:
                    for b in range(2):
                        t = 2 * i + b
                        pool.wait_ge(a.out_ready, made(1, a.lay(l) * NT + t + 1))
                        settled(pool)
                        pool.dma_start(mixed[tok(t), a.col:a.col + GW], a.out_t[:, b]).then_inc(a.stored[b], 16)
                pool.wait_ge(a.sf_ready, made(1, (a.lay(l) + 1) * NT))
                pool.wait_ge(a.bs_ready, made(1, (a.lay(l) + 1) * NT))
                settled(pool)
                for d, state in enumerate((a.sf, a.sb)):
                    for g, dst in enumerate(state_ap(out_ret if a is ret else out_hgrn, l, d)):
                        pool.dma_start(dst, state[:, 0, g * HD:(g + 1) * HD]).then_inc(a.s_saved, 16)
                for b in range(2):
                    pool.wait_ge(a.stored[b], 16 * NP * (a.lay(l) + 1))
                pool.wait_ge(a.s_saved, 64 * (a.lay(l) + 1))
                settled(pool)
                gate(pool, l, a.stage)
            with pool.Fori(0, NP) as i:
                for b in range(2):
                    t = 2 * i + b
                    pool.wait_ge(y_ready, made(1, l * NT + t + 1))
                    settled(pool)
                    pool.dma_start(streams[bass.ds(l + 1, 1), tok(t), :].rearrange("a p n -> p (a n)"), y_t[:, b]
                                   ).then_inc(y_stored[b], 16)
            for b in range(2):
                pool.wait_ge(y_stored[b], 16 * (l + 1) * NP)
            settled(pool)
            gate(pool, l, OUTPUT)

    @block.tensor
    def _(pe):
        pe.wait_ge(consts_in, 48)
        pe.sem_inc(wa_used, AHEAD)
        pe.sem_inc(x_turned, AHEAD)
        pe.sem_inc(proj_done, AHEAD * NG)
        pe.sem_inc(mx_turned, AHEAD)
        pe.sem_inc(y_done, AHEAD)
        for name in (win.k_turned, win.q_turned, win.s_done, win.p_turned, win.pv_done):
            pe.sem_inc(name, AHEAD)
        for name in (ret.bkv_done, ret.kv_done):
            pe.sem_inc(name, AHEAD)
        for name in (ret.turned, ret.p_done, ret.o_done, hg.x_ready, hg.f_turned):
            pe.sem_inc(name, AHEAD)
        for name in (hg.p_done, hg.o_done, hg.e_done):
            pe.sem_inc(name, AHEAD * 4)
        pe.wait_ge(setup, SETUP_DVE)
        with pe.Fori(0, DEPTH) as l:
            for n in range(KC):
                pe.wait_ge(wa_in[n % 2], 16 * (l * (KC // 2) + n // 2 + 1))
                for j in range(3):
                    at = 3 * n + j
                    for k in range(KC):
                        last = nc.tensor.matmul(ps[:, 0, 2 * at:2 * at + 2], wa[:, n % 2, k, j * P:(j + 1) * P],
                                                cond[:, k, :], start=(k == 0), stop=(k == KC - 1))
                last.then_inc(wa_used, 1)
            gate(pe, l, MODULATE)

            def turn_x(i, b, c):
                u = l * NT + 2 * i + b
                pe.wait_ge(x_normed, made(1, u + 1))
                pe.wait_ge(h_act, made(1, u - 1))
                pe.wait_ge(h_dve, made(1, u - 1))
                for k in range(KC):
                    last = nc.tensor.transpose(ps[:, 2 * b + k // 4, (k % 4) * P:(k % 4 + 1) * P],
                                               xt[:, b, k * P:(k + 1) * P], ident[:, :])
                last.then_inc(x_turned, 1)

            def project(i, b, c):
                u = l * NT + 2 * i + b
                pe.wait_ge(h_act, made(1, u + 1))
                pe.wait_ge(h_dve, made(1, u + 1))
                for g in range(NG):
                    pe.wait_ge(w_loaded[g], (32 if g == NG - 1 else 16) * (l + 1))
                    if g < 4:
                        pe.wait_ge(out_g[g + 4], made(1, u))
                    else:
                        pe.wait_ge(out_g[g - 4], made(1, u + 1))
                    for k in range(KC):
                        last = nc.tensor.matmul(ps[:, 4 + g % 4, :], hT[:, b, k, :], w_sb[:, k, g * GRP:(g + 1) * GRP],
                                                start=(k == 0), stop=(k == KC - 1))
                    last.then_inc(proj_done, 1)

            tiles(pe, turn_x, project)
            gate(pe, l, PROJECT)
            for a in (win, nei):
                with pe.Fori(0, SLOT_N // 2) as i:
                    for b in range(2):
                        u, v = l * SLOT_N + 2 * i + b, a.lay(l) * SLOT_N + 2 * i + b
                        if a is win:
                            pe.wait_ge(a.k_rot, made(1, u + 1))
                        else:
                            pe.wait_ge(a.k_in[b], 16 * (l * (SLOT_N // 2) + i + 1))
                        pe.wait_ge(a.k_out, made(1, v - 1))
                        settled(pe)
                        src = a.k_rope if a is win else a.k_raw
                        for h in range(a.nkv):
                            last = nc.tensor.transpose(ps[0:HD, b, h * P:(h + 1) * P], src[:, b, h * HD:(h + 1) * HD], ident[:, :])
                        last.then_inc(a.k_turned, 1)
                pe.wait_ge(a.k_out, made(1, (a.lay(l) + 1) * SLOT_N))
                for b in range(2):
                    pe.wait_ge(a.v_in[b], 16 * (a.lay(l) + 1) * (SLOT_N // 2))
                settled(pe)

                def turn_q(i, b):
                    u, v = l * NT + 2 * i + b, a.lay(l) * NT + 2 * i + b
                    if a is win:
                        pe.wait_ge(a.q_rot, made(1, u + 1))
                    else:
                        pe.wait_ge(a.q_in[b], 32 * (l * NP + i + 1))
                    pe.wait_ge(a.q_ready, made(1, v))
                    if b == 0:
                        pe.wait_ge(a.out_ready, made(1, v))
                    settled(pe)
                    src = a.q_rope if a is win else a.q_raw
                    for h in range(HEADS):
                        last = nc.tensor.transpose(ps[0:HD, 0, h * P:(h + 1) * P], src[:, b, h * HD:(h + 1) * HD], ident[:, :])
                    last.then_inc(a.q_turned, 1)

                def scores(i, b, h, kind, base):
                    x = (a.lay(l) * NT + 2 * i + b) * HEADS + h
                    if h == 0:
                        pe.wait_ge(a.q_ready, made(1, a.lay(l) * NT + 2 * i + b + 1))
                    pe.wait_ge(a.e_ready, made(1, x - 1))
                    settled(pe)
                    q = a.qT[:, b, h, :]
                    s = score_banks(w_par(b, h))
                    kv = h // (HEADS // a.nkv)
                    if kind is None:
                        last = nc.tensor.matmul(s[:, 0:CTX], q, a.kT[:, kv, 0:CTX], start=True, stop=True)
                    else:
                        n = min(a.near * P, GRP)
                        nc.tensor.matmul(s[:, 0:n], q, a.kT[:, kv, bass.ds(base * P, n)], start=True, stop=True)
                        if a.near * P > n:
                            nc.tensor.matmul(s[:, n:a.near * P], q, a.kT[:, kv, bass.ds(base * P + n, a.near * P - n)],
                                             start=True, stop=True)
                        for c in range(CT):
                            at = (a.near + c) * P
                            last = nc.tensor.matmul(s[:, at:at + P], q, a.kT[:, kv, (NT + c) * P:(NT + c + 1) * P],
                                                    start=True, stop=True)
                    last.then_inc(a.s_done, 1)

                def turn_p(i, b, h, kind, base):
                    x = (a.lay(l) * NT + 2 * i + b) * HEADS + h
                    pe.wait_ge(a.e_ready, made(1, x + 1))
                    pe.wait_ge(a.pt_act, made(1, x))
                    pe.wait_ge(a.pt_dve, made(1, x))
                    n = CT if kind is None else a.near + CT
                    cut = n // 2
                    for c in range(n):
                        bank, at = (5, c) if c < cut else (6, c - cut)
                        last = nc.tensor.transpose(ps[:, bank, at * P:(at + 1) * P],
                                                   a.e[:, w_par(b, h), c * P:(c + 1) * P], ident[:, :])
                    last.then_inc(a.p_turned, 1)

                def weigh(i, b, h, kind, base):
                    x = (a.lay(l) * NT + 2 * i + b) * HEADS + h
                    pe.wait_ge(a.pt_act, made(1, x + 1))
                    pe.wait_ge(a.pt_dve, made(1, x + 1))
                    pe.wait_ge(a.out_ready, made(1, a.lay(l) * NT + 2 * i + b - 1))
                    if b == 1:
                        pe.wait_ge(a.q_ready, made(1, a.lay(l) * NT + 2 * i + 2))
                    settled(pe)
                    kv = h // (HEADS // a.nkv)
                    out = ps[:, OUT_BANK[b], h * HD:(h + 1) * HD]
                    near = 0 if kind is None else a.near
                    slots = [base + c for c in range(near)] + [(0 if kind is None else NT) + c for c in range(CT)]
                    for c, slot in enumerate(slots):
                        last = nc.tensor.matmul(out, a.pT[:, w_par(b, h), c, :],
                                                a.v[:, bass.ds(slot, 1), kv * HD:(kv + 1) * HD].rearrange("p a n -> p (a n)"),
                                                start=(c == 0), stop=(c == len(slots) - 1))
                    last.then_inc(a.pv_done, 1)

                attend(pe, a, turn_q, scores, turn_p, weigh)
                gate(pe, l, a.stage)
            def outer(keys, values, bank, b):
                for h in range(HEADS):
                    hp, g = h % 2, h // 2
                    last = nc.tensor.matmul(ps[hp * HD:(hp + 1) * HD, bank, KV_AT + g * HD:KV_AT + (g + 1) * HD],
                                            keys[:, h * HD:(h + 1) * HD], values[:, h * HD:(h + 1) * HD], start=True, stop=True)
                return last

            def back_ret(i, b, c):
                u = l * NT + 2 * i + b
                v = ret.lay(l) * NT + 2 * i + b
                pe.wait_ge(ret.bk_ready, made(1, v + 1))
                pe.wait_ge(ret.bs_ready, made(1, v - 1))
                outer(ret.kd[:, b], ret.braw[:, b, GW:2 * GW], b, b).then_inc(ret.bkv_done, 1)

            backward(pe, back_ret)

            def turn_ret(i, b, c):
                u = l * NT + 2 * i + b
                v = ret.lay(l) * NT + 2 * i + b
                pe.wait_ge(ret.x_ready, made(1, u + 1))
                pe.wait_ge(ret.xT_ready, made(1, v - 1))
                for n in range(4):
                    last = nc.tensor.transpose(ps[:, b, n * P:(n + 1) * P], ret.x[:, b, n * P:(n + 1) * P], ident[:, :])
                last.then_inc(ret.turned, 1)

            def products_ret(i, b, c):
                u = l * NT + 2 * i + b
                v = ret.lay(l) * NT + 2 * i + b
                pe.wait_ge(ret.xT_ready, made(1, v + 1))
                pe.wait_ge(ret.p_ready, made(1, u))
                for h in range(HEADS):
                    hp, g = h % 2, h // 2
                    rows_h = slice(hp * HD, (hp + 1) * HD)
                    last = nc.tensor.matmul(ps[:, 2 + hp, g * P:(g + 1) * P], ret.xT[rows_h, b, 2 + g, :],
                                            ret.xT[rows_h, b, g, :], start=True, stop=True)
                last.then_inc(ret.p_done, 1)
                pe.wait_ge(ret.kf_ready, made(1, v + 1))
                pe.wait_ge(ret.sf_ready, made(1, v))
                outer(ret.kd[:, b], ret.raw[:, b, 2 * GW:3 * GW], 6, b).then_inc(ret.kv_done, 1)
                pe.wait_ge(ret.p_ready, made(1, u + 1))
                pe.wait_ge(ret.qd_ready, made(1, u + 1))
                pe.wait_ge(ret.sb_ready, made(1, v + 1))
                pe.wait_ge(ret.ready, made(1, v))
                for h in range(HEADS):
                    hp, g = h % 2, h // 2
                    rows_h = slice(hp * HD, (hp + 1) * HD)
                    out = ps[:, 4 + hp, g * HD:(g + 1) * HD]
                    nc.tensor.matmul(out, ret.p[:, b, hp, g, :], ret.raw[:, b, 2 * GW + h * HD:2 * GW + (h + 1) * HD],
                                     start=True, stop=False)
                    nc.tensor.matmul(out, ret.qd[rows_h, b, 0, g, :], ret.sf[rows_h, c, g * HD:(g + 1) * HD],
                                     start=False, stop=False)
                    last = nc.tensor.matmul(out, ret.qd[rows_h, b, 1, g, :], ret.sb_at[rows_h, b, g * HD:(g + 1) * HD],
                                            start=False, stop=True)
                last.then_inc(ret.o_done, 1)

            tiles(pe, turn_ret, products_ret)
            gate(pe, l, RET)

            def sums_to_end(a, lf, side, bank):
                nc.tensor.matmul(ps[:, bank, 0:GW], past[:, side, :], lf, start=True, stop=True)
                for g in range(2):
                    last = nc.tensor.matmul(ps[:, bank, GW + g:GW + g + 1], lf[:, g * P:(g + 1) * P], ones[:, :],
                                            start=True, stop=True)
                return last

            def back_hg(i, b, c):
                u = l * NT + 2 * i + b
                v = hg.lay(l) * NT + 2 * i + b
                pe.wait_ge(hg.b_in[b], 48 * (l * NP + i + 1))
                pe.wait_ge(hg.bs_ready, made(1, v - 1))
                sums_to_end(hg, hg.braw[:, b, 0:GW], 1, b).then_inc(hg.turned, 1)
                pe.wait_ge(hg.bk_ready, made(1, v + 1))
                outer(hg.kd[:, b], hg.braw[:, b, GW:2 * GW], b, b).then_inc(hg.bkv_done, 1)

            pe.wait_ge(hg.tab_in, 80 * (l + 1))
            backward(pe, back_hg)

            def turn_hg(i, b, c):
                u = l * NT + 2 * i + b
                v = hg.lay(l) * NT + 2 * i + b
                pe.wait_ge(hg.raw_in[b], 16 * (l * NP + i + 1))
                pe.wait_ge(hg.xT_ready, made(1, v))
                for n, at in enumerate((0, P, 5 * GW, 5 * GW + P, 6 * GW, 6 * GW + P)):
                    last = nc.tensor.transpose(ps[:, n // 4, n % 4 * P:(n % 4 + 1) * P], hg.raw[:, b, at:at + P], ident[:, :])
                last.then_inc(hg.x_ready, 1)

            def products_hg(i, b, c):
                u = l * NT + 2 * i + b
                v = hg.lay(l) * NT + 2 * i + b
                pe.wait_ge(hg.sf_ready, made(1, v))
                sums_to_end(hg, hg.raw[:, b, GW:2 * GW], 0, 6).then_inc(hg.f_turned, 1)
                for g in range(2):
                    for d in range(2):
                        at = GW * (1 + d) + g * P
                        pe.wait_ge(hg.d_ready, made(4, u) + 2 * g + d)
                        for half in range(2):
                            last = nc.tensor.matmul(ps[:, 2 + half, :], hg.raw[:, b, at:at + P],
                                                    sums[:, d, 4 * half:4 * half + 4, :].rearrange("p s n -> p (s n)"),
                                                    start=True, stop=True)
                        last.then_inc(hg.e_done, 1)
                    if g == 0:
                        pe.wait_ge(hg.kf_ready, made(1, v + 1))
                        outer(hg.kd[:, b], hg.raw[:, b, 4 * GW:5 * GW], 6, b).then_inc(hg.kv_done, 1)
                for h in range(HEADS):
                    hp, g = h % 2, h // 2
                    rows_h = slice(hp * HD, (hp + 1) * HD)
                    pe.wait_ge(hg.qk_ready, made(4, u) + 2 * (g + 1))
                    pe.wait_ge(hg.p_ready, made(HEADS, u) + h)
                    settled(pe)

                    def slot(n):
                        return ps[:, 4 + n // 8, n % 8 * 64:(n % 8 + 1) * 64]

                    for blk in range(2):
                        at = slice(blk * 64, (blk + 1) * 64)
                        for d in range(2):
                            for lv in range(SLOTS):
                                nc.tensor.matmul(slot(d * SLOTS + lv)[at, :], hg.k[rows_h, g, d, lv, at], hg.q[rows_h, g, d, lv, at],
                                                 start=True, stop=True)
                        for d in range(2):
                            nc.tensor.matmul(slot(2 * SLOTS)[at, :], hg.xT[rows_h, b, 2 + 2 * d + g, at], hg.xT[rows_h, b, g, at],
                                             start=(d == 0), stop=(d == 1))
                        other = slice((1 - blk) * 64, (2 - blk) * 64)
                        last = nc.tensor.matmul(slot(2 * SLOTS + 1)[at, :], hg.k[rows_h, g, blk, LEVELS - 1, at],
                                                hg.q[rows_h, g, blk, LEVELS - 1, other], start=True, stop=True)
                    last.then_inc(hg.p_done, 1)
                    pe.wait_ge(hg.p_ready, made(HEADS, u) + h + 1)
                    if h == 0:
                        pe.wait_ge(hg.sb_ready, made(1, v + 1))
                        pe.wait_ge(hg.out_ready, made(1, v))
                    out = ps[:, 7, h * HD:(h + 1) * HD]
                    nc.tensor.matmul(out, hg.p[:, h % 2, :], hg.raw[:, b, 4 * GW + h * HD:4 * GW + (h + 1) * HD],
                                     start=True, stop=False)
                    nc.tensor.matmul(out, hg.q[rows_h, g, 0, LEVELS, :], hg.sf[rows_h, c, g * HD:(g + 1) * HD],
                                     start=False, stop=False)
                    last = nc.tensor.matmul(out, hg.q[rows_h, g, 1, LEVELS, :], hg.sb_at[rows_h, b, g * HD:(g + 1) * HD],
                                            start=False, stop=True)
                    last.then_inc(hg.o_done, 1)

            pe.wait_ge(hg.bs_ready, made(1, (hg.lay(l) + 1) * NT))
            settled(pe)
            tiles(pe, turn_hg, products_hg)
            gate(pe, l, HGRN)
            pe.wait_ge(wo_in, 48 * (l + 1))

            def turn_mixed(i, b, c):
                u = l * NT + 2 * i + b
                pe.wait_ge(mx_in[b], 16 * (l * NP + i + 1))
                pe.wait_ge(mT_act, made(1, u - 1))
                pe.wait_ge(mT_dve, made(1, u - 1))
                for k in range(KC):
                    last = nc.tensor.transpose(ps[:, 2 * b + k // 4, (k % 4) * P:(k % 4 + 1) * P],
                                               mx_t[:, b, k * P:(k + 1) * P], ident[:, :])
                last.then_inc(mx_turned, 1)

            def project_out(i, b, c):
                u = l * NT + 2 * i + b
                pe.wait_ge(mT_act, made(1, u + 1))
                pe.wait_ge(mT_dve, made(1, u + 1))
                pe.wait_ge(y_ready, made(1, u - 1))
                for g in range(2):
                    for k in range(KC):
                        last = nc.tensor.matmul(ps[:, 4 + 2 * b + g, :], mT[:, b, k, :], wo_sb[:, k, g * GRP:(g + 1) * GRP],
                                                start=(k == 0), stop=(k == KC - 1))
                last.then_inc(y_done, 1)

            tiles(pe, turn_mixed, project_out)
            gate(pe, l, OUTPUT)

    @block.scalar
    def _(act):
        act.sem_inc(rstd_ready, AHEAD)
        act.sem_inc(h_act, AHEAD)
        act.sem_inc(mT_act, AHEAD)
        act.sem_inc(exp_ready, AHEAD * 5)
        act.sem_inc(ln_out, AHEAD * 2)
        act.sem_inc(yr_ready, AHEAD)
        for g in ACT_GROUPS:
            act.sem_inc(out_g[g], AHEAD)
        for name in (win.k_out, win.q_ready, win.e_ready, win.pt_act):
            act.sem_inc(name, AHEAD)
        for name in (ret.xT_ready, ret.sb_ready, ret.sq_ready, ret.r_ready):
            act.sem_inc(name, AHEAD)
        act.sem_inc(hg.f_exp, AHEAD)
        act.sem_inc(hg.d_ready, AHEAD * 4)
        act.sem_inc(hg.p_ready, AHEAD * HEADS)
        act.wait_ge(consts_in, 48)
        nc.scalar.activation(cond_e[:, :, :], cond[:, :, :], ACT.Exp, scale=-1.0).then_inc(setup_act, 1)
        act.wait_ge(setup, SETUP_LB)
        nc.scalar.activation(lb_raw[:, :, :], lb_raw[:, :, :], ACT.Exp).then_inc(setup_act, 1)
        with act.Fori(0, DEPTH) as l:
            gate(act, l, MODULATE)

            def rstd(x, b, steps, ready, junk):
                steps.mark(nc.scalar.activation(junk, x, ACT.Square, accum_out=stat[:, b, 0:1]))
                steps.wait()
                steps.mark(nc.scalar.activation(stat[:, b, 1:2], stat[:, b, 0:1], ACT.Ln, bias=eps[:, 0:1],
                                                scale=1.0 / D_MODEL))
                steps.wait()
                nc.scalar.activation(stat[:, b, 2:3], stat[:, b, 1:2], ACT.Exp, scale=-0.5).then_inc(ready, 1)

            def normed(i, b, c):
                u = l * NT + 2 * i + b
                steps = Steps(act, act_step, u * 2)
                act.wait_ge(x_in[b], 16 * (l * NP + i + 1))
                rstd(xt[:, b], b, steps, rstd_ready, sq_junk[:, :])
                act.wait_ge(x_turned, made(1, u + 1))
                act.wait_ge(proj_done, made(NG, u - 1))
                for k in range(0, 4):
                    last = nc.scalar.activation(hT[:, b, k, :], ps[:, 2 * b + k // 4, (k % 4) * P:(k % 4 + 1) * P],
                                                ACT.Identity, scale=mod[:, KC + k, c:c + 1], bias=mod[:, k, c:c + 1])
                last.then_inc(h_act, 1)

            def emit(i, b, c):
                u = l * NT + 2 * i + b
                act.wait_ge(row_stored[b], 16 * (l * NP + i))
                for g in range(NG):
                    act.wait_ge(proj_done, made(NG, u) + g + 1)
                    bank = ps[:, 4 + g % 4, :]
                    out = row_t[:, b, g * GRP:(g + 1) * GRP]
                    if g in ACT_GROUPS:
                        nc.scalar.activation(out, bank, ACT.Copy).then_inc(out_g[g], 1)
                        continue
                    n = EXP_COLS[g]
                    act.wait_ge(out_g[last_exp[g]], made(1, u + (1 if last_exp[g] < g else 0)))
                    nc.scalar.activation(e_t[:, 0, 0:n], bank[:, 0:n], ACT.Exp, scale=-1.0).then_inc(exp_ready, 1)
                    if g == 6:
                        for j in range(2):
                            act.wait_ge(ln_in, 2 * u + j + 1)
                            nc.scalar.activation(e_t[:, j, :], e_t[:, j, :], ACT.Ln).then_inc(ln_out, 1)

            tiles(act, normed, emit)
            gate(act, l, PROJECT)
            for a in (win, nei):
                with act.Fori(0, SLOT_N // 2) as i:
                    for b in range(2):
                        t = 2 * i + b
                        act.wait_ge(a.k_turned, made(1, a.lay(l) * SLOT_N + t + 1))
                        settled(act)
                        nc.scalar.activation(a.kT[:, :, bass.ds(t * P, P)],
                                             ps[0:HD, b, 0:a.nkv * P].rearrange("p (h n) -> p h n", n=P), ACT.Copy
                                             ).then_inc(a.k_out, 1)

                def take_q(i, b):
                    u, v = l * NT + 2 * i + b, a.lay(l) * NT + 2 * i + b
                    act.wait_ge(a.q_turned, made(1, v + 1))
                    act.wait_ge(a.out_ready, made(1, v - 1))
                    nc.scalar.activation(a.qT[:, b].rearrange("p h n -> p (h n)"), ps[0:HD, 0, :], ACT.Copy,
                                         scale=HD ** -0.5).then_inc(a.q_ready, 1)

                def exps(i, b, h, kind, base):
                    x = (a.lay(l) * NT + 2 * i + b) * HEADS + h
                    e, st, s = a.e[:, w_par(b, h)], a.st[:, b, :, h], score_banks(w_par(b, h))
                    act.wait_ge(a.nm_ready, made(1, x + 1))
                    act.wait_ge(a.p_turned, made(1, x - 1))
                    near = 0 if kind is None else a.near * P
                    if a is win:
                        nc.scalar.activation(st[:, ES:ES + 1], st[:, NM:NM + 1], ACT.Exp, bias=sink[:, h:h + 1])
                    if kind is not None:
                        nc.scalar.activation(e[:, 0:near], a.sl[:, w_par(b, h), :], ACT.Exp, bias=st[:, NM:NM + 1],
                                             accum_out=st[:, D1:D1 + 1])
                    nc.scalar.activation(e[:, near:near + CTX], s[:, near:near + CTX], ACT.Exp, bias=st[:, NM:NM + 1],
                                         accum_out=st[:, D2:D2 + 1]).then_inc(a.e_ready, 1)

                def take_p(i, b, h, kind, base):
                    x = (a.lay(l) * NT + 2 * i + b) * HEADS + h
                    n = CT if kind is None else a.near + CT
                    act.wait_ge(a.p_turned, made(1, x + 1))
                    act.wait_ge(a.pv_done, made(1, x - 1))
                    cut = n // 2
                    nc.scalar.activation(a.pT[:, w_par(b, h), cut:n, :].rearrange("p c n -> p (c n)"),
                                         ps[:, 6, 0:(n - cut) * P], ACT.Copy).then_inc(a.pt_act, 1)

                attend(act, a, take_q, exps, take_p, None)
                gate(act, l, a.stage)
            def norm_stats(a, b, u, v):
                steps = Steps(act, a.n_step, v)
                act.wait_ge(a.var_ready, made(1, v + 1))
                steps.mark(nc.scalar.activation(a.st[:, b, 2], a.st[:, b, 1], ACT.Ln, bias=eps[:, 0:1], scale=1.0 / HD))
                steps.wait()
                nc.scalar.activation(a.st[:, b, 3], a.st[:, b, 2], ACT.Exp, scale=-0.5).then_inc(a.r_ready, 1)

            def state_at(a, i, b, u, v):
                act.wait_ge(a.o_done, made(HEADS if a is hg else 1, u - 1))
                settled(act)
                nc.scalar.activation(a.sb_at[:, b, :], a.sb_all[:, bass.ds(2 * i + b, 1), :].rearrange("p a n -> p (a n)"),
                                     ACT.Copy).then_inc(a.sb_ready, 1)

            act.wait_ge(lg_step, 8 * l + 2)
            nc.scalar.activation(lg_t[:, 1], lg_t[:, 1], ACT.Exp).then_inc(lg_act, 1)
            act.wait_ge(lg_act, 17 * l + 1)
            nc.scalar.activation(lg_t[:, 1], lg_t[:, 1], ACT.Ln, bias=ones[:, 0:1]).then_inc(lg_act, 1)
            act.wait_ge(lg_step, 8 * l + 6)
            nc.scalar.activation(pair_decay[:, :, :], lgp[:, :, :], ACT.Exp, scale=float(P)).then_inc(lg_act, 1)
            for d in range(2):
                nc.scalar.activation(key_decay[:, d], lg[:, d * HEADS:(d + 1) * HEADS], ACT.Exp, scale=dcol[:, d:d + 1]
                                     ).then_inc(lg_act, 1)
                for g in range(2):
                    nc.scalar.activation(row_decay[:, d, g], dtab[:, 4 + d], ACT.Exp, scale=lgp[:, d, g:g + 1]).then_inc(lg_act, 1)
            for h in range(HEADS):
                for d in range(2):
                    act.wait_ge(dm_step, 3 * HEADS * l + 3 * h)
                    nc.scalar.activation(dtmp[:, d], dtab[:, d], ACT.Exp, scale=lg[:, d * HEADS + h:d * HEADS + h + 1]
                                         ).then_inc(lg_act, 1)

            def take_x(i, b, c):
                u = l * NT + 2 * i + b
                v = ret.lay(l) * NT + 2 * i + b
                act.wait_ge(ret.turned, made(1, u + 1))
                act.wait_ge(ret.p_done, made(1, u - 1))
                act.wait_ge(ret.qd_ready, made(1, u - 1))
                nc.scalar.activation(ret.xT[:, b].rearrange("p k n -> p (k n)"), ps[:, b, :], ACT.Copy).then_inc(ret.xT_ready, 1)
                state_at(ret, i, b, u, v)

            def norm_ret(i, b, c):
                u = l * NT + 2 * i + b
                v = ret.lay(l) * NT + 2 * i + b
                act.wait_ge(ret.ready, made(1, v + 1))
                act.wait_ge(ret.var_ready, made(1, v - 1))
                nc.scalar.activation(ret.o_sq[:, b], ret.o_c[:, b], ACT.Square).then_inc(ret.sq_ready, 1)
                norm_stats(ret, b, u, v)

            tiles(act, take_x, norm_ret)
            gate(act, l, RET)

            def decay_back(i, b, c):
                u = l * NT + 2 * i + b
                v = hg.lay(l) * NT + 2 * i + b
                act.wait_ge(hg.turned, u + 1)
                act.wait_ge(hg.bs_ready, made(1, v - 1))
                nc.scalar.activation(hg.ed[:, b], ps[:, b, 0:GW + 2], ACT.Exp).then_inc(hg.ready, 1)

            backward(act, decay_back)

            def take_hg(i, b, c):
                u = l * NT + 2 * i + b
                v = hg.lay(l) * NT + 2 * i + b
                act.wait_ge(hg.x_ready, made(1, u + 1))
                act.wait_ge(hg.p_done, made(HEADS, u - 1))
                nc.scalar.activation(hg.xT[:, b, 0:4].rearrange("p k n -> p (k n)"), ps[:, 0, :], ACT.Copy)
                nc.scalar.activation(hg.xT[:, b, 4:6].rearrange("p k n -> p (k n)"), ps[:, 1, 0:2 * P], ACT.Copy
                                     ).then_inc(hg.xT_ready, 1)
                state_at(hg, i, b, u, v)

            def decays_hg(i, b, c):
                u = l * NT + 2 * i + b
                v = hg.lay(l) * NT + 2 * i + b
                act.wait_ge(hg.f_turned, made(1, u + 1))
                act.wait_ge(hg.sf_ready, made(1, v - 1))
                nc.scalar.activation(hg.ed[:, b], ps[:, 6, 0:GW + 2], ACT.Exp).then_inc(hg.f_exp, 1)
                for g in range(2):
                    for d in range(2):
                        act.wait_ge(hg.e_done, made(4, u) + 2 * g + d + 1)
                        act.wait_ge(hg.qk_ready, made(4, u) + 2 * g + d - 1)
                        nc.scalar.activation(hg.d[:, d].rearrange("p s n -> p (s n)"),
                                             ps[:, 2:4, :].rearrange("p a n -> p (a n)"), ACT.Exp).then_inc(hg.d_ready, 1)
                for h in range(HEADS):
                    act.wait_ge(hg.tc_ready, made(HEADS, u) + h + 1)
                    act.wait_ge(hg.o_done, made(HEADS, u) + h - 1)
                    for blk in range(2):
                        at, other = slice(blk * 64, (blk + 1) * 64), slice((1 - blk) * 64, (2 - blk) * 64)
                        nc.scalar.activation(hg.p[at, h % 2, at], hg.tc[at, h % 2, :], ACT.Copy)
                        last = nc.scalar.activation(hg.p[at, h % 2, other], ps[at, 5, 5 * 64:6 * 64], ACT.Copy)
                    last.then_inc(hg.p_ready, 1)
                act.wait_ge(hg.o_done, made(HEADS, u + 1))
                act.wait_ge(hg.var_ready, made(1, v - 1))
                nc.scalar.activation(hg.o_sq[:, b], ps[:, 7, 0:GW], ACT.Square).then_inc(hg.sq_ready, 1)
                norm_stats(hg, b, u, v)

            tiles(act, take_hg, decays_hg)
            gate(act, l, HGRN)

            def turned(i, b, c):
                u = l * NT + 2 * i + b
                act.wait_ge(mx_turned, made(1, u + 1))
                act.wait_ge(y_done, made(1, u - 1))
                nc.scalar.activation(mT[:, b, 0:4, :], ps[:, 2 * b, :].rearrange("p (k n) -> p k n", n=P), ACT.Copy
                                     ).then_inc(mT_act, 1)

            def y_rstd(i, b, c):
                u = l * NT + 2 * i + b
                steps = Steps(act, o_act, u * 2)
                act.wait_ge(y_done, made(1, u + 1))
                act.wait_ge(y_stored[b], 16 * (l * NP + i))
                rstd(ps[:, 4 + 2 * b:6 + 2 * b, :], b, steps, yr_ready,
                     y_t[:, b].rearrange("p (k n) -> p k n", n=GRP))

            tiles(act, turned, y_rstd)
            gate(act, l, OUTPUT)

    @block.vector
    def _(dve):
        dve.sem_inc(x_normed, AHEAD)
        dve.sem_inc(h_dve, AHEAD)
        dve.sem_inc(mT_dve, AHEAD)
        dve.sem_inc(y_ready, AHEAD)
        for g in range(NG):
            if g not in ACT_GROUPS:
                dve.sem_inc(out_g[g], AHEAD)
        for name in (win.k_rot, win.q_rot, win.nm_ready, win.pt_dve, win.out_ready):
            dve.sem_inc(name, AHEAD)
        for name in (ret.bk_ready, ret.bs_ready, ret.kf_ready, ret.sf_ready, ret.var_ready, ret.out_ready):
            dve.sem_inc(name, AHEAD)
        for name in (ret.x_ready, ret.qd_ready, ret.p_ready):
            dve.sem_inc(name, AHEAD)
        dve.sem_inc(ret.ready, AHEAD)
        dve.sem_inc(hg.qk_ready, AHEAD * 4)
        dve.sem_inc(hg.tc_ready, AHEAD * HEADS)
        nc.vector.memset(eps[:, :], EPS)
        nc.vector.memset(ones[:, :], 1.0)
        dve.wait_ge(consts_in, 48)
        nc.vector.memset(neg_t[:, :], NEG).then_inc(neg_ready, 1)
        dve.wait_ge(lb_loaded, 16 * DEPTH)
        steps = Steps(dve, setup, 0)
        steps.mark(nc.vector.tensor_tensor(lbd[:, 0], lb_raw[:, 0], lb_raw[:, 1], ALU.max))
        steps.wait()
        for d in range(DEPTH):
            steps.mark(nc.vector.tensor_tensor(lb_raw[:, d], lb_raw[:, d], lbd[:, 0], ALU.subtract))
        assert steps.n == SETUP_LB
        dve.wait_ge(setup_act, 2)
        steps.mark(nc.vector.tensor_tensor(lb_raw[:, 0], lb_raw[:, 0], lb_raw[:, 1], ALU.add))
        steps.mark(nc.vector.tensor_scalar(cond_e[:, :, :], cond_e[:, :, :], 1.0, None, ALU.add))
        steps.wait()
        steps.mark(nc.vector.reciprocal(oml[:, 0], lb_raw[:, 0]))
        steps.mark(nc.vector.reciprocal(cond_e[:, :, :], cond_e[:, :, :]))
        steps.wait()
        steps.mark(nc.vector.tensor_tensor(lbd[:, 1], lb_raw[:, 1], oml[:, 0], ALU.mult))
        steps.mark(nc.vector.memset(lbd[:, 0], 0.0))
        steps.mark(nc.vector.tensor_tensor(cond[:, :, :], cond[:, :, :], cond_e[:, :, :], ALU.mult))
        steps.wait()
        steps.mark(nc.vector.tensor_scalar(lbd[:, :, :], lbd[:, :, :], LB_FLOOR, None, ALU.max))
        steps.wait()
        steps.mark(nc.vector.tensor_scalar(oml[:, :, :], lbd[:, :, :], -1.0, 1.0, ALU.mult, ALU.add))
        assert steps.n == SETUP_DVE, steps.n
        with dve.Fori(0, DEPTH) as l:
            steps = Steps(dve, mod_step, l * MOD_STEPS)
            dve.wait_ge(modw_in, 48 * (l + 1))
            dve.wait_ge(wa_used, made(1, (l + 1) * KC))
            steps.mark(nc.vector.tensor_tensor(
                mod[:, :, :], ps[:, 0, 0:6 * KC].rearrange("p (n c) -> p n c", c=2),
                mod_w[:, 0:3 * KC].unsqueeze(2).broadcast_to([P, 3 * KC, 2]), ALU.add))
            steps.wait()
            steps.mark(nc.vector.tensor_scalar(mod[:, KC:2 * KC, :], mod[:, KC:2 * KC, :], 1.0, None, ALU.add))
            steps.wait()
            nc.vector.tensor_tensor(mod[:, KC:3 * KC, :], mod[:, KC:3 * KC, :],
                                    mod_w[:, 3 * KC:5 * KC].unsqueeze(2).broadcast_to([P, 2 * KC, 2]), ALU.mult
                                    ).then_inc(mod_ready, 1)
            assert steps.n == MOD_STEPS
            gate(dve, l, MODULATE)

            def normed(i, b, c):
                u = l * NT + 2 * i + b
                dve.wait_ge(rstd_ready, made(1, u + 1))
                nc.vector.tensor_scalar(xt[:, b], xt[:, b], stat[:, b, 2:3], None, ALU.mult).then_inc(x_normed, 1)
                dve.wait_ge(x_turned, made(1, u + 1))
                dve.wait_ge(proj_done, made(NG, u - 1))
                for k in range(4, KC):
                    last = nc.vector.tensor_scalar(hT[:, b, k, :], ps[:, 2 * b + k // 4, (k % 4) * P:(k % 4 + 1) * P],
                                                   mod[:, KC + k, c:c + 1], mod[:, k, c:c + 1], ALU.mult, ALU.add)
                last.then_inc(h_dve, 1)

            def emit(i, b, c):
                u = l * NT + 2 * i + b
                steps = Steps(dve, emit_dve, u * EMIT_DVE)
                dve.wait_ge(row_stored[b], 16 * (l * NP + i))
                seen = 0
                for g in range(NG):
                    if g in ACT_GROUPS:
                        continue
                    bank = ps[:, 4 + g % 4, :]
                    out = row_t[:, b, g * GRP:(g + 1) * GRP]
                    n = EXP_COLS[g]
                    seen += 1
                    dve.wait_ge(exp_ready, made(5, u) + seen)
                    steps.mark(nc.vector.tensor_scalar(e_t[:, 0, 0:n], e_t[:, 0, 0:n], 1.0, None, ALU.add))
                    steps.wait()
                    steps.mark(nc.vector.reciprocal(e_t[:, 0, 0:n], e_t[:, 0, 0:n]))
                    steps.wait()
                    if g != 6:
                        if n < GRP:
                            nc.vector.tensor_copy(out[:, n:], bank[:, n:])
                        nc.vector.tensor_tensor(out[:, 0:n], e_t[:, 0, 0:n], bank[:, 0:n], ALU.mult
                                                ).then_inc(out_g[g], 1)
                        continue
                    steps.mark(nc.vector.tensor_tensor(e_t[:, 0], e_t[:, 0], oml_l[:, :], ALU.mult))
                    steps.wait()
                    steps.mark(nc.vector.tensor_tensor(e_t[:, 2], e_t[:, 0], lbd_l[:, :], ALU.add))
                    steps.wait()
                    nc.vector.tensor_scalar(row_t[:, b, C_KD:C_KD + GRP], e_t[:, 2], -1.0, 1.0, ALU.mult, ALU.add)
                    nc.vector.tensor_scalar(e_t[:, 0], e_t[:, 2], LN_SPLIT, None, ALU.max).then_inc(ln_in, 1)
                    nc.vector.tensor_scalar(e_t[:, 1], e_t[:, 2], LN_SPLIT, 1.0 / LN_SPLIT, ALU.min, ALU.mult
                                            ).then_inc(ln_in, 1)
                    dve.wait_ge(ln_out, made(2, u + 1))
                    nc.vector.tensor_tensor(out, e_t[:, 0], e_t[:, 1], ALU.add).then_inc(out_g[g], 1)
                assert steps.n == EMIT_DVE, steps.n

            nc.vector.tensor_copy(lbd_l[:, :], lbd[:, bass.ds(l, 1), :].rearrange("p a n -> p (a n)"))
            nc.vector.tensor_copy(oml_l[:, :], oml[:, bass.ds(l, 1), :].rearrange("p a n -> p (a n)")
                                  ).then_inc(bounds_ready, 1)
            dve.wait_ge(bounds_ready, l + 1)
            tiles(dve, normed, emit)
            gate(dve, l, PROJECT)
            def rope(steps, dst, src, tab, tmp, heads):
                nf = HD // 4
                cos = tab[:, 0:HD].unsqueeze(1).broadcast_to([P, heads, HD])
                steps.mark(nc.vector.tensor_tensor(dst.rearrange("p (h n) -> p h n", n=HD),
                                                   src.rearrange("p (h n) -> p h n", n=HD), cos, ALU.mult))
                for s in range(2):
                    x = src.rearrange("p (h f s n) -> p h f s n", f=2, s=2, n=nf)[:, :, :, 1 - s, :]
                    y = tmp.rearrange("p (h f s n) -> p h f s n", f=2, s=2, n=nf)[:, :, :, s, :]
                    sin = tab[:, HD:2 * HD].rearrange("p (f s n) -> p f s n", f=2, s=2)[:, :, s, :].unsqueeze(1)
                    steps.mark(nc.vector.tensor_tensor(y, x, sin.broadcast_to([P, heads, 2, nf]), ALU.mult))
                steps.wait()
                return nc.vector.tensor_tensor(dst, dst, tmp, ALU.add)

            for a in (win, nei):
                if a is win:
                    with dve.Fori(0, SLOT_N // 2) as i:
                        for b in range(2):
                            u, v = l * SLOT_N + 2 * i + b, a.lay(l) * SLOT_N + 2 * i + b
                            steps = Steps(dve, a.k_step, u * 3)
                            dve.wait_ge(a.k_in[b], 32 * (l * (SLOT_N // 2) + i + 1))
                            dve.wait_ge(a.k_turned, made(1, v - 1))
                            dve.wait_ge(a.k_rot, made(1, u))
                            rope(steps, a.k_rope[:, b], a.k_raw[:, b], a.rope_t[:, b], a.rot_tmp[:, 0:2 * HD], 2
                                 ).then_inc(a.k_rot, 1)
                    dve.wait_ge(a.k_rot, made(1, (l + 1) * SLOT_N))
                    dve.wait_ge(mask_in, 32 * (l + 1) + 16 * 10 * HEADS * l)
                else:
                    dve.wait_ge(mask_in, (32 + 16 * 10 * HEADS) * (l + 1))

                def turn(i, b):
                    if a is nei:
                        dve.wait_ge(a.q_in[b], 32 * (l * NP + i + 1))
                    if a is win:
                        u, v = l * NT + 2 * i + b, a.lay(l) * NT + 2 * i + b
                        steps = Steps(dve, a.q_step, u * 3)
                        dve.wait_ge(a.q_in[b], 48 * (l * NP + i + 1))
                        dve.wait_ge(a.q_turned, made(1, v - 1))
                        dve.wait_ge(a.q_rot, made(1, u))
                        rope(steps, a.q_rope[:, b], a.q_raw[:, b], a.rope_q[:, b], a.rot_tmp[:, :], HEADS
                             ).then_inc(a.q_rot, 1)

                def maxima(i, b, h, kind, base):
                    x = (a.lay(l) * NT + 2 * i + b) * HEADS + h
                    seen = (2 * i + b) * HEADS + h
                    ctx_units = CT * HEADS
                    steps = Steps(dve, a.s_step, a.lay(l) * (2 * NT * HEADS - ctx_units)
                                  + (seen if kind is None else 2 * seen - ctx_units))
                    st, s = a.st[:, b, :, h], score_banks(w_par(b, h))
                    near = 0 if kind is None else a.near * P
                    dve.wait_ge(a.s_done, made(1, x + 1))
                    steps.mark(nc.vector.reduce_max(st[:, MX:MX + 1], s[:, near:near + CTX], AX_X))
                    if kind is not None:
                        dve.wait_ge(a.e_ready, made(1, x - 1))
                        mask = win_mask[:, kind, :] if a is win else nei_bias[:, kind, h, :]
                        steps.wait()
                        settled(dve)
                        steps.mark(nc.vector.tensor_tensor_reduce(a.sl[:, w_par(b, h), :], s[:, 0:near], mask, 1.0,
                                                                  st[:, MX:MX + 1], ALU.add, ALU.max, st[:, M2:M2 + 1]))
                    steps.wait()
                    mx = st[:, MX:MX + 1] if kind is None else st[:, M2:M2 + 1]
                    if a is win:
                        nm = nc.vector.tensor_scalar(st[:, NM:NM + 1], mx, sink[:, h:h + 1], -1.0, ALU.max, ALU.mult)
                    else:
                        nm = nc.vector.tensor_scalar(st[:, NM:NM + 1], mx, -1.0, None, ALU.mult)
                    nm.then_inc(a.nm_ready, 1)

                def take_p(i, b, h, kind, base):
                    x = (a.lay(l) * NT + 2 * i + b) * HEADS + h
                    n = CT if kind is None else a.near + CT
                    dve.wait_ge(a.p_turned, made(1, x + 1))
                    dve.wait_ge(a.pv_done, made(1, x - 1))
                    cut = n // 2
                    nc.vector.tensor_copy(a.pT[:, w_par(b, h), 0:cut, :].rearrange("p c n -> p (c n)"),
                                          ps[:, 5, 0:cut * P]).then_inc(a.pt_dve, 1)

                def finish(i, b, h, kind, base):
                    if h < HEADS - 1:
                        return
                    u, v = l * NT + 2 * i + b, a.lay(l) * NT + 2 * i + b
                    marks = 4 if a is win else 3
                    steps = Steps(dve, a.f_step, u * marks)
                    st = a.st[:, b]
                    dve.wait_ge(a.pv_done, made(1, (v + 1) * HEADS))
                    if kind is None:
                        steps.mark(nc.vector.tensor_copy(st[:, DN], st[:, D2]))
                    else:
                        steps.mark(nc.vector.tensor_tensor(st[:, DN], st[:, D1], st[:, D2], ALU.add))
                    steps.wait()
                    if a is win:
                        steps.mark(nc.vector.tensor_tensor(st[:, DN], st[:, DN], st[:, ES], ALU.add))
                        steps.wait()
                    steps.mark(nc.vector.reciprocal(st[:, RD], st[:, DN]))
                    steps.wait()
                    dve.wait_ge(a.stored[b], 16 * (a.lay(l) * NP + i))
                    out = a.out_t[:, b].rearrange("p (h n) -> p h n", n=HD)
                    steps.mark(nc.vector.tensor_tensor(out, ps[:, OUT_BANK[b], 0:GW].rearrange("p (h n) -> p h n", n=HD),
                                                       st[:, RD].unsqueeze(2).broadcast_to([P, HEADS, HD]), ALU.mult))
                    steps.wait()
                    nc.vector.tensor_tensor(a.out_t[:, b], a.out_t[:, b], a.gate_t[:, b], ALU.mult).then_inc(a.out_ready, 1)

                attend(dve, a, turn, maxima, take_p, finish)
                gate(dve, l, a.stage)
            def heads_of(x):
                return x.rearrange("p (h n) -> p h n", n=HD)

            def begin_states(a):
                dve.wait_ge(a.s_saved, 64 * a.lay(l))
                nc.vector.memset(a.sf[:, 0, :], 0.0)
                nc.vector.memset(a.sb[:, 0, :], 0.0).then_inc(states_clear, 1)
                dve.wait_ge(states_clear, a.lay(l) + 1)
                dve.wait_ge(a.s_in, 64 * (a.lay(l) + 1))
                settled(dve)

            def back_state(a, steps, i, b, c, bank, decay):
                steps.wait()
                dve.wait_ge(a.bs_ready, made(1, a.lay(l) * NT + 2 * i + b))
                settled(dve)
                steps.mark(nc.vector.tensor_copy(a.sb_all[:, bass.ds(back_tile(i, b), 1), :].rearrange("p a n -> p (a n)"),
                                                 a.sb[:, c, :]))
                dve.wait_ge(a.bkv_done, made(1, a.lay(l) * NT + 2 * i + b + 1))
                steps.wait()
                for g in range(2):
                    at = slice(g * HD, (g + 1) * HD)
                    last = nc.vector.scalar_tensor_tensor(a.sb[:, c, at], a.sb[:, c, at], decay(g),
                                                          ps[:, bank, KV_AT + g * HD:KV_AT + (g + 1) * HD], ALU.mult, ALU.add)
                last.then_inc(a.bs_ready, 1)

            def forward_state(a, u, v, c, decay):
                dve.wait_ge(a.kv_done, made(1, v + 1))
                dve.wait_ge(a.o_done, made(HEADS if a is hg else 1, u + 1))
                dve.wait_ge(a.sf_ready, made(1, v))
                for g in range(2):
                    at = slice(g * HD, (g + 1) * HD)
                    last = nc.vector.scalar_tensor_tensor(a.sf[:, c, at], a.sf[:, c, at], decay(g),
                                                          ps[:, 6, KV_AT + g * HD:KV_AT + (g + 1) * HD], ALU.mult, ALU.add)
                last.then_inc(a.sf_ready, 1)

            def scaled_out(a, steps, b, u, v, src, g_at, i):
                dve.wait_ge(a.r_ready, made(1, v + 1))
                dve.wait_ge(a.stored[b], 16 * (a.lay(l) * NP + i))
                steps.mark(nc.vector.tensor_tensor(heads_of(a.out_t[:, b]), heads_of(src),
                                                   a.st[:, b, 3].unsqueeze(2).broadcast_to([P, HEADS, HD]), ALU.mult))
                steps.wait()
                nc.vector.tensor_tensor(a.out_t[:, b], a.out_t[:, b], a.raw[:, b, g_at:g_at + GW], ALU.mult
                                        ).then_inc(a.out_ready, 1)

            dve.wait_ge(ret.tab_in, 144 * (l + 1))
            dve.wait_ge(lg_step, 8 * l)
            nc.vector.tensor_scalar(lg_t[:, 0], lg[:, :], -1.0, None, ALU.mult).then_inc(lg_step, 1)
            dve.wait_ge(lg_step, 8 * l + 1)
            nc.vector.tensor_tensor(lg_t[:, 1], lg_t[:, 0], lg[:, :], ALU.min).then_inc(lg_step, 1)
            dve.wait_ge(lg_act, 17 * l + 2)
            nc.vector.tensor_scalar(lg_t[:, 2], lg[:, :], 0.0, None, ALU.min).then_inc(lg_step, 1)
            dve.wait_ge(lg_step, 8 * l + 3)
            nc.vector.tensor_tensor(lg[:, :], lg_t[:, 2], lg_t[:, 1], ALU.subtract).then_inc(lg_step, 1)
            dve.wait_ge(lg_step, 8 * l + 4)
            for hp in range(2):
                at = slice(hp * HD, (hp + 1) * HD)
                nc.vector.tensor_copy(lgp[at, :, :], lg[at, :].rearrange("p (d g h) -> p d g h", d=2, g=2)[:, :, :, hp]
                                      ).then_inc(lg_step, 1)
            dve.wait_ge(lg_act, 17 * l + 9)
            nc.vector.tensor_scalar(key_decay[:, :, :], key_decay[:, :, :], HD ** -0.5, None, ALU.mult).then_inc(lg_step, 1)
            for h in range(HEADS):
                dve.wait_ge(lg_act, 17 * l + 9 + 2 * (h + 1))
                nc.vector.tensor_tensor(dtmp[:, 0], dtmp[:, 0], dtab[:, 2], ALU.mult).then_inc(dm_step, 1)
                nc.vector.tensor_tensor(dtmp[:, 1], dtmp[:, 1], dtab[:, 3], ALU.mult).then_inc(dm_step, 1)
                dve.wait_ge(dm_step, 3 * HEADS * l + 3 * h + 2)
                nc.vector.tensor_tensor(dmat[:, h % 2, h // 2], dtmp[:, 0], dtmp[:, 1], ALU.add).then_inc(dm_step, 1)
            dve.wait_ge(dm_step, 3 * HEADS * (l + 1))
            nc.vector.memset(lg_t[:, 0], 0.0).then_inc(lg_step, 1)
            dve.wait_ge(lg_step, 8 * (l + 1))
            begin_states(ret)

            def back_ret(i, b, c):
                u = l * NT + 2 * i + b
                v = ret.lay(l) * NT + 2 * i + b
                steps = Steps(dve, ret.b_step, u * 5)
                dve.wait_ge(ret.b_in[b], 32 * (l * NP + i + 1))
                dve.wait_ge(ret.bkv_done, made(1, v - 1))
                steps.wait()
                steps.mark(rope(steps, ret.x[:, b, 0:GW], ret.braw[:, b, 0:GW], ret.rope_b[:, b], ret.tmp[:, 0:GW], HEADS))
                steps.wait()
                nc.vector.tensor_tensor(heads_of(ret.kd[:, b]), heads_of(ret.x[:, b, 0:GW]),
                                        key_decay[:, 1].unsqueeze(2).broadcast_to([P, HEADS, HD]), ALU.mult
                                        ).then_inc(ret.bk_ready, 1)
                back_state(ret, steps, i, b, c, b, lambda g: pair_decay[:, 1, g:g + 1])

            backward(dve, back_ret)

            def rope_ret(i, b, c):
                u = l * NT + 2 * i + b
                v = ret.lay(l) * NT + 2 * i + b
                steps = Steps(dve, ret.x_step, u * 3)
                dve.wait_ge(ret.raw_in[b], 32 * (l * NP + i + 1))
                dve.wait_ge(ret.turned, made(1, u - 1))
                dve.wait_ge(ret.kf_ready, made(1, v))
                steps.wait()
                rope(steps, ret.x[:, b], ret.raw[:, b, 0:2 * GW], ret.rope_t[:, b], ret.tmp[:, :], 2 * HEADS
                     ).then_inc(ret.x_ready, 1)
                dve.wait_ge(ret.x_ready, made(1, u + 1))
                dve.wait_ge(ret.kv_done, made(1, v - 1))
                nc.vector.tensor_tensor(heads_of(ret.kd[:, b]), heads_of(ret.x[:, b, GW:2 * GW]),
                                        key_decay[:, 0].unsqueeze(2).broadcast_to([P, HEADS, HD]), ALU.mult
                                        ).then_inc(ret.kf_ready, 1)

            def rest_ret(i, b, c):
                u = l * NT + 2 * i + b
                v = ret.lay(l) * NT + 2 * i + b
                steps = Steps(dve, ret.f_step, u * 3)
                dve.wait_ge(ret.xT_ready, made(1, v + 1))
                dve.wait_ge(ret.o_done, made(1, u - 1))
                for d in range(2):
                    last = nc.vector.tensor_tensor(ret.qd[:, b, d], ret.xT[:, b, 0:2, :], row_decay[:, d], ALU.mult)
                last.then_inc(ret.qd_ready, 1)
                dve.wait_ge(ret.p_done, made(1, u + 1))
                nc.vector.tensor_tensor(ret.p[:, b].rearrange("p h g n -> p h (g n)"), ps[:, 2:4, 0:2 * P],
                                        dmat[:, :, :, :].rearrange("p h g n -> p h (g n)"), ALU.mult).then_inc(ret.p_ready, 1)
                dve.wait_ge(ret.o_done, made(1, u + 1))
                st = ret.st[:, b]
                o = ps[:, 4:6, 0:2 * HD].rearrange("p a (g n) -> p g a n", n=HD)

                def pairs(x):
                    return x.rearrange("p (g a) -> p g a", a=2)

                steps.mark(nc.vector.reduce_sum(pairs(st[:, 0]), o, AX_X))
                steps.wait()
                steps.mark(nc.vector.tensor_scalar(st[:, 0], st[:, 0], 1.0 / HD, None, ALU.mult))
                steps.wait()
                nc.vector.tensor_tensor(ret.o_c[:, b].rearrange("p (g a n) -> p g a n", g=2, a=2), o,
                                        pairs(st[:, 0]).unsqueeze(3).broadcast_to([P, 2, 2, HD]), ALU.subtract).then_inc(ret.ready, 1)
                forward_state(ret, u, v, c, lambda g: pair_decay[:, 0, g:g + 1])
                dve.wait_ge(ret.sq_ready, made(1, v + 1))
                nc.vector.reduce_sum(st[:, 1], heads_of(ret.o_sq[:, b]), AX_X).then_inc(ret.var_ready, 1)
                scaled_out(ret, steps, b, u, v, ret.o_c[:, b], 3 * GW, i)
                dve.wait_ge(ret.out_ready, made(1, v + 1))
                settled(dve)

            tiles(dve, rope_ret, rest_ret)
            gate(dve, l, RET)

            dve.wait_ge(hg.tab_in, 80 * (l + 1))
            begin_states(hg)

            def back_hg(i, b, c):
                u = l * NT + 2 * i + b
                v = hg.lay(l) * NT + 2 * i + b
                steps = Steps(dve, hg.b_step, u)
                dve.wait_ge(hg.ready, made(1, v + 1))
                dve.wait_ge(hg.b_in[b], 48 * (l * NP + i + 1))
                dve.wait_ge(hg.bkv_done, made(1, v - 1))
                nc.vector.tensor_tensor(hg.kd[:, b], hg.ed[:, b, 0:GW], hg.braw[:, b, 2 * GW:3 * GW], ALU.mult
                                        ).then_inc(hg.bk_ready, 1)
                back_state(hg, steps, i, b, c, b, lambda g: hg.ed[:, b, GW + g:GW + g + 1])

            backward(dve, back_hg)

            def nothing(i, b, c):
                pass

            def rest_hg(i, b, c):
                u = l * NT + 2 * i + b
                v = hg.lay(l) * NT + 2 * i + b
                steps = Steps(dve, hg.f_step, u * 5)
                dve.wait_ge(hg.raw_in[b], 16 * (l * NP + i + 1))
                dve.wait_ge(hg.f_exp, made(1, u + 1))
                dve.wait_ge(hg.kv_done, made(1, v - 1))
                nc.vector.tensor_tensor(hg.kd[:, b], hg.ed[:, b, 0:GW], hg.raw[:, b, 5 * GW:6 * GW], ALU.mult
                                        ).then_inc(hg.kf_ready, 1)
                dve.wait_ge(hg.xT_ready, made(1, v + 1))

                def decay_qk(g, d):
                    dve.wait_ge(hg.d_ready, made(4, u) + 2 * g + d + 1)
                    dve.wait_ge(hg.o_done, made(HEADS, u - 1) + 2 * g + 2)
                    x = hg.xT[:, b]
                    nc.vector.tensor_tensor(hg.q[:, g, d], hg.d[:, d], x[:, g, :].unsqueeze(1).broadcast_to([P, 8, P]), ALU.mult)
                    nc.vector.tensor_tensor(hg.k[:, g, d], hg.d[:, d, 0:LEVELS],
                                            x[:, 2 + 2 * d + g, :].unsqueeze(1).broadcast_to([P, LEVELS, P]), ALU.mult
                                            ).then_inc(hg.qk_ready, 1)

                def weights(h):
                    dve.wait_ge(hg.p_done, made(HEADS, u) + h + 1)
                    dve.wait_ge(hg.tc_ready, made(HEADS, u) + h)
                    n = 2 * SLOTS + 1
                    steps.mark(nc.vector.tensor_tensor(hg.w[:, :, :].rearrange("p s n -> p (s n)"),
                                                       ps[:, 4:6, :].rearrange("p a n -> p (a n)")[:, 0:n * 64],
                                                       keep[:, :, :].rearrange("p s n -> p (s n)"), ALU.mult))
                    steps.wait()
                    dve.wait_ge(hg.p_ready, made(HEADS, u) + h - 1)
                    nc.vector.tensor_reduce(hg.tc[:, h % 2, :], hg.w[:, :, :].rearrange("p s n -> p n s"), AX_X, ALU.add
                                            ).then_inc(hg.tc_ready, 1)

                for d in range(2):
                    decay_qk(0, d)
                for d in range(2):
                    decay_qk(1, d)
                for h in range(HEADS):
                    weights(h)
                forward_state(hg, u, v, c, lambda g: hg.ed[:, b, GW + g:GW + g + 1])
                dve.wait_ge(hg.sq_ready, made(1, v + 1))
                nc.vector.reduce_sum(hg.st[:, b, 1], heads_of(hg.o_sq[:, b]), AX_X).then_inc(hg.var_ready, 1)
                scaled_out(hg, steps, b, u, v, ps[:, 7, 0:GW], 3 * GW, i)

            tiles(dve, nothing, rest_hg)
            gate(dve, l, HGRN)

            def turned(i, b, c):
                u = l * NT + 2 * i + b
                dve.wait_ge(mx_turned, made(1, u + 1))
                dve.wait_ge(y_done, made(1, u - 1))
                nc.vector.tensor_copy(mT[:, b, 4:8, :], ps[:, 2 * b + 1, :].rearrange("p (k n) -> p k n", n=P)
                                      ).then_inc(mT_dve, 1)

            def residual(i, b, c):
                u = l * NT + 2 * i + b
                steps = Steps(dve, o_dve, u)
                y = y_t[:, b].rearrange("p (k n) -> p k n", n=GRP)
                dve.wait_ge(yr_ready, made(1, u + 1))
                dve.wait_ge(xo_in[b], 16 * (l * NP + i + 1))
                steps.mark(nc.vector.scalar_tensor_tensor(
                    y, ps[:, 4 + 2 * b:6 + 2 * b, :], stat[:, b, 2:3], gp_sb[:, c].rearrange("p (k n) -> p k n", n=GRP),
                    ALU.mult, ALU.mult))
                steps.wait()
                nc.vector.tensor_tensor(y_t[:, b], y_t[:, b], xo_t[:, b], ALU.add).then_inc(y_ready, 1)

            dve.wait_ge(wo_in, 48 * (l + 1))
            tiles(dve, turned, residual)
            gate(dve, l, OUTPUT)

    arena.close()


ACT_GROUPS = (0, 2, 4)
EXP_COLS = {1: GW, 3: GW, 5: GRP, 6: GRP, 7: GW}
last_exp = {1: 7, 3: 1, 5: 3, 6: 5, 7: 6}
SETUP_LB, SETUP_DVE, MOD_STEPS = 3, 12, 2
EMIT_DVE = 12


def kernel(**inputs):
    import numpy as _np
    import concourse.bacc as _bacc
    from concourse.bass_utils import run_bass_kernel_spmd as _run

    g = {k: _np.asarray(v) for k, v in inputs.items()}
    arrays = {
        "x_all": _np.concatenate([g["x_prompt"].reshape(CTX, D_MODEL), g["x_sample"].reshape(LAT, D_MODEL)]),
        "cond_in": _np.concatenate([g["c_ctx"].reshape(1, D_MODEL), g["c"].reshape(1, D_MODEL)]),
        "cache_win_k": g["cache_win_k"].reshape(DEPTH, PAST, 2 * HD),
        "cache_win_v": g["cache_win_v"].reshape(DEPTH, PAST, 2 * HD),
        "cache_na_k": g["cache_na_k"].reshape(DEPTH, PAST, GW),
        "cache_na_v": g["cache_na_v"].reshape(DEPTH, PAST, GW),
        "state_ret": g["state_ret"].reshape(DEPTH, 2, HEADS, HD, HD),
        "state_hgrn": g["state_hgrn"].reshape(DEPTH, 2, HEADS, HD, HD),
        "w_ada": g["w_ada"], "b_ada": g["b_ada"], "g_pre": g["g_pre"], "g_post": g["g_post"],
        "w_in": g["w_in"], "w_out": g["w_out"], "attn_sink": g["attn_sink"],
        "na_rpb": g["na_rpb"].reshape(DEPTH, HEADS * 15, 31),
        "ret_decay_logit": g["ret_decay_logit"].reshape(DEPTH, 2 * HEADS),
        "hgrn_lb_logit": g["hgrn_lb_logit"].reshape(DEPTH, 2 * GW),
        "table": TABLE, "rope": ROPE,
    }
    arrays = {k: _np.ascontiguousarray(v) for k, v in arrays.items()}
    nc = _bacc.Bacc("TRN2", target_bir_lowering=False, num_devices=1)
    ins = [nc.dram_tensor(f"in_{k}", v.shape, F32, kind="ExternalInput").ap() for k, v in arrays.items()]
    shapes = {"streams": (DEPTH + 1, NT * P, D_MODEL), "win_k": (DEPTH, CTX, 2 * HD), "win_v": (DEPTH, CTX, 2 * HD),
              "na_k": (DEPTH, CTX, GW), "na_v": (DEPTH, CTX, GW),
              "ret": (DEPTH, 2, HEADS, HD, HD), "hgrn": (DEPTH, 2, HEADS, HD, HD)}
    outs = [nc.dram_tensor(f"out_{k}", s, F32, kind="ExternalOutput").ap() for k, s in shapes.items()]
    build(nc, ins, outs)
    r = _run(nc, [{f"in_{k}": v for k, v in arrays.items()}], core_ids=[0]).results[0]
    y = r["out_streams"][DEPTH]
    return (y[:CTX].reshape(1, CTX, D_MODEL), y[CTX:].reshape(1, LAT, D_MODEL),
            r["out_win_k"].reshape(1, DEPTH, CTX, 2, HD), r["out_win_v"].reshape(1, DEPTH, CTX, 2, HD),
            r["out_na_k"].reshape(1, DEPTH, CTX, HEADS, HD), r["out_na_v"].reshape(1, DEPTH, CTX, HEADS, HD),
            r["out_ret"].reshape(1, DEPTH, 2, HEADS, HD, HD), r["out_hgrn"].reshape(1, DEPTH, 2, HEADS, HD, HD))
```

```python
from contextlib import ExitStack

import numpy as np

import concourse.bass as bass
from concourse import mybir

F32 = mybir.dt.float32
BF16 = mybir.dt.bfloat16
ALU = mybir.AluOpType
ACT = mybir.ActivationFunctionType
AX_X = mybir.AxisListType.X

P = 128
D_MODEL = 1024
KC = D_MODEL // P
DEPTH = 2
CTX, LAT, PAST = 256, 2048, 256
CT = CTX // P
NT = (CTX + LAT) // P
HD = 64
HEADS = 4
GW = HEADS * HD
IN_W = 4096
GRP = 512
NG = IN_W // GRP
ROW_W = IN_W + 2 * GW
NP = NT // 2
GRID_W = 64
WINDOW = 128
NA_ROWS, NA_COLS = 8, 16
EPS = 1e-6
NEG = -1e30
LB_FLOOR = 1e-30
LN_SPLIT = 2.0 ** -50
LEVELS = 7
SLOTS = LEVELS - 1
AHEAD = 2

KV_AT = 384
SLOT_N = NT + PAST // P
MX, M2, NM, ES, D1, D2, DN, RD = range(8)
BIAS_PARTS = ([(0, r, 7 - r, 0) for r in range(2)] + [(1, r, 5 - r, 0) for r in range(2)]
              + [(2, r, 3, r) for r in range(2)] + [(3, r, 3 - r, 2) for r in range(2)]
              + [(4, r, 1 - r, 2) for r in range(2)])

C_AQ, C_AK, C_AV, C_AG = 0, 256, 384, 512
C_BQ, C_BK, C_BV, C_BG = 768, 1024, 1280, 1536
C_CQ, C_CK, C_CV, C_CG = 1792, 2048, 2304, 2560
C_DQ, C_LF, C_DG, C_DI, C_KD = 2816, 3072, 3584, 3840, 4096


def shape_constants():
    t = np.arange(P)
    low = (t[:, None] >= 0)
    before = t[:, None] < t[None, :]
    cols = {"ident": np.eye(P)}
    window = np.zeros((P, 3, 3 * P))
    for kind, off in enumerate((0, P, 2 * P)):
        dist = np.abs(t[:, None] + off - np.arange(3 * P)[None, :])
        window[:, kind] = np.where(dist <= WINDOW, 0.0, NEG)
    cols["window"] = window.reshape(P, -1)
    ahead = t[None, :] - t[:, None]
    cols["dist_f"] = np.maximum(ahead, 0)
    cols["dist_b"] = np.maximum(-ahead, 0)
    cols["keep_f"] = (ahead >= 0) * HD ** -0.5
    cols["keep_b"] = (ahead <= 0) * HD ** -0.5
    cols["row_f"] = np.broadcast_to(t[None, :] + 1.0, (P, P))
    cols["row_b"] = np.broadcast_to(P - t[None, :], (P, P))
    cols["col_f"] = (P - 1.0 - t)[:, None]
    cols["col_b"] = (t * 1.0)[:, None]
    sums_f, sums_b = np.zeros((P, 8, P)), np.zeros((P, 8, P))
    for lv in range(LEVELS):
        s = 2 ** lv
        for i in range(P):
            m = i // (2 * s) * 2 * s + s
            if i >= m:
                sums_f[m:i + 1, lv, i] = 1
                sums_b[m:i, lv, i] = 1
            else:
                sums_f[i + 1:m, lv, i] = 1
                sums_b[i:m, lv, i] = 1
    sums_f[:, 7] = t[:, None] <= t[None, :]
    sums_b[:, 7] = t[:, None] >= t[None, :]
    cols["sums_f"], cols["sums_b"] = sums_f.reshape(P, -1), sums_b.reshape(P, -1)
    cols["after"] = (t[:, None] > t[None, :])
    cols["before"] = before
    keep = np.zeros((P, SLOTS + 1, 64))
    j, i = t % 64, np.arange(64)
    for lv in range(SLOTS):
        s = 2 ** lv
        same = (j[:, None] // (2 * s)) == (i[None, :] // (2 * s))
        keep[:, lv] = same & ((j[:, None] // s) % 2 != (i[None, :] // s) % 2)
    keep[:, SLOTS] = j[:, None] == i[None, :]
    cols["keep"] = keep.reshape(P, -1)
    cols["ones"] = np.ones((P, 1))
    at, parts = {}, []
    n = 0
    for name, a in cols.items():
        a = np.asarray(a, np.float32)
        at[name] = (n, n + a.shape[1])
        n += a.shape[1]
        parts.append(a)
    table = np.ascontiguousarray(np.concatenate(parts, axis=1))
    nf = HD // 4
    freq = (np.float32(10000.0) ** (-np.arange(nf, dtype=np.float32) / np.float32(nf))).astype(np.float32)
    pos = np.arange(LAT)
    rope = np.zeros((CTX + LAT + PAST, 2, HD), np.float32)
    rope[:, 0] = 1.0
    for half, place in enumerate((pos // GRID_W, pos % GRID_W)):
        ang = (place.astype(np.float32)[:, None] * freq[None, :]).astype(np.float32)
        c, s = np.cos(ang), np.sin(ang)
        o = half * 2 * nf
        rope[CTX:CTX + LAT, 0, o:o + nf] = c
        rope[CTX:CTX + LAT, 0, o + nf:o + 2 * nf] = c
        rope[CTX:CTX + LAT, 1, o:o + nf] = -s
        rope[CTX:CTX + LAT, 1, o + nf:o + 2 * nf] = s
    return at, table, rope.reshape(-1, 2 * HD)


AT, TABLE, ROPE = shape_constants()


def made(n, units=0):
    return n * (units + AHEAD)


class Steps:

    def __init__(self, eng, sem, base):
        self.eng, self.sem, self.base, self.n = eng, sem, base, 0

    def mark(self, ins):
        ins.then_inc(self.sem, 1)
        self.n += 1

    def wait(self):
        self.eng.wait_ge(self.sem, self.base + self.n)


def build(nc, ins, outs):
    (x_all, cond_in, cwk, cwv, cnk, cnv, st_ret, st_hgrn, w_ada, b_ada, g_pre, g_post, w_in, w_out,
     sink_in, rpb_in, decay_in, lb_in, table_in, rope_in) = ins
    streams, out_wk, out_wv, out_nk, out_nv, out_ret, out_hgrn = outs

    rows = nc.dram_tensor("projected", (NT * P, ROW_W), F32, kind="Internal").ap()
    mixed = nc.dram_tensor("mixed", (NT * P, D_MODEL), F32, kind="Internal").ap()
    gate_row = nc.dram_tensor("gate_row", (2, D_MODEL), F32, kind="Internal").ap()
    skew = nc.dram_tensor("skew", (HEADS * 15 * 64 * 128,), F32, kind="Internal").ap()

    nc.disable_value_cache = True
    arena = ExitStack()
    arena.enter_context(nc.allow_non_contiguous_dma(reason="vectors of the model, a few thousand elements"))

    def sb(stack, name, shape, dt=F32):
        return stack.enter_context(nc.sbuf_tensor(name, shape, dt))

    def sem(name):
        return arena.enter_context(nc.semaphore(name))

    def pair(name):
        return [sem(f"{name}{b}") for b in range(2)]

    def skew_ap(offset, pattern):
        return bass.AP(tensor=skew.tensor, offset=offset, ap=pattern)

    ident = sb(arena, "ident", [P, P])
    eps = sb(arena, "eps", [P, 1])
    ones = sb(arena, "ones", [P, 1])
    lbd = sb(arena, "lbd", [P, DEPTH, 2 * GW])
    oml = sb(arena, "oml", [P, DEPTH, 2 * GW])
    cond = sb(arena, "cond", [P, KC, 2])
    cond_e = sb(arena, "cond_e", [P, KC, 2])
    mod = sb(arena, "mod", [P, 3 * KC, 2])
    lbd_l = sb(arena, "lbd_l", [P, 2 * GW])
    oml_l = sb(arena, "oml_l", [P, 2 * GW])
    mod_w = sb(arena, "mod_w", [P, 5 * KC])
    stat = sb(arena, "stat", [P, 2, 8])
    ps = arena.enter_context(nc.psum_tensor("ps", [P, 8, GRP], F32))

    STAGES = 7
    (MODULATE, PROJECT, WIN, NEI, RET, HGRN, OUTPUT) = range(STAGES)

    with ExitStack() as s:
        w_sb = sb(s, "w_sb", [P, KC, IN_W])
        with ExitStack() as s2:
            wa = sb(s2, "wa", [P, 2, KC, 3 * P])
            lb_raw = sb(s2, "lb_raw", [P, DEPTH, 2 * GW])
            neg_t = sb(s2, "neg_t", [P, 15 * HEADS * 64])
        xt = sb(s, "xt", [P, 2, D_MODEL])
        hT = sb(s, "hT", [P, 2, KC, P])
        row_t = sb(s, "row_t", [P, 2, ROW_W])
        e_t = sb(s, "e_t", [P, 3, GRP])
        sq_junk = sb(s, "sq_junk", [P, D_MODEL], BF16)
    with ExitStack() as s:
        wo_sb = sb(s, "wo_sb", [P, KC, D_MODEL])
        gp_sb = sb(s, "gp_sb", [P, 2, D_MODEL])
        mx_t = sb(s, "mx_t", [P, 2, D_MODEL])
        xo_t = sb(s, "xo_t", [P, 2, D_MODEL])
        mT = sb(s, "mT", [P, 2, KC, P])
        y_t = sb(s, "y_t", [P, 2, D_MODEL])

    class Group:
        pass

    def attention(s, name, near, nkv, cq, ck, cv, cg, cache_k, cache_v, col):
        a = Group()
        a.near, a.nkv, a.cq, a.ck, a.cv, a.cg, a.col = near, nkv, cq, ck, cv, cg, col
        a.cache_k, a.cache_v = cache_k, cache_v
        a.kT = sb(s, f"{name}_kT", [HD, nkv, SLOT_N * P])
        a.v = sb(s, f"{name}_v", [P, SLOT_N, nkv * HD])
        a.k_raw = sb(s, f"{name}_k_raw", [P, 2, nkv * HD])
        a.q_raw = sb(s, f"{name}_q_raw", [P, 2, GW])
        a.gate_t = sb(s, f"{name}_gate_t", [P, 2, GW])
        a.out_t = sb(s, f"{name}_out_t", [P, 2, GW])
        a.qT = sb(s, f"{name}_qT", [HD, 2, HEADS, P])
        a.sl = sb(s, f"{name}_sl", [P, 2, near * P])
        a.e = sb(s, f"{name}_e", [P, 2, (near + CT) * P])
        a.pT = sb(s, f"{name}_pT", [P, 2, near + CT, P])
        a.st = sb(s, f"{name}_st", [P, 2, 8, HEADS])
        return a

    with ExitStack() as s:
        win = attention(s, "win", 3, 2, C_AQ, C_AK, C_AV, C_AG, cwk, cwv, 0)
        win_mask = sb(s, "win_mask", [P, 3, 3 * P])
        sink = sb(s, "sink", [P, HEADS])
        win.k_rope = sb(s, "win_k_rope", [P, 2, 2 * HD])
        win.q_rope = sb(s, "win_q_rope", [P, 2, GW])
        win.rope_t = sb(s, "win_rope_t", [P, 2, 2 * HD])
        win.rope_q = sb(s, "win_rope_q", [P, 2, 2 * HD])
        win.rot_tmp = sb(s, "win_rot_tmp", [P, GW])
    with ExitStack() as s:
        nei = attention(s, "nei", 5, 4, C_BQ, C_BK, C_BV, C_BG, cnk, cnv, GW)
        nei_bias = sb(s, "nei_bias", [P, 5, HEADS, 5 * P])
    def scan(s, name, stage, stream_w, back_w, col):
        a = Group()
        a.name, a.stage, a.col = name, stage, col
        a.raw = sb(s, f"{name}_raw", [P, 2, stream_w])
        a.braw = sb(s, f"{name}_braw", [P, 2, back_w])
        a.kd = sb(s, f"{name}_kd", [P, 2, GW])
        a.sf = sb(s, f"{name}_sf", [P, 2, P])
        a.sb = sb(s, f"{name}_sb", [P, 2, P])
        a.sb_all = sb(s, f"{name}_sb_all", [P, NT, P])
        a.sb_at = sb(s, f"{name}_sb_at", [P, 2, P])
        a.out_t = sb(s, f"{name}_out_t", [P, 2, GW])
        a.o_c = sb(s, f"{name}_o_c", [P, 2, GW])
        a.o_sq = sb(s, f"{name}_o_sq", [P, 2, GW])
        a.st = sb(s, f"{name}_st", [P, 2, 4, HEADS])
        return a

    with ExitStack() as s:
        ret = scan(s, "ret", RET, 4 * GW, 2 * GW, 2 * GW)
        ret.rope_t = sb(s, "ret_rope_t", [P, 2, 2 * HD])
        ret.rope_b = sb(s, "ret_rope_b", [P, 2, 2 * HD])
        ret.tmp = sb(s, "ret_tmp", [P, 2 * GW])
        ret.x = sb(s, "ret_x", [P, 2, 2 * GW])
        ret.xT = sb(s, "ret_xT", [P, 2, 4, P])
        ret.qd = sb(s, "ret_qd", [P, 2, 2, 2, P])
        ret.p = sb(s, "ret_p", [P, 2, 2, 2, P])
        lg = sb(s, "lg", [P, 2 * HEADS])
        lg_t = sb(s, "lg_t", [P, 3, 2 * HEADS])
        lgp = sb(s, "lgp", [P, 2, 2])
        pair_decay = sb(s, "pair_decay", [P, 2, 2])
        key_decay = sb(s, "key_decay", [P, 2, HEADS])
        row_decay = sb(s, "row_decay", [P, 2, 2, P])
        dmat = sb(s, "dmat", [P, 2, 2, P])
        dtab = sb(s, "dtab", [P, 6, P])
        dcol = sb(s, "dcol", [P, 2])
        dtmp = sb(s, "dtmp", [P, 2, P])
    with ExitStack() as s:
        hg = scan(s, "hg", HGRN, 7 * GW, 3 * GW, 3 * GW)
        hg.ed = sb(s, "hg_ed", [P, 2, GW + 2])
        hg.xT = sb(s, "hg_xT", [P, 2, 6, P])
        hg.d = sb(s, "hg_d", [P, 2, 2, 8, P])
        hg.q = sb(s, "hg_q", [P, 2, 2, LEVELS, P])
        hg.k = sb(s, "hg_k", [P, 2, 2, LEVELS, P])
        hg.qx = sb(s, "hg_qx", [P, 2, 2, 2, P])
        hg.ks = sb(s, "hg_ks", [P, 2, 2, P])
        hg.w = sb(s, "hg_w", [P, SLOTS + 1, 64])
        hg.tc = sb(s, "hg_tc", [P, 2, 64])
        hg.p = sb(s, "hg_p", [P, 2, P])
        sums = sb(s, "sums", [P, 2, 8, P])
        keep = sb(s, "keep", [P, SLOTS + 1, 64])
        past = sb(s, "past", [P, 2, P])

    passed = sem("passed")
    consts_in = sem("consts_in")
    lb_loaded = sem("lb_loaded")
    setup = sem("setup")
    setup_act = sem("setup_act")
    x_copied = sem("x_copied")
    stage_done = sem("stage_done")
    wa_in, wa_used = pair("wa_in"), sem("wa_used")
    modw_in = sem("modw_in")
    ada_done = sem("ada_done")
    mod_ready = sem("mod_ready")
    gate_out = sem("gate_out")
    w_loaded = [sem(f"w_loaded{g}") for g in range(NG)]
    x_in, x_normed = pair("x_in"), sem("x_normed")
    act_step, dve_step = sem("act_step"), sem("dve_step")
    rstd_ready = sem("rstd_ready")
    x_turned = sem("x_turned")
    h_act, h_dve = sem("h_act"), sem("h_dve")
    proj_done = sem("proj_done")
    exp_ready = sem("exp_ready")
    ln_in, ln_out = sem("ln_in"), sem("ln_out")
    out_g = [sem(f"out_g{g}") for g in range(NG)]
    bounds_ready = sem("bounds_ready")
    row_stored = pair("row_stored")
    kv_saved = sem("kv_saved")
    wo_in = sem("wo_in")
    mx_in, xo_in, mx_turned = pair("mx_in"), pair("xo_in"), sem("mx_turned")
    mT_act, mT_dve = sem("mT_act"), sem("mT_dve")
    y_done, yr_ready, y_ready, y_stored = sem("y_done"), sem("yr_ready"), sem("y_ready"), pair("y_stored")

    def gate(eng, l, stage):
        settled(eng)
        eng.drain().then_inc(stage_done, 1)
        eng.wait_ge(stage_done, (l * STAGES + stage + 1) * 5)
        settled(eng)

    def settled(eng):
        eng.sem_inc(passed, 1)

    win.stage, nei.stage = WIN, NEI
    both_v_in, both_gate_in, both_stored = pair("v_in"), pair("gate_in"), pair("attention_stored")
    both = [sem(x) for x in ("k_turned", "k_out", "q_turned", "q_ready", "s_done", "nm_ready", "e_ready", "p_turned",
                             "pt_act", "pt_dve", "pv_done", "attention_ready", "s_step")]
    win.lay, nei.lay = (lambda l: 2 * l), (lambda l: 2 * l + 1)
    for name, a in (("win", win), ("nei", nei)):
        a.k_in, a.q_in, a.gate_in = pair(f"{name}_k_in"), pair(f"{name}_q_in"), both_gate_in
        a.v_in, a.stored = both_v_in, both_stored
        (a.k_turned, a.k_out, a.q_turned, a.q_ready, a.s_done, a.nm_ready, a.e_ready, a.p_turned, a.pt_act, a.pt_dve,
         a.pv_done, a.out_ready, a.s_step) = both
        a.f_step = sem(f"{name}_f_step")
    win.k_rot, win.q_rot, win.r_step = (sem(f"win_{x}") for x in ("k_rot", "q_rot", "r_step"))
    ret.lay, hg.lay = win.lay, nei.lay
    SHARED = ("bk_ready", "bkv_done", "bs_ready", "xT_ready", "sb_ready", "kf_ready", "kv_done", "sf_ready",
              "var_ready", "r_ready", "out_ready", "n_step", "s_in", "s_saved", "ready")
    shared = [sem(f"scan_{x}") for x in SHARED]
    ret.stored = hg.stored = pair("scan_stored")
    ret.val_in = hg.val_in = pair("scan_val_in")
    for a in (ret, hg):
        (a.bk_ready, a.bkv_done, a.bs_ready, a.xT_ready, a.sb_ready, a.kf_ready, a.kv_done, a.sf_ready,
         a.var_ready, a.r_ready, a.out_ready, a.n_step, a.s_in, a.s_saved, a.ready) = shared
        a.b_in, a.raw_in = pair(f"{a.name}_b_in"), pair(f"{a.name}_raw_in")
        a.tab_in, a.turned, a.p_done, a.p_ready, a.o_done, a.x_ready, a.f_step = (
            sem(f"{a.name}_{x}") for x in ("tab_in", "turned", "p_done", "p_ready", "o_done", "x_ready", "f_step"))
    ret.b_step, ret.x_step, ret.qd_ready = sem("ret_b_step"), sem("ret_x_step"), sem("ret_qd_ready")
    hg.b_step, hg.gated = hg.f_step, sem("hg_gated")
    hg.f_turned, hg.f_exp, hg.e_done, hg.d_ready, hg.qk_ready, hg.tc_ready = (
        sem(f"hg_{x}") for x in ("f_turned", "f_exp", "e_done", "d_ready", "qk_ready", "tc_ready"))
    lg_step, lg_act, dm_step, states_clear = (sem(x) for x in ("lg_step", "lg_act", "dm_step", "states_clear"))
    mask_in, bias_in, skew_in, bias_clear, neg_ready, skew_clear = (
        sem(x) for x in ("mask_in", "bias_in", "skew_in", "bias_clear", "neg_ready", "skew_clear"))

    OUT_BANK = (7, 0)

    def score_banks(p):
        return ps[:, 1 + 2 * p:3 + 2 * p, :].rearrange("p a n -> p (a n)")

    def w_par(b, h):
        return h % 2

    def attend(eng, a, first, score, turn, last):
        def both(i, kinds, base):
            units = [(i, b, h, kinds[b], base[b]) for b in range(2) for h in range(HEADS)]
            for b in range(2):
                first(i, b)
            for n in range(len(units) + 2):
                if n < len(units):
                    score(*units[n])
                if 1 <= n <= len(units):
                    turn(*units[n - 1])
                if n >= 2 and last:
                    last(*units[n - 2])
        edge = a.near // 2
        top = CT + (NT - CT) - a.near
        both(0, (None, None), (0, 0))
        both(1, (0, 1), (CT, CT + max(0, 1 - edge)))
        with eng.Fori(2, NP - 1) as i:
            both(i, (edge, edge), (2 * i - edge, 2 * i + 1 - edge))
        last_kind = 2 * edge
        both(NP - 1, (last_kind - 1, last_kind), (min(top, NT - 2 - edge), top))

    def back_tile(i, b):
        return 1 - b if isinstance(i, int) and i == 0 else NT + 1 - 2 * i - b

    def backward(eng, unit):
        for b in range(2):
            unit(0, b, 0)
        with eng.Fori(1, NP) as i:
            for b in range(2):
                unit(i, b, 1)

    def state_ap(dram, l, direction):
        return [dram[bass.ds(l, 1), direction, 2 * g:2 * g + 2, :, :].rearrange("a h d e -> (a h d) e")
                for g in range(2)]

    def woven(eng, start, end, work):
        start(0, 0, 0)
        end(0, 0, 0)
        work(0, 0, 0, (0, 1, 0))
        work(0, 1, 0, (1, 0, 1))
        with eng.Fori(1, NP - 1) as i:
            work(i, 0, 1, (i, 1, 1))
            work(i, 1, 1, (i + 1, 0, 1))
        work(NP - 1, 0, 1, (NP - 1, 1, 1))
        work(NP - 1, 1, 1, None)

    def tok(t):
        return bass.ds(t * P, P)

    def tiles(eng, pre, post):
        pre(0, 0, 0)
        pre(0, 1, 0)
        post(0, 0, 0)
        pre(1, 0, 1)
        post(0, 1, 0)
        with eng.Fori(1, NP - 1) as i:
            pre(i, 1, 1)
            post(i, 0, 1)
            pre(i + 1, 0, 1)
            post(i, 1, 1)
        pre(NP - 1, 1, 1)
        post(NP - 1, 0, 1)
        post(NP - 1, 1, 1)

    def nothing(i, b, c):
        pass

    block = arena.enter_context(nc.Block())

    @block.sync
    def _(sp):
        def cols(name, part=P):
            a, b = AT[name]
            return table_in[0:part, a:b]

        sp.dma_start(ident[:, :], cols("ident")).then_inc(consts_in, 16)
        sp.dma_start(cond[:, :, 0], cond_in[0, :].rearrange("(k p) -> p k", p=P)).then_inc(consts_in, 16)
        sp.dma_start(cond[:, :, 1], cond_in[1, :].rearrange("(k p) -> p k", p=P)).then_inc(consts_in, 16)
        sp.dma_start(lb_raw[:, 0, :], lb_in[0:1, :].broadcast_to([P, 2 * GW])).then_inc(lb_loaded, 16)
        for d in range(1, DEPTH):
            sp.dma_start(lb_raw[:, d, :], lb_in[d:d + 1, :].broadcast_to([P, 2 * GW])).then_inc(lb_loaded, 16)
        with sp.Fori(0, DEPTH) as l:
            for part, at, n in ((b_ada, 0, 3 * KC), (g_pre, 3 * KC, KC), (g_post, 4 * KC, KC)):
                sp.dma_start(mod_w[:, at:at + n], part[bass.ds(l, 1), :].rearrange("a (n p) -> p (a n)", p=P)
                             ).then_inc(modw_in, 16)
            for n in range(KC):
                sp.wait_ge(wa_used, made(1, l * KC + n - 1))
                sp.dma_start(wa[:, n % 2], w_ada[bass.ds(l, 1), :, n * 3 * P:(n + 1) * 3 * P].rearrange(
                    "a (k p) n -> p (a k) n", p=P)).then_inc(wa_in[n % 2], 16)
            for g in range(NG):
                src = w_in[bass.ds(l, 1)].rearrange("a (k p) n -> p (a k) n", p=P)
                if g < NG - 1:
                    sp.dma_start(w_sb[:, :, g * GRP:(g + 1) * GRP], src[:, :, g * GRP:(g + 1) * GRP]
                                 ).then_inc(w_loaded[g], 16)
                else:
                    for at, frm in ((C_DG, IN_W - GW), (C_DI, IN_W - GRP)):
                        sp.dma_start(w_sb[:, :, at:at + GW], src[:, :, frm:frm + GW]).then_inc(w_loaded[g], 16)
            sp.wait_ge(x_copied, 16)
            gate(sp, l, MODULATE)

            with sp.Fori(0, NP) as i:
                for b in range(2):
                    t = 2 * i + b
                    sp.wait_ge(x_turned, made(1, l * NT + t - 1))
                    sp.dma_start(xt[:, b], streams[bass.ds(l, 1), tok(t), :].rearrange("a p n -> p (a n)")
                                 ).then_inc(x_in[b], 16)
            gate(sp, l, PROJECT)
            for a in (win, nei):
                if a is win:
                    sp.dma_start(win_mask[:, :, :].rearrange("p a n -> p (a n)"), cols("window")).then_inc(mask_in, 16)
                    sp.dma_start(sink[:, :], sink_in[bass.ds(l, 1), :].broadcast_to([P, HEADS])).then_inc(mask_in, 16)

                def load_kv(i, b, k_src, v_src, t):
                    sp.wait_ge(a.k_turned, made(1, a.lay(l) * SLOT_N + 2 * i + b - 1))
                    settled(sp)
                    sp.dma_start(a.k_raw[:, b], k_src).then_inc(a.k_in[b], 16)
                    if a is win:
                        sp.dma_start(a.rope_t[:, b], rope_in[tok(t), :]).then_inc(a.k_in[b], 16)
                    sp.dma_start(a.v[:, bass.ds(t, 1), :].rearrange("p a n -> p (a n)"), v_src).then_inc(a.v_in[b], 16)

                with sp.Fori(0, NP) as i:
                    for b in range(2):
                        t = 2 * i + b
                        load_kv(i, b, rows[tok(t), a.ck:a.ck + a.nkv * HD], rows[tok(t), a.cv:a.cv + a.nkv * HD], t)
                for b in range(2):
                    load_kv(NP, b, a.cache_k[bass.ds(l, 1), b * P:(b + 1) * P, :].rearrange("a p n -> p (a n)"),
                            a.cache_v[bass.ds(l, 1), b * P:(b + 1) * P, :].rearrange("a p n -> p (a n)"), NT + b)
                with sp.Fori(0, NP) as i:
                    for b in range(2):
                        t = 2 * i + b
                        if a is win:
                            sp.wait_ge(a.q_rot, made(1, l * NT + t - 1))
                        else:
                            sp.wait_ge(a.q_turned, made(1, a.lay(l) * NT + t - 1))
                        settled(sp)
                        sp.dma_start(a.q_raw[:, b], rows[tok(t), a.cq:a.cq + GW]).then_inc(a.q_in[b], 16)
                        if a is win:
                            sp.dma_start(a.rope_q[:, b], rope_in[tok(t), :]).then_inc(a.q_in[b], 16)
                        sp.wait_ge(a.out_ready, made(1, a.lay(l) * NT + t - 1))
                        settled(sp)
                        sp.dma_start(a.gate_t[:, b], rows[tok(t), a.cg:a.cg + GW]).then_inc(a.gate_in[b], 16)
                gate(sp, l, a.stage)
            for a in (ret, hg):
                if a is ret:
                    sp.dma_start(lg[:, :], decay_in[bass.ds(l, 1), :].broadcast_to([P, 2 * HEADS])).then_inc(a.tab_in, 16)
                    for k, name in enumerate(("dist_f", "dist_b", "keep_f", "keep_b", "row_f", "row_b")):
                        sp.dma_start(dtab[:, k], cols(name)).then_inc(a.tab_in, 16)
                    for k, name in enumerate(("col_f", "col_b")):
                        sp.dma_start(dcol[:, k:k + 1], cols(name)).then_inc(a.tab_in, 16)
                else:
                    for k, name in enumerate(("sums_f", "sums_b")):
                        sp.dma_start(sums[:, k].rearrange("p s n -> p (s n)"), cols(name)).then_inc(a.tab_in, 16)
                    sp.dma_start(keep[:, :, :].rearrange("p s n -> p (s n)"), cols("keep")).then_inc(a.tab_in, 16)
                    for k, name in enumerate(("after", "before")):
                        sp.dma_start(past[:, k], cols(name)).then_inc(a.tab_in, 16)
                for d, state in enumerate((a.sf, a.sb)):
                    for g, src in enumerate(state_ap(st_ret if a is ret else st_hgrn, l, d)):
                        sp.dma_start(state[:, 1, g * HD:(g + 1) * HD], src).then_inc(a.s_in, 16)

                def load_back(i, b, c):
                    t = back_tile(i, b)
                    u = l * NT + 2 * i + b
                    v = a.lay(l) * NT + 2 * i + b
                    sp.wait_ge(a.bk_ready, made(1, v - 1))
                    sp.wait_ge(a.bkv_done, made(1, v - 1))
                    settled(sp)
                    if a is ret:
                        sp.dma_start(a.braw[:, b], rows[tok(t), C_CK:C_CK + 2 * GW]).then_inc(a.b_in[b], 16)
                        sp.dma_start(a.rope_b[:, b], rope_in[tok(t), :]).then_inc(a.b_in[b], 16)
                    else:
                        sp.dma_start(a.braw[:, b, 0:GW], rows[tok(t), C_LF + GW:C_LF + 2 * GW]).then_inc(a.b_in[b], 16)
                        sp.dma_start(a.braw[:, b, GW:2 * GW], rows[tok(t), C_DI:C_DI + GW]).then_inc(a.b_in[b], 16)
                        sp.dma_start(a.braw[:, b, 2 * GW:3 * GW], rows[tok(t), C_KD + GW:C_KD + 2 * GW]).then_inc(a.b_in[b], 16)

                backward(sp, load_back)
                with sp.Fori(0, NP) as i:
                    for b in range(2):
                        t = 2 * i + b
                        v = a.lay(l) * NT + t
                        sp.wait_ge(a.kf_ready, made(1, v - 1))
                        if a is ret:
                            sp.wait_ge(a.x_ready, made(1, l * NT + t - 1))
                            settled(sp)
                            sp.dma_start(a.raw[:, b, 0:2 * GW], rows[tok(t), C_CQ:C_CV]).then_inc(a.raw_in[b], 16)
                            sp.dma_start(a.rope_t[:, b], rope_in[tok(t), :]).then_inc(a.raw_in[b], 16)
                        else:
                            sp.wait_ge(a.e_done, made(8, l * NT + t - 1))
                            settled(sp)
                            sp.dma_start(a.raw[:, b, 0:3 * GW], rows[tok(t), C_DQ:C_DG]).then_inc(a.raw_in[b], 16)
                            sp.dma_start(a.raw[:, b, 5 * GW:7 * GW], rows[tok(t), C_KD:C_KD + 2 * GW]).then_inc(a.raw_in[b], 16)
                        if a is ret:
                            sp.wait_ge(a.out_ready, made(1, v - 1))
                        else:
                            sp.wait_ge(a.gated, made(1, l * NT + t - 1))
                        sp.wait_ge(a.kv_done, made(1, v - 1))
                        settled(sp)
                        if a is ret:
                            sp.dma_start(a.raw[:, b, 2 * GW:4 * GW], rows[tok(t), C_CV:C_CV + 2 * GW]).then_inc(a.val_in[b], 16)
                        else:
                            sp.dma_start(a.raw[:, b, 3 * GW:5 * GW], rows[tok(t), C_DG:C_DG + 2 * GW]).then_inc(a.val_in[b], 16)
                gate(sp, l, a.stage)
            sp.dma_start(wo_sb[:, :, :], w_out[bass.ds(l, 1)].rearrange("a (k p) n -> p (a k) n", p=P)
                         ).then_inc(wo_in, 16)
            for c in range(2):
                sp.dma_start(gp_sb[:, c], gate_row[c:c + 1, :].broadcast_to([P, D_MODEL])).then_inc(wo_in, 16)
            with sp.Fori(0, NP) as i:
                for b in range(2):
                    t = 2 * i + b
                    sp.wait_ge(mx_turned, made(1, l * NT + t - 1))
                    sp.dma_start(mx_t[:, b], mixed[tok(t), :]).then_inc(mx_in[b], 16)
                    sp.wait_ge(y_ready, made(1, l * NT + t - 1))
                    sp.dma_start(xo_t[:, b], streams[bass.ds(l, 1), tok(t), :].rearrange("a p n -> p (a n)")
                                 ).then_inc(xo_in[b], 16)
            gate(sp, l, OUTPUT)

    @block.gpsimd
    def _(pool):
        pool.dma_start(streams[0], x_all).then_inc(x_copied, 16)
        pool.wait_ge(neg_ready, 1)
        pool.dma_start(skew.rearrange("(p n) -> p n", p=P), neg_t[:, :]).then_inc(skew_clear, 16)
        pool.wait_ge(skew_clear, 16)
        with pool.Fori(0, DEPTH) as l:
            pool.wait_ge(mod_ready, l + 1)
            settled(pool)
            for c in range(2):
                pool.dma_start(gate_row[c, :].rearrange("(k p) -> p k", p=P), mod[:, 2 * KC:3 * KC, c]
                               ).then_inc(gate_out, 16)
            pool.wait_ge(gate_out, 32 * (l + 1))
            settled(pool)
            gate(pool, l, MODULATE)
            with pool.Fori(0, NP) as i:
                for b in range(2):
                    t = 2 * i + b
                    for g in range(NG):
                        pool.wait_ge(out_g[g], made(1, l * NT + t + 1))
                    settled(pool)
                    pool.dma_start(rows[tok(t), :], row_t[:, b]).then_inc(row_stored[b], 16)
            for b in range(2):
                pool.wait_ge(row_stored[b], 16 * (l + 1) * NP)
            settled(pool)
            for dst, at, n in ((out_wk, C_AK, P), (out_wv, C_AV, P), (out_nk, C_BK, GW), (out_nv, C_BV, GW)):
                pool.dma_start(dst[bass.ds(l, 1)].rearrange("a t n -> t (a n)"), rows[0:CTX, at:at + n]
                               ).then_inc(kv_saved, 16)
            pool.wait_ge(kv_saved, 64 * (l + 1))
            settled(pool)
            gate(pool, l, PROJECT)
            for a in (win, nei):
                if a is win:
                    rpb = rpb_in[bass.ds(l, 1)].rearrange("a r c -> (a r) c")
                    inner = NA_COLS // 2
                    for q0, nq in [(q, 1) for q in range(inner)] + [(inner, GRID_W - 2 * inner + 1)] + \
                            [(q, 1) for q in range(GRID_W - inner + 1, GRID_W)]:
                        first = min(max(q0 - inner, 0), GRID_W - NA_COLS)
                        pool.dma_start(skew_ap(q0 * P + first - q0 + 63, [[64 * P, HEADS * 15], [P, nq], [1, NA_COLS]]),
                                     rpb[:, first - q0 + 15:first - q0 + 15 + NA_COLS].unsqueeze(1).broadcast_to(
                                         [HEADS * 15, nq, NA_COLS])).then_inc(skew_in, 16)
                else:
                    nc.gpsimd.memset(nei_bias[:, :, :, :], NEG).then_inc(bias_clear, 1)
                    pool.wait_ge(bias_clear, l + 1)
                    settled(pool)
                    for kind, h0, r0, first_row in BIAS_PARTS:
                        for h in range(HEADS):
                            pool.dma_start(nei_bias[64 * h0:64 * h0 + 64, kind, h, first_row * 64:first_row * 64 + 512].rearrange(
                                "p (j n) -> p j n", n=64),
                                skew_ap((h * 15 + r0) * 64 * P + 63, [[P - 1, 64], [64 * P, NA_ROWS], [1, 64]])
                                ).then_inc(bias_in, 16)
                with pool.Fori(0, NP) as i:
                    for b in range(2):
                        t = 2 * i + b
                        pool.wait_ge(a.out_ready, made(1, a.lay(l) * NT + t + 1))
                        settled(pool)
                        pool.dma_start(mixed[tok(t), a.col:a.col + GW], a.out_t[:, b]).then_inc(a.stored[b], 16)
                for b in range(2):
                    pool.wait_ge(a.stored[b], 16 * NP * (a.lay(l) + 1))
                if a is win:
                    pool.wait_ge(skew_in, 16 * NA_COLS * (l + 1))
                settled(pool)
                gate(pool, l, a.stage)
            for a in (ret, hg):
                with pool.Fori(0, NP) as i:
                    for b in range(2):
                        t = 2 * i + b
                        pool.wait_ge(a.out_ready, made(1, a.lay(l) * NT + t + 1))
                        settled(pool)
                        pool.dma_start(mixed[tok(t), a.col:a.col + GW], a.out_t[:, b]).then_inc(a.stored[b], 16)
                pool.wait_ge(a.sf_ready, made(1, (a.lay(l) + 1) * NT))
                pool.wait_ge(a.bs_ready, made(1, (a.lay(l) + 1) * NT))
                settled(pool)
                for d, state in enumerate((a.sf, a.sb)):
                    for g, dst in enumerate(state_ap(out_ret if a is ret else out_hgrn, l, d)):
                        pool.dma_start(dst, state[:, 0, g * HD:(g + 1) * HD]).then_inc(a.s_saved, 16)
                for b in range(2):
                    pool.wait_ge(a.stored[b], 16 * NP * (a.lay(l) + 1))
                pool.wait_ge(a.s_saved, 64 * (a.lay(l) + 1))
                settled(pool)
                gate(pool, l, a.stage)
            with pool.Fori(0, NP) as i:
                for b in range(2):
                    t = 2 * i + b
                    pool.wait_ge(y_ready, made(1, l * NT + t + 1))
                    settled(pool)
                    pool.dma_start(streams[bass.ds(l + 1, 1), tok(t), :].rearrange("a p n -> p (a n)"), y_t[:, b]
                                   ).then_inc(y_stored[b], 16)
            for b in range(2):
                pool.wait_ge(y_stored[b], 16 * (l + 1) * NP)
            settled(pool)
            gate(pool, l, OUTPUT)

    @block.tensor
    def _(pe):
        pe.wait_ge(consts_in, 48)
        pe.sem_inc(wa_used, AHEAD)
        pe.sem_inc(x_turned, AHEAD)
        pe.sem_inc(proj_done, AHEAD * NG)
        pe.sem_inc(mx_turned, AHEAD)
        pe.sem_inc(y_done, AHEAD)
        for name in (win.k_turned, win.q_turned, win.s_done, win.p_turned, win.pv_done):
            pe.sem_inc(name, AHEAD)
        for name in (ret.bkv_done, ret.kv_done):
            pe.sem_inc(name, AHEAD)
        for name in (ret.turned, ret.p_done, ret.o_done, hg.x_ready, hg.f_turned):
            pe.sem_inc(name, AHEAD)
        for name in (hg.p_done, hg.o_done):
            pe.sem_inc(name, AHEAD * HEADS)
        pe.sem_inc(hg.e_done, AHEAD * 8)
        pe.wait_ge(setup, SETUP_DVE)
        with pe.Fori(0, DEPTH) as l:
            for n in range(KC):
                pe.wait_ge(wa_in[n % 2], 16 * (l * (KC // 2) + n // 2 + 1))
                for j in range(3):
                    at = 3 * n + j
                    for k in range(KC):
                        last = nc.tensor.matmul(ps[:, 0, 2 * at:2 * at + 2], wa[:, n % 2, k, j * P:(j + 1) * P],
                                                cond[:, k, :], start=(k == 0), stop=(k == KC - 1))
                last.then_inc(wa_used, 1)
            gate(pe, l, MODULATE)

            def turn_x(i, b, c):
                u = l * NT + 2 * i + b
                pe.wait_ge(x_normed, made(1, u + 1))
                pe.wait_ge(h_act, made(1, u - 1))
                pe.wait_ge(h_dve, made(1, u - 1))
                for k in range(KC):
                    last = nc.tensor.transpose(ps[:, 2 * b + k // 4, (k % 4) * P:(k % 4 + 1) * P],
                                               xt[:, b, k * P:(k + 1) * P], ident[:, :])
                last.then_inc(x_turned, 1)

            def project(i, b, c, following):
                u = l * NT + 2 * i + b
                pe.wait_ge(h_act, made(1, u + 1))
                pe.wait_ge(h_dve, made(1, u + 1))
                for g in range(NG):
                    pe.wait_ge(w_loaded[g], (32 if g == NG - 1 else 16) * (l + 1))
                    if g < 4:
                        pe.wait_ge(out_g[g + 4], made(1, u))
                    else:
                        pe.wait_ge(out_g[g - 4], made(1, u + 1))
                    for k in range(KC):
                        last = nc.tensor.matmul(ps[:, 4 + g % 4, :], hT[:, b, k, :], w_sb[:, k, g * GRP:(g + 1) * GRP],
                                                start=(k == 0), stop=(k == KC - 1))
                    last.then_inc(proj_done, 1)
                    if g == TURN_AFTER and following:
                        turn_x(*following)

            woven(pe, turn_x, nothing, project)
            gate(pe, l, PROJECT)
            for a in (win, nei):
                with pe.Fori(0, SLOT_N // 2) as i:
                    for b in range(2):
                        u, v = l * SLOT_N + 2 * i + b, a.lay(l) * SLOT_N + 2 * i + b
                        if a is win:
                            pe.wait_ge(a.k_rot, made(1, u + 1))
                        else:
                            pe.wait_ge(a.k_in[b], 16 * (l * (SLOT_N // 2) + i + 1))
                        pe.wait_ge(a.k_out, made(1, v - 1))
                        settled(pe)
                        src = a.k_rope if a is win else a.k_raw
                        for h in range(a.nkv):
                            last = nc.tensor.transpose(ps[0:HD, b, h * P:(h + 1) * P], src[:, b, h * HD:(h + 1) * HD], ident[:, :])
                        last.then_inc(a.k_turned, 1)
                pe.wait_ge(a.k_out, made(1, (a.lay(l) + 1) * SLOT_N))
                for b in range(2):
                    pe.wait_ge(a.v_in[b], 16 * (a.lay(l) + 1) * (SLOT_N // 2))
                settled(pe)

                def turn_q(i, b):
                    u, v = l * NT + 2 * i + b, a.lay(l) * NT + 2 * i + b
                    if a is win:
                        pe.wait_ge(a.q_rot, made(1, u + 1))
                    else:
                        pe.wait_ge(a.q_in[b], 16 * (l * NP + i + 1))
                    pe.wait_ge(a.q_ready, made(1, v))
                    if b == 0:
                        pe.wait_ge(a.out_ready, made(1, v))
                    settled(pe)
                    src = a.q_rope if a is win else a.q_raw
                    for h in range(HEADS):
                        last = nc.tensor.transpose(ps[0:HD, 0, h * P:(h + 1) * P], src[:, b, h * HD:(h + 1) * HD], ident[:, :])
                    last.then_inc(a.q_turned, 1)

                def scores(i, b, h, kind, base):
                    x = (a.lay(l) * NT + 2 * i + b) * HEADS + h
                    if h == 0:
                        pe.wait_ge(a.q_ready, made(1, a.lay(l) * NT + 2 * i + b + 1))
                    pe.wait_ge(a.e_ready, made(1, x - 1))
                    settled(pe)
                    q = a.qT[:, b, h, :]
                    s = score_banks(w_par(b, h))
                    kv = h // (HEADS // a.nkv)
                    if kind is None:
                        last = nc.tensor.matmul(s[:, 0:CTX], q, a.kT[:, kv, 0:CTX], start=True, stop=True)
                    else:
                        n = min(a.near * P, GRP)
                        nc.tensor.matmul(s[:, 0:n], q, a.kT[:, kv, bass.ds(base * P, n)], start=True, stop=True)
                        if a.near * P > n:
                            nc.tensor.matmul(s[:, n:a.near * P], q, a.kT[:, kv, bass.ds(base * P + n, a.near * P - n)],
                                             start=True, stop=True)
                        for c in range(CT):
                            at = (a.near + c) * P
                            last = nc.tensor.matmul(s[:, at:at + P], q, a.kT[:, kv, (NT + c) * P:(NT + c + 1) * P],
                                                    start=True, stop=True)
                    last.then_inc(a.s_done, 1)

                def turn_p(i, b, h, kind, base):
                    x = (a.lay(l) * NT + 2 * i + b) * HEADS + h
                    pe.wait_ge(a.e_ready, made(1, x + 1))
                    pe.wait_ge(a.pt_act, made(1, x))
                    pe.wait_ge(a.pt_dve, made(1, x))
                    n = CT if kind is None else a.near + CT
                    cut = n // 2
                    for c in range(n):
                        bank, at = (5, c) if c < cut else (6, c - cut)
                        last = nc.tensor.transpose(ps[:, bank, at * P:(at + 1) * P],
                                                   a.e[:, w_par(b, h), c * P:(c + 1) * P], ident[:, :])
                    last.then_inc(a.p_turned, 1)

                def weigh(i, b, h, kind, base):
                    x = (a.lay(l) * NT + 2 * i + b) * HEADS + h
                    pe.wait_ge(a.pt_act, made(1, x + 1))
                    pe.wait_ge(a.pt_dve, made(1, x + 1))
                    pe.wait_ge(a.out_ready, made(1, a.lay(l) * NT + 2 * i + b - 1))
                    if b == 1:
                        pe.wait_ge(a.q_ready, made(1, a.lay(l) * NT + 2 * i + 2))
                    settled(pe)
                    kv = h // (HEADS // a.nkv)
                    out = ps[:, OUT_BANK[b], h * HD:(h + 1) * HD]
                    near = 0 if kind is None else a.near
                    slots = [base + c for c in range(near)] + [(0 if kind is None else NT) + c for c in range(CT)]
                    for c, slot in enumerate(slots):
                        last = nc.tensor.matmul(out, a.pT[:, w_par(b, h), c, :],
                                                a.v[:, bass.ds(slot, 1), kv * HD:(kv + 1) * HD].rearrange("p a n -> p (a n)"),
                                                start=(c == 0), stop=(c == len(slots) - 1))
                    last.then_inc(a.pv_done, 1)

                attend(pe, a, turn_q, scores, turn_p, weigh)
                gate(pe, l, a.stage)
            def outer(keys, values, bank, b):
                for h in range(HEADS):
                    hp, g = h % 2, h // 2
                    last = nc.tensor.matmul(ps[hp * HD:(hp + 1) * HD, bank, KV_AT + g * HD:KV_AT + (g + 1) * HD],
                                            keys[:, h * HD:(h + 1) * HD], values[:, h * HD:(h + 1) * HD], start=True, stop=True)
                return last

            def back_ret(i, b, c):
                u = l * NT + 2 * i + b
                v = ret.lay(l) * NT + 2 * i + b
                pe.wait_ge(ret.bk_ready, made(1, v + 1))
                pe.wait_ge(ret.bs_ready, made(1, v - 1))
                outer(ret.kd[:, b], ret.braw[:, b, GW:2 * GW], b, b).then_inc(ret.bkv_done, 1)

            backward(pe, back_ret)

            def turn_ret(i, b, c):
                u = l * NT + 2 * i + b
                v = ret.lay(l) * NT + 2 * i + b
                pe.wait_ge(ret.x_ready, made(1, u + 1))
                pe.wait_ge(ret.xT_ready, made(1, v - 1))
                for n in range(4):
                    last = nc.tensor.transpose(ps[:, b, n * P:(n + 1) * P], ret.x[:, b, n * P:(n + 1) * P], ident[:, :])
                last.then_inc(ret.turned, 1)

            def products_ret(i, b, c):
                u = l * NT + 2 * i + b
                v = ret.lay(l) * NT + 2 * i + b
                pe.wait_ge(ret.xT_ready, made(1, v + 1))
                pe.wait_ge(ret.p_ready, made(1, u))
                for h in range(HEADS):
                    hp, g = h % 2, h // 2
                    rows_h = slice(hp * HD, (hp + 1) * HD)
                    last = nc.tensor.matmul(ps[:, 2 + hp, g * P:(g + 1) * P], ret.xT[rows_h, b, 2 + g, :],
                                            ret.xT[rows_h, b, g, :], start=True, stop=True)
                last.then_inc(ret.p_done, 1)
                pe.wait_ge(ret.kf_ready, made(1, v + 1))
                pe.wait_ge(ret.val_in[b], 16 * (ret.lay(l) * NP + i + 1))
                pe.wait_ge(ret.sf_ready, made(1, v))
                outer(ret.kd[:, b], ret.raw[:, b, 2 * GW:3 * GW], 6, b).then_inc(ret.kv_done, 1)
                pe.wait_ge(ret.p_ready, made(1, u + 1))
                pe.wait_ge(ret.qd_ready, made(1, u + 1))
                pe.wait_ge(ret.sb_ready, made(1, v + 1))
                pe.wait_ge(ret.ready, made(1, v))
                for h in range(HEADS):
                    hp, g = h % 2, h // 2
                    rows_h = slice(hp * HD, (hp + 1) * HD)
                    out = ps[:, 4 + hp, g * HD:(g + 1) * HD]
                    nc.tensor.matmul(out, ret.p[:, b, hp, g, :], ret.raw[:, b, 2 * GW + h * HD:2 * GW + (h + 1) * HD],
                                     start=True, stop=False)
                    nc.tensor.matmul(out, ret.qd[rows_h, b, 0, g, :], ret.sf[rows_h, c, g * HD:(g + 1) * HD],
                                     start=False, stop=False)
                    last = nc.tensor.matmul(out, ret.qd[rows_h, b, 1, g, :], ret.sb_at[rows_h, b, g * HD:(g + 1) * HD],
                                            start=False, stop=True)
                last.then_inc(ret.o_done, 1)

            tiles(pe, turn_ret, products_ret)
            gate(pe, l, RET)

            def sums_to_end(a, lf, side, bank):
                nc.tensor.matmul(ps[:, bank, 0:GW], past[:, side, :], lf, start=True, stop=True)
                for g in range(2):
                    last = nc.tensor.matmul(ps[:, bank, GW + g:GW + g + 1], lf[:, g * P:(g + 1) * P], ones[:, :],
                                            start=True, stop=True)
                return last

            def back_hg(i, b, c):
                u = l * NT + 2 * i + b
                v = hg.lay(l) * NT + 2 * i + b
                pe.wait_ge(hg.b_in[b], 48 * (l * NP + i + 1))
                pe.wait_ge(hg.bs_ready, made(1, v - 1))
                sums_to_end(hg, hg.braw[:, b, 0:GW], 1, b).then_inc(hg.turned, 1)
                pe.wait_ge(hg.bk_ready, made(1, v + 1))
                outer(hg.kd[:, b], hg.braw[:, b, GW:2 * GW], b, b).then_inc(hg.bkv_done, 1)

            pe.wait_ge(hg.tab_in, 80 * (l + 1))
            backward(pe, back_hg)

            def turn_hg(i, b, c):
                u = l * NT + 2 * i + b
                v = hg.lay(l) * NT + 2 * i + b
                pe.wait_ge(hg.raw_in[b], 32 * (l * NP + i + 1))
                pe.wait_ge(hg.xT_ready, made(1, v))
                for n, at in enumerate((0, P, 5 * GW, 5 * GW + P, 6 * GW, 6 * GW + P)):
                    last = nc.tensor.transpose(ps[:, n // 4, n % 4 * P:(n % 4 + 1) * P], hg.raw[:, b, at:at + P], ident[:, :])
                last.then_inc(hg.x_ready, 1)
                pe.wait_ge(hg.f_exp, made(1, u))
                sums_to_end(hg, hg.raw[:, b, GW:2 * GW], 0, 6).then_inc(hg.f_turned, 1)
                for d in range(2):
                    for g in range(2):
                        at = GW * (1 + d) + g * P
                        for half in range(2):
                            pe.wait_ge(hg.d_ready, made(8, u) + 4 * d + 2 * g + half - 1)
                            nc.tensor.matmul(ps[:, 2 + half, :], hg.raw[:, b, at:at + P],
                                             sums[:, d, 4 * half:4 * half + 4, :].rearrange("p s n -> p (s n)"),
                                             start=True, stop=True).then_inc(hg.e_done, 1)

            def products_hg(i, b, c):
                u = l * NT + 2 * i + b
                v = hg.lay(l) * NT + 2 * i + b

                def weights(h):
                    hp, g = h % 2, h // 2
                    rows_h = slice(hp * HD, (hp + 1) * HD)
                    if h == 0:
                        pe.wait_ge(hg.qk_ready, made(1, u + 1))
                    pe.wait_ge(hg.p_ready, made(HEADS, u) + h - 1)
                    settled(pe)
                    for blk in range(2):
                        at = slice(blk * 64, (blk + 1) * 64)
                        other = slice((1 - blk) * 64, (2 - blk) * 64)

                        def slot(n):
                            return ps[at, 4 + hp, n * 64:(n + 1) * 64]

                        for lv in range(SLOTS):
                            nc.tensor.matmul(slot(lv), hg.k[rows_h, b, g, lv, at], hg.q[rows_h, b, g, lv, at], start=True, stop=True)
                        nc.tensor.matmul(slot(SLOTS), hg.ks[rows_h, b, g, at], hg.xT[rows_h, b, g, at], start=True, stop=True)
                        last = nc.tensor.matmul(slot(SLOTS + 1), hg.k[rows_h, b, g, LEVELS - 1, at],
                                                hg.q[rows_h, b, g, LEVELS - 1, other], start=True, stop=True)
                    last.then_inc(hg.p_done, 1)

                def weigh(h):
                    hp, g = h % 2, h // 2
                    rows_h = slice(hp * HD, (hp + 1) * HD)
                    if h == 0:
                        pe.wait_ge(hg.gated, made(1, u))
                        pe.wait_ge(hg.kf_ready, made(1, v + 1))
                        pe.wait_ge(hg.val_in[b], 16 * (hg.lay(l) * NP + i + 1))
                        outer(hg.kd[:, b], hg.raw[:, b, 4 * GW:5 * GW], 7, b).then_inc(hg.kv_done, 1)
                        pe.wait_ge(hg.sb_ready, made(1, v + 1))
                        pe.wait_ge(hg.sf_ready, made(1, v))
                    else:
                        pe.wait_ge(hg.o_done, made(HEADS, u) + h)
                    pe.wait_ge(hg.p_ready, made(HEADS, u) + h + 1)
                    out = ps[:, 7, h * HD:(h + 1) * HD]
                    nc.tensor.matmul(out, hg.p[:, h % 2, :], hg.raw[:, b, 4 * GW + h * HD:4 * GW + (h + 1) * HD],
                                     start=True, stop=False)
                    nc.tensor.matmul(out, hg.qx[rows_h, b, g, 0, :], hg.sf[rows_h, c, g * HD:(g + 1) * HD],
                                     start=False, stop=False)
                    nc.tensor.matmul(out, hg.qx[rows_h, b, g, 1, :], hg.sb_at[rows_h, b, g * HD:(g + 1) * HD],
                                     start=False, stop=True).then_inc(hg.o_done, 1)

                for h in range(HEADS + 1):
                    if h < HEADS:
                        weights(h)
                    if h > 0:
                        weigh(h - 1)

            pe.wait_ge(hg.bs_ready, made(1, (hg.lay(l) + 1) * NT))
            settled(pe)
            tiles(pe, turn_hg, products_hg)
            gate(pe, l, HGRN)
            pe.wait_ge(wo_in, 48 * (l + 1))

            def turn_mixed(i, b, c):
                u = l * NT + 2 * i + b
                pe.wait_ge(mx_in[b], 16 * (l * NP + i + 1))
                pe.wait_ge(mT_act, made(1, u - 1))
                pe.wait_ge(mT_dve, made(1, u - 1))
                for k in range(KC):
                    last = nc.tensor.transpose(ps[:, 2 * b + k // 4, (k % 4) * P:(k % 4 + 1) * P],
                                               mx_t[:, b, k * P:(k + 1) * P], ident[:, :])
                last.then_inc(mx_turned, 1)

            def project_out(i, b, c):
                u = l * NT + 2 * i + b
                pe.wait_ge(mT_act, made(1, u + 1))
                pe.wait_ge(mT_dve, made(1, u + 1))
                pe.wait_ge(y_ready, made(1, u - 1))
                for g in range(2):
                    for k in range(KC):
                        last = nc.tensor.matmul(ps[:, 4 + 2 * b + g, :], mT[:, b, k, :], wo_sb[:, k, g * GRP:(g + 1) * GRP],
                                                start=(k == 0), stop=(k == KC - 1))
                last.then_inc(y_done, 1)

            tiles(pe, turn_mixed, project_out)
            gate(pe, l, OUTPUT)

    @block.scalar
    def _(act):
        act.sem_inc(rstd_ready, AHEAD)
        act.sem_inc(h_act, AHEAD)
        act.sem_inc(mT_act, AHEAD)
        act.sem_inc(exp_ready, AHEAD * 5)
        act.sem_inc(ln_out, AHEAD * 2)
        act.sem_inc(yr_ready, AHEAD)
        for g in ACT_GROUPS:
            act.sem_inc(out_g[g], AHEAD)
        for name in (win.k_out, win.q_ready, win.e_ready, win.pt_act):
            act.sem_inc(name, AHEAD)
        for name in (ret.xT_ready, ret.sb_ready, ret.r_ready):
            act.sem_inc(name, AHEAD)
        act.sem_inc(hg.f_exp, AHEAD)
        act.sem_inc(hg.d_ready, AHEAD * 8)
        act.sem_inc(hg.p_ready, AHEAD * HEADS)
        act.wait_ge(consts_in, 48)
        nc.scalar.activation(cond_e[:, :, :], cond[:, :, :], ACT.Exp, scale=-1.0).then_inc(setup_act, 1)
        act.wait_ge(setup, SETUP_LB)
        nc.scalar.activation(lb_raw[:, :, :], lb_raw[:, :, :], ACT.Exp).then_inc(setup_act, 1)
        with act.Fori(0, DEPTH) as l:
            gate(act, l, MODULATE)

            def rstd(x, b, steps, ready, junk):
                steps.mark(nc.scalar.activation(junk, x, ACT.Square, accum_out=stat[:, b, 0:1]))
                steps.wait()
                steps.mark(nc.scalar.activation(stat[:, b, 1:2], stat[:, b, 0:1], ACT.Ln, bias=eps[:, 0:1],
                                                scale=1.0 / D_MODEL))
                steps.wait()
                nc.scalar.activation(stat[:, b, 2:3], stat[:, b, 1:2], ACT.Exp, scale=-0.5).then_inc(ready, 1)

            def x_rstd(i, b, c):
                u = l * NT + 2 * i + b
                steps = Steps(act, act_step, (u + l * NT) * 2)
                act.wait_ge(x_in[b], 16 * (l * NP + i + 1))
                rstd(xt[:, b], b, steps, rstd_ready, sq_junk[:, :])

            def modulated(i, b, c):
                u = l * NT + 2 * i + b
                act.wait_ge(x_turned, made(1, u + 1))
                act.wait_ge(proj_done, made(NG, u - 1))
                for k in range(0, 4):
                    last = nc.scalar.activation(hT[:, b, k, :], ps[:, 2 * b + k // 4, (k % 4) * P:(k % 4 + 1) * P],
                                                ACT.Identity, scale=mod[:, KC + k, c:c + 1], bias=mod[:, k, c:c + 1])
                last.then_inc(h_act, 1)

            def emit(i, b, c, following):
                u = l * NT + 2 * i + b
                if following:
                    x_rstd(*following)
                act.wait_ge(row_stored[b], 16 * (l * NP + i))
                for g in range(NG):
                    if g == TURN_AFTER + 1 and following:
                        modulated(*following)
                    act.wait_ge(proj_done, made(NG, u) + g + 1)
                    bank = ps[:, 4 + g % 4, :]
                    out = row_t[:, b, g * GRP:(g + 1) * GRP]
                    if g in ACT_GROUPS:
                        nc.scalar.activation(out, bank, ACT.Copy).then_inc(out_g[g], 1)
                        continue
                    n = EXP_COLS[g]
                    act.wait_ge(out_g[last_exp[g]], made(1, u + (1 if last_exp[g] < g else 0)))
                    nc.scalar.activation(e_t[:, 0, 0:n], bank[:, 0:n], ACT.Exp, scale=-1.0).then_inc(exp_ready, 1)
                    if g == 6:
                        for j in range(2):
                            act.wait_ge(ln_in, 2 * u + j + 1)
                            nc.scalar.activation(e_t[:, j, :], e_t[:, j, :], ACT.Ln).then_inc(ln_out, 1)

            woven(act, x_rstd, modulated, emit)
            gate(act, l, PROJECT)
            for a in (win, nei):
                with act.Fori(0, SLOT_N // 2) as i:
                    for b in range(2):
                        t = 2 * i + b
                        act.wait_ge(a.k_turned, made(1, a.lay(l) * SLOT_N + t + 1))
                        settled(act)
                        nc.scalar.activation(a.kT[:, :, bass.ds(t * P, P)],
                                             ps[0:HD, b, 0:a.nkv * P].rearrange("p (h n) -> p h n", n=P), ACT.Copy
                                             ).then_inc(a.k_out, 1)

                def take_q(i, b):
                    u, v = l * NT + 2 * i + b, a.lay(l) * NT + 2 * i + b
                    act.wait_ge(a.q_turned, made(1, v + 1))
                    act.wait_ge(a.out_ready, made(1, v - 1))
                    nc.scalar.activation(a.qT[:, b].rearrange("p h n -> p (h n)"), ps[0:HD, 0, :], ACT.Copy,
                                         scale=HD ** -0.5).then_inc(a.q_ready, 1)

                def exps(i, b, h, kind, base):
                    x = (a.lay(l) * NT + 2 * i + b) * HEADS + h
                    e, st, s = a.e[:, w_par(b, h)], a.st[:, b, :, h], score_banks(w_par(b, h))
                    act.wait_ge(a.nm_ready, made(1, x + 1))
                    act.wait_ge(a.p_turned, made(1, x - 1))
                    near = 0 if kind is None else a.near * P
                    if a is win:
                        nc.scalar.activation(st[:, ES:ES + 1], st[:, NM:NM + 1], ACT.Exp, bias=sink[:, h:h + 1])
                    if kind is not None:
                        nc.scalar.activation(e[:, 0:near], a.sl[:, w_par(b, h), :], ACT.Exp, bias=st[:, NM:NM + 1],
                                             accum_out=st[:, D1:D1 + 1])
                    nc.scalar.activation(e[:, near:near + CTX], s[:, near:near + CTX], ACT.Exp, bias=st[:, NM:NM + 1],
                                         accum_out=st[:, D2:D2 + 1]).then_inc(a.e_ready, 1)

                def take_p(i, b, h, kind, base):
                    x = (a.lay(l) * NT + 2 * i + b) * HEADS + h
                    n = CT if kind is None else a.near + CT
                    act.wait_ge(a.p_turned, made(1, x + 1))
                    act.wait_ge(a.pv_done, made(1, x - 1))
                    cut = n // 2
                    nc.scalar.activation(a.pT[:, w_par(b, h), cut:n, :].rearrange("p c n -> p (c n)"),
                                         ps[:, 6, 0:(n - cut) * P], ACT.Copy).then_inc(a.pt_act, 1)

                attend(act, a, take_q, exps, take_p, None)
                gate(act, l, a.stage)
            def norm_stats(a, b, u, v):
                steps = Steps(act, a.n_step, v)
                act.wait_ge(a.var_ready, made(1, v + 1))
                steps.mark(nc.scalar.activation(a.st[:, b, 2], a.st[:, b, 1], ACT.Ln, bias=eps[:, 0:1], scale=1.0 / HD))
                steps.wait()
                nc.scalar.activation(a.st[:, b, 3], a.st[:, b, 2], ACT.Exp, scale=-0.5).then_inc(a.r_ready, 1)

            def state_at(a, i, b, u, v):
                act.wait_ge(a.o_done, made(HEADS if a is hg else 1, u - 1))
                settled(act)
                nc.scalar.activation(a.sb_at[:, b, :], a.sb_all[:, bass.ds(2 * i + b, 1), :].rearrange("p a n -> p (a n)"),
                                     ACT.Copy).then_inc(a.sb_ready, 1)

            act.wait_ge(lg_step, 8 * l + 2)
            nc.scalar.activation(lg_t[:, 1], lg_t[:, 1], ACT.Exp).then_inc(lg_act, 1)
            act.wait_ge(lg_act, 17 * l + 1)
            nc.scalar.activation(lg_t[:, 1], lg_t[:, 1], ACT.Ln, bias=ones[:, 0:1]).then_inc(lg_act, 1)
            act.wait_ge(lg_step, 8 * l + 6)
            nc.scalar.activation(pair_decay[:, :, :], lgp[:, :, :], ACT.Exp, scale=float(P)).then_inc(lg_act, 1)
            for d in range(2):
                nc.scalar.activation(key_decay[:, d], lg[:, d * HEADS:(d + 1) * HEADS], ACT.Exp, scale=dcol[:, d:d + 1]
                                     ).then_inc(lg_act, 1)
                for g in range(2):
                    nc.scalar.activation(row_decay[:, d, g], dtab[:, 4 + d], ACT.Exp, scale=lgp[:, d, g:g + 1]).then_inc(lg_act, 1)
            for h in range(HEADS):
                for d in range(2):
                    act.wait_ge(dm_step, 3 * HEADS * l + 3 * h)
                    nc.scalar.activation(dtmp[:, d], dtab[:, d], ACT.Exp, scale=lg[:, d * HEADS + h:d * HEADS + h + 1]
                                         ).then_inc(lg_act, 1)

            def take_x(i, b, c):
                u = l * NT + 2 * i + b
                v = ret.lay(l) * NT + 2 * i + b
                act.wait_ge(ret.turned, made(1, u + 1))
                act.wait_ge(ret.p_done, made(1, u - 1))
                act.wait_ge(ret.qd_ready, made(1, u - 1))
                nc.scalar.activation(ret.xT[:, b].rearrange("p k n -> p (k n)"), ps[:, b, :], ACT.Copy).then_inc(ret.xT_ready, 1)
                state_at(ret, i, b, u, v)

            def norm_ret(i, b, c):
                u = l * NT + 2 * i + b
                v = ret.lay(l) * NT + 2 * i + b
                norm_stats(ret, b, u, v)

            tiles(act, take_x, norm_ret)
            gate(act, l, RET)

            def decay_back(i, b, c):
                u = l * NT + 2 * i + b
                v = hg.lay(l) * NT + 2 * i + b
                act.wait_ge(hg.turned, u + 1)
                act.wait_ge(hg.bs_ready, made(1, v - 1))
                nc.scalar.activation(hg.ed[:, b], ps[:, b, 0:GW + 2], ACT.Exp).then_inc(hg.ready, 1)

            backward(act, decay_back)

            def take_hg(i, b, c):
                u = l * NT + 2 * i + b
                v = hg.lay(l) * NT + 2 * i + b
                act.wait_ge(hg.x_ready, made(1, u + 1))
                act.wait_ge(hg.p_done, made(HEADS, u - 1))
                nc.scalar.activation(hg.xT[:, b, 0:4].rearrange("p k n -> p (k n)"), ps[:, 0, :], ACT.Copy)
                nc.scalar.activation(hg.xT[:, b, 4:6].rearrange("p k n -> p (k n)"), ps[:, 1, 0:2 * P], ACT.Copy
                                     ).then_inc(hg.xT_ready, 1)
                state_at(hg, i, b, u, v)
                act.wait_ge(hg.f_turned, made(1, u + 1))
                act.wait_ge(hg.sf_ready, made(1, v - 1))
                nc.scalar.activation(hg.ed[:, b], ps[:, 6, 0:GW + 2], ACT.Exp).then_inc(hg.f_exp, 1)
                act.wait_ge(hg.qk_ready, made(1, u))
                for d in range(2):
                    for g in range(2):
                        for half in range(2):
                            act.wait_ge(hg.e_done, made(8, u) + 4 * d + 2 * g + half + 1)
                            nc.scalar.activation(hg.d[:, d, g, 4 * half:4 * half + 4].rearrange("p s n -> p (s n)"),
                                                 ps[:, 2 + half, :], ACT.Exp).then_inc(hg.d_ready, 1)

            def weights_hg(i, b, c):
                u = l * NT + 2 * i + b
                v = hg.lay(l) * NT + 2 * i + b
                for h in range(HEADS):
                    act.wait_ge(hg.tc_ready, made(HEADS, u) + h + 1)
                    act.wait_ge(hg.o_done, made(HEADS, u) + h - 1)
                    for blk in range(2):
                        at, other = slice(blk * 64, (blk + 1) * 64), slice((1 - blk) * 64, (2 - blk) * 64)
                        nc.scalar.activation(hg.p[at, h % 2, at], hg.tc[at, h % 2, :], ACT.Copy)
                        last = nc.scalar.activation(hg.p[at, h % 2, other], ps[at, 4 + h % 2, (SLOTS + 1) * 64:(SLOTS + 2) * 64],
                                                    ACT.Copy)
                    last.then_inc(hg.p_ready, 1)
                norm_stats(hg, b, u, v)

            tiles(act, take_hg, weights_hg)
            gate(act, l, HGRN)

            def turned(i, b, c):
                u = l * NT + 2 * i + b
                act.wait_ge(mx_turned, made(1, u + 1))
                act.wait_ge(y_done, made(1, u - 1))
                nc.scalar.activation(mT[:, b, 0:4, :], ps[:, 2 * b, :].rearrange("p (k n) -> p k n", n=P), ACT.Copy
                                     ).then_inc(mT_act, 1)

            def y_rstd(i, b, c):
                u = l * NT + 2 * i + b
                steps = Steps(act, act_step, (u + (l + 1) * NT) * 2)
                act.wait_ge(y_done, made(1, u + 1))
                act.wait_ge(y_stored[b], 16 * (l * NP + i))
                rstd(ps[:, 4 + 2 * b:6 + 2 * b, :], b, steps, yr_ready,
                     y_t[:, b].rearrange("p (k n) -> p k n", n=GRP))

            tiles(act, turned, y_rstd)
            gate(act, l, OUTPUT)

    @block.vector
    def _(dve):
        dve.sem_inc(x_normed, AHEAD)
        dve.sem_inc(h_dve, AHEAD)
        dve.sem_inc(mT_dve, AHEAD)
        dve.sem_inc(y_ready, AHEAD)
        for g in range(NG):
            if g not in ACT_GROUPS:
                dve.sem_inc(out_g[g], AHEAD)
        for name in (win.k_rot, win.q_rot, win.nm_ready, win.pt_dve, win.out_ready):
            dve.sem_inc(name, AHEAD)
        for name in (ret.bk_ready, ret.bs_ready, ret.kf_ready, ret.sf_ready, ret.var_ready, ret.out_ready):
            dve.sem_inc(name, AHEAD)
        for name in (ret.x_ready, ret.qd_ready, ret.p_ready):
            dve.sem_inc(name, AHEAD)
        dve.sem_inc(ret.ready, AHEAD)
        dve.sem_inc(hg.qk_ready, AHEAD)
        dve.sem_inc(hg.gated, AHEAD)
        dve.sem_inc(hg.tc_ready, AHEAD * HEADS)
        nc.vector.memset(eps[:, :], EPS)
        nc.vector.memset(ones[:, :], 1.0)
        dve.wait_ge(consts_in, 48)
        nc.vector.memset(neg_t[:, :], NEG).then_inc(neg_ready, 1)
        dve.wait_ge(lb_loaded, 16 * DEPTH)
        steps = Steps(dve, setup, 0)
        steps.mark(nc.vector.tensor_tensor(lbd[:, 0], lb_raw[:, 0], lb_raw[:, 1], ALU.max))
        steps.wait()
        for d in range(DEPTH):
            steps.mark(nc.vector.tensor_tensor(lb_raw[:, d], lb_raw[:, d], lbd[:, 0], ALU.subtract))
        assert steps.n == SETUP_LB
        dve.wait_ge(setup_act, 2)
        steps.mark(nc.vector.tensor_tensor(lb_raw[:, 0], lb_raw[:, 0], lb_raw[:, 1], ALU.add))
        steps.mark(nc.vector.tensor_scalar(cond_e[:, :, :], cond_e[:, :, :], 1.0, None, ALU.add))
        steps.wait()
        steps.mark(nc.vector.reciprocal(oml[:, 0], lb_raw[:, 0]))
        steps.mark(nc.vector.reciprocal(cond_e[:, :, :], cond_e[:, :, :]))
        steps.wait()
        steps.mark(nc.vector.tensor_tensor(lbd[:, 1], lb_raw[:, 1], oml[:, 0], ALU.mult))
        steps.mark(nc.vector.memset(lbd[:, 0], 0.0))
        steps.mark(nc.vector.tensor_tensor(cond[:, :, :], cond[:, :, :], cond_e[:, :, :], ALU.mult))
        steps.wait()
        steps.mark(nc.vector.tensor_scalar(lbd[:, :, :], lbd[:, :, :], LB_FLOOR, None, ALU.max))
        steps.wait()
        steps.mark(nc.vector.tensor_scalar(oml[:, :, :], lbd[:, :, :], -1.0, 1.0, ALU.mult, ALU.add))
        assert steps.n == SETUP_DVE, steps.n
        with dve.Fori(0, DEPTH) as l:
            steps = Steps(dve, dve_step, l * DVE_STEPS)
            dve.wait_ge(modw_in, 48 * (l + 1))
            dve.wait_ge(wa_used, made(1, (l + 1) * KC))
            steps.mark(nc.vector.tensor_tensor(
                mod[:, :, :], ps[:, 0, 0:6 * KC].rearrange("p (n c) -> p n c", c=2),
                mod_w[:, 0:3 * KC].unsqueeze(2).broadcast_to([P, 3 * KC, 2]), ALU.add))
            steps.wait()
            steps.mark(nc.vector.tensor_scalar(mod[:, KC:2 * KC, :], mod[:, KC:2 * KC, :], 1.0, None, ALU.add))
            steps.wait()
            nc.vector.tensor_tensor(mod[:, KC:3 * KC, :], mod[:, KC:3 * KC, :],
                                    mod_w[:, 3 * KC:5 * KC].unsqueeze(2).broadcast_to([P, 2 * KC, 2]), ALU.mult
                                    ).then_inc(mod_ready, 1)
            assert steps.n == MOD_STEPS
            gate(dve, l, MODULATE)

            def normed(i, b, c):
                u = l * NT + 2 * i + b
                dve.wait_ge(rstd_ready, made(1, u + 1))
                nc.vector.tensor_scalar(xt[:, b], xt[:, b], stat[:, b, 2:3], None, ALU.mult).then_inc(x_normed, 1)

            def modulated(i, b, c):
                u = l * NT + 2 * i + b
                dve.wait_ge(x_turned, made(1, u + 1))
                dve.wait_ge(proj_done, made(NG, u - 1))
                for k in range(4, KC):
                    last = nc.vector.tensor_scalar(hT[:, b, k, :], ps[:, 2 * b + k // 4, (k % 4) * P:(k % 4 + 1) * P],
                                                   mod[:, KC + k, c:c + 1], mod[:, k, c:c + 1], ALU.mult, ALU.add)
                last.then_inc(h_dve, 1)

            def emit(i, b, c, following):
                u = l * NT + 2 * i + b
                steps = Steps(dve, dve_step, l * DVE_STEPS + MOD_STEPS + (2 * i + b) * EMIT_DVE)
                dve.wait_ge(row_stored[b], 16 * (l * NP + i))
                seen = 0
                for g in range(NG):
                    if g == TURN_AFTER - 1 and following:
                        normed(*following)
                    if g == TURN_AFTER + 1 and following:
                        modulated(*following)
                    if g in ACT_GROUPS:
                        continue
                    bank = ps[:, 4 + g % 4, :]
                    out = row_t[:, b, g * GRP:(g + 1) * GRP]
                    n = EXP_COLS[g]
                    seen += 1
                    dve.wait_ge(exp_ready, made(5, u) + seen)
                    steps.mark(nc.vector.tensor_scalar(e_t[:, 0, 0:n], e_t[:, 0, 0:n], 1.0, None, ALU.add))
                    steps.wait()
                    steps.mark(nc.vector.reciprocal(e_t[:, 0, 0:n], e_t[:, 0, 0:n]))
                    steps.wait()
                    if g != 6:
                        if n < GRP:
                            nc.vector.tensor_copy(out[:, n:], bank[:, n:])
                        nc.vector.tensor_tensor(out[:, 0:n], e_t[:, 0, 0:n], bank[:, 0:n], ALU.mult
                                                ).then_inc(out_g[g], 1)
                        continue
                    steps.mark(nc.vector.tensor_tensor(e_t[:, 0], e_t[:, 0], oml_l[:, :], ALU.mult))
                    steps.wait()
                    steps.mark(nc.vector.tensor_tensor(e_t[:, 2], e_t[:, 0], lbd_l[:, :], ALU.add))
                    steps.wait()
                    nc.vector.tensor_scalar(row_t[:, b, C_KD:C_KD + GRP], e_t[:, 2], -1.0, 1.0, ALU.mult, ALU.add)
                    nc.vector.tensor_scalar(e_t[:, 0], e_t[:, 2], LN_SPLIT, None, ALU.max).then_inc(ln_in, 1)
                    nc.vector.tensor_scalar(e_t[:, 1], e_t[:, 2], LN_SPLIT, 1.0 / LN_SPLIT, ALU.min, ALU.mult
                                            ).then_inc(ln_in, 1)
                    dve.wait_ge(ln_out, made(2, u + 1))
                    nc.vector.tensor_tensor(out, e_t[:, 0], e_t[:, 1], ALU.add).then_inc(out_g[g], 1)
                assert steps.n == EMIT_DVE, steps.n

            nc.vector.tensor_copy(lbd_l[:, :], lbd[:, bass.ds(l, 1), :].rearrange("p a n -> p (a n)"))
            nc.vector.tensor_copy(oml_l[:, :], oml[:, bass.ds(l, 1), :].rearrange("p a n -> p (a n)")
                                  ).then_inc(bounds_ready, 1)
            dve.wait_ge(bounds_ready, l + 1)
            woven(dve, normed, modulated, emit)
            gate(dve, l, PROJECT)
            def rope(steps, dst, src, tab, tmp, heads):
                nf = HD // 4
                cos = tab[:, 0:HD].unsqueeze(1).broadcast_to([P, heads, HD])
                steps.mark(nc.vector.tensor_tensor(dst.rearrange("p (h n) -> p h n", n=HD),
                                                   src.rearrange("p (h n) -> p h n", n=HD), cos, ALU.mult))
                for s in range(2):
                    x = src.rearrange("p (h f s n) -> p h f s n", f=2, s=2, n=nf)[:, :, :, 1 - s, :]
                    y = tmp.rearrange("p (h f s n) -> p h f s n", f=2, s=2, n=nf)[:, :, :, s, :]
                    sin = tab[:, HD:2 * HD].rearrange("p (f s n) -> p f s n", f=2, s=2)[:, :, s, :].unsqueeze(1)
                    steps.mark(nc.vector.tensor_tensor(y, x, sin.broadcast_to([P, heads, 2, nf]), ALU.mult))
                steps.wait()
                return nc.vector.tensor_tensor(dst, dst, tmp, ALU.add)

            for a in (win, nei):
                if a is win:
                    with dve.Fori(0, SLOT_N // 2) as i:
                        for b in range(2):
                            u, v = l * SLOT_N + 2 * i + b, a.lay(l) * SLOT_N + 2 * i + b
                            steps = Steps(dve, a.r_step, (l * (SLOT_N + NT) + 2 * i + b) * 3)
                            dve.wait_ge(a.k_in[b], 32 * (l * (SLOT_N // 2) + i + 1))
                            dve.wait_ge(a.k_turned, made(1, v - 1))
                            dve.wait_ge(a.k_rot, made(1, u))
                            rope(steps, a.k_rope[:, b], a.k_raw[:, b], a.rope_t[:, b], a.rot_tmp[:, 0:2 * HD], 2
                                 ).then_inc(a.k_rot, 1)
                    dve.wait_ge(a.k_rot, made(1, (l + 1) * SLOT_N))
                    dve.wait_ge(mask_in, 32 * (l + 1))
                else:
                    dve.wait_ge(bias_in, 16 * len(BIAS_PARTS) * HEADS * (l + 1))

                def turn(i, b):
                    if a is win:
                        u, v = l * NT + 2 * i + b, a.lay(l) * NT + 2 * i + b
                        steps = Steps(dve, a.r_step, (l * (SLOT_N + NT) + SLOT_N + 2 * i + b) * 3)
                        dve.wait_ge(a.q_in[b], 32 * (l * NP + i + 1))
                        dve.wait_ge(a.q_turned, made(1, v - 1))
                        dve.wait_ge(a.q_rot, made(1, u))
                        rope(steps, a.q_rope[:, b], a.q_raw[:, b], a.rope_q[:, b], a.rot_tmp[:, :], HEADS
                             ).then_inc(a.q_rot, 1)

                def maxima(i, b, h, kind, base):
                    x = (a.lay(l) * NT + 2 * i + b) * HEADS + h
                    seen = (2 * i + b) * HEADS + h
                    ctx_units = CT * HEADS
                    steps = Steps(dve, a.s_step, a.lay(l) * (2 * NT * HEADS - ctx_units)
                                  + (seen if kind is None else 2 * seen - ctx_units))
                    st, s = a.st[:, b, :, h], score_banks(w_par(b, h))
                    near = 0 if kind is None else a.near * P
                    dve.wait_ge(a.s_done, made(1, x + 1))
                    steps.mark(nc.vector.reduce_max(st[:, MX:MX + 1], s[:, near:near + CTX], AX_X))
                    if kind is not None:
                        dve.wait_ge(a.e_ready, made(1, x - 1))
                        mask = win_mask[:, kind, :] if a is win else nei_bias[:, kind, h, :]
                        steps.wait()
                        settled(dve)
                        steps.mark(nc.vector.tensor_tensor_reduce(a.sl[:, w_par(b, h), :], s[:, 0:near], mask, 1.0,
                                                                  st[:, MX:MX + 1], ALU.add, ALU.max, st[:, M2:M2 + 1]))
                    steps.wait()
                    mx = st[:, MX:MX + 1] if kind is None else st[:, M2:M2 + 1]
                    if a is win:
                        nm = nc.vector.tensor_scalar(st[:, NM:NM + 1], mx, sink[:, h:h + 1], -1.0, ALU.max, ALU.mult)
                    else:
                        nm = nc.vector.tensor_scalar(st[:, NM:NM + 1], mx, -1.0, None, ALU.mult)
                    nm.then_inc(a.nm_ready, 1)

                def take_p(i, b, h, kind, base):
                    x = (a.lay(l) * NT + 2 * i + b) * HEADS + h
                    n = CT if kind is None else a.near + CT
                    dve.wait_ge(a.p_turned, made(1, x + 1))
                    dve.wait_ge(a.pv_done, made(1, x - 1))
                    cut = n // 2
                    nc.vector.tensor_copy(a.pT[:, w_par(b, h), 0:cut, :].rearrange("p c n -> p (c n)"),
                                          ps[:, 5, 0:cut * P]).then_inc(a.pt_dve, 1)

                def finish(i, b, h, kind, base):
                    if h < HEADS - 1:
                        return
                    u, v = l * NT + 2 * i + b, a.lay(l) * NT + 2 * i + b
                    marks = 4 if a is win else 3
                    steps = Steps(dve, a.f_step, u * marks)
                    st = a.st[:, b]
                    dve.wait_ge(a.pv_done, made(1, (v + 1) * HEADS))
                    if kind is None:
                        steps.mark(nc.vector.tensor_copy(st[:, DN], st[:, D2]))
                    else:
                        steps.mark(nc.vector.tensor_tensor(st[:, DN], st[:, D1], st[:, D2], ALU.add))
                    steps.wait()
                    if a is win:
                        steps.mark(nc.vector.tensor_tensor(st[:, DN], st[:, DN], st[:, ES], ALU.add))
                        steps.wait()
                    steps.mark(nc.vector.reciprocal(st[:, RD], st[:, DN]))
                    steps.wait()
                    dve.wait_ge(a.stored[b], 16 * (a.lay(l) * NP + i))
                    out = a.out_t[:, b].rearrange("p (h n) -> p h n", n=HD)
                    steps.mark(nc.vector.tensor_tensor(out, ps[:, OUT_BANK[b], 0:GW].rearrange("p (h n) -> p h n", n=HD),
                                                       st[:, RD].unsqueeze(2).broadcast_to([P, HEADS, HD]), ALU.mult))
                    steps.wait()
                    dve.wait_ge(a.gate_in[b], 16 * (a.lay(l) * NP + i + 1))
                    nc.vector.tensor_tensor(a.out_t[:, b], a.out_t[:, b], a.gate_t[:, b], ALU.mult).then_inc(a.out_ready, 1)

                attend(dve, a, turn, maxima, take_p, finish)
                gate(dve, l, a.stage)
            def heads_of(x):
                return x.rearrange("p (h n) -> p h n", n=HD)

            def begin_states(a):
                dve.wait_ge(a.s_saved, 64 * a.lay(l))
                nc.vector.memset(a.sf[:, 0, :], 0.0)
                nc.vector.memset(a.sb[:, 0, :], 0.0).then_inc(states_clear, 1)
                dve.wait_ge(states_clear, a.lay(l) + 1)
                dve.wait_ge(a.s_in, 64 * (a.lay(l) + 1))
                settled(dve)

            def back_state(a, steps, i, b, c, bank, decay):
                steps.wait()
                dve.wait_ge(a.bs_ready, made(1, a.lay(l) * NT + 2 * i + b))
                settled(dve)
                steps.mark(nc.vector.tensor_copy(a.sb_all[:, bass.ds(back_tile(i, b), 1), :].rearrange("p a n -> p (a n)"),
                                                 a.sb[:, c, :]))
                dve.wait_ge(a.bkv_done, made(1, a.lay(l) * NT + 2 * i + b + 1))
                steps.wait()
                for g in range(2):
                    at = slice(g * HD, (g + 1) * HD)
                    last = nc.vector.scalar_tensor_tensor(a.sb[:, c, at], a.sb[:, c, at], decay(g),
                                                          ps[:, bank, KV_AT + g * HD:KV_AT + (g + 1) * HD], ALU.mult, ALU.add)
                last.then_inc(a.bs_ready, 1)

            def forward_state(a, u, v, c, decay):
                dve.wait_ge(a.kv_done, made(1, v + 1))
                dve.wait_ge(a.o_done, made(HEADS if a is hg else 1, u + 1))
                dve.wait_ge(a.sf_ready, made(1, v))
                for g in range(2):
                    at = slice(g * HD, (g + 1) * HD)
                    last = nc.vector.scalar_tensor_tensor(a.sf[:, c, at], a.sf[:, c, at], decay(g),
                                                          ps[:, 7 if a is hg else 6, KV_AT + g * HD:KV_AT + (g + 1) * HD],
                                                          ALU.mult, ALU.add)
                last.then_inc(a.sf_ready, 1)

            def scaled_ret(i, b):
                v = ret.lay(l) * NT + 2 * i + b
                dve.wait_ge(ret.r_ready, made(1, v + 1))
                dve.wait_ge(ret.val_in[b], 16 * (ret.lay(l) * NP + i + 1))
                dve.wait_ge(ret.stored[b], 16 * (ret.lay(l) * NP + i))
                steps = Steps(dve, ret.b_step, l * NT * 6 + NT * 5 + 2 * i + b)
                steps.mark(nc.vector.tensor_tensor(heads_of(ret.out_t[:, b]), heads_of(ret.o_c[:, b]),
                                                   ret.st[:, b, 3].unsqueeze(2).broadcast_to([P, HEADS, HD]), ALU.mult))
                steps.wait()
                nc.vector.tensor_tensor(ret.out_t[:, b], ret.out_t[:, b], ret.raw[:, b, 3 * GW:4 * GW], ALU.mult
                                        ).then_inc(ret.out_ready, 1)

            dve.wait_ge(ret.tab_in, 144 * (l + 1))
            dve.wait_ge(lg_step, 8 * l)
            nc.vector.tensor_scalar(lg_t[:, 0], lg[:, :], -1.0, None, ALU.mult).then_inc(lg_step, 1)
            dve.wait_ge(lg_step, 8 * l + 1)
            nc.vector.tensor_tensor(lg_t[:, 1], lg_t[:, 0], lg[:, :], ALU.min).then_inc(lg_step, 1)
            dve.wait_ge(lg_act, 17 * l + 2)
            nc.vector.tensor_scalar(lg_t[:, 2], lg[:, :], 0.0, None, ALU.min).then_inc(lg_step, 1)
            dve.wait_ge(lg_step, 8 * l + 3)
            nc.vector.tensor_tensor(lg[:, :], lg_t[:, 2], lg_t[:, 1], ALU.subtract).then_inc(lg_step, 1)
            dve.wait_ge(lg_step, 8 * l + 4)
            for hp in range(2):
                at = slice(hp * HD, (hp + 1) * HD)
                nc.vector.tensor_copy(lgp[at, :, :], lg[at, :].rearrange("p (d g h) -> p d g h", d=2, g=2)[:, :, :, hp]
                                      ).then_inc(lg_step, 1)
            dve.wait_ge(lg_act, 17 * l + 9)
            nc.vector.tensor_scalar(key_decay[:, :, :], key_decay[:, :, :], HD ** -0.5, None, ALU.mult).then_inc(lg_step, 1)
            for h in range(HEADS):
                dve.wait_ge(lg_act, 17 * l + 9 + 2 * (h + 1))
                nc.vector.tensor_tensor(dtmp[:, 0], dtmp[:, 0], dtab[:, 2], ALU.mult).then_inc(dm_step, 1)
                nc.vector.tensor_tensor(dtmp[:, 1], dtmp[:, 1], dtab[:, 3], ALU.mult).then_inc(dm_step, 1)
                dve.wait_ge(dm_step, 3 * HEADS * l + 3 * h + 2)
                nc.vector.tensor_tensor(dmat[:, h % 2, h // 2], dtmp[:, 0], dtmp[:, 1], ALU.add).then_inc(dm_step, 1)
            dve.wait_ge(dm_step, 3 * HEADS * (l + 1))
            nc.vector.memset(lg_t[:, 0], 0.0).then_inc(lg_step, 1)
            dve.wait_ge(lg_step, 8 * (l + 1))
            begin_states(ret)

            def back_ret(i, b, c):
                u = l * NT + 2 * i + b
                v = ret.lay(l) * NT + 2 * i + b
                steps = Steps(dve, ret.b_step, l * NT * 6 + (2 * i + b) * 5)
                dve.wait_ge(ret.b_in[b], 32 * (l * NP + i + 1))
                dve.wait_ge(ret.bkv_done, made(1, v - 1))
                steps.wait()
                steps.mark(rope(steps, ret.x[:, b, 0:GW], ret.braw[:, b, 0:GW], ret.rope_b[:, b], ret.tmp[:, 0:GW], HEADS))
                steps.wait()
                nc.vector.tensor_tensor(heads_of(ret.kd[:, b]), heads_of(ret.x[:, b, 0:GW]),
                                        key_decay[:, 1].unsqueeze(2).broadcast_to([P, HEADS, HD]), ALU.mult
                                        ).then_inc(ret.bk_ready, 1)
                back_state(ret, steps, i, b, c, b, lambda g: pair_decay[:, 1, g:g + 1])

            backward(dve, back_ret)

            def rope_ret(i, b, c):
                u = l * NT + 2 * i + b
                v = ret.lay(l) * NT + 2 * i + b
                steps = Steps(dve, ret.x_step, u * 3)
                dve.wait_ge(ret.raw_in[b], 32 * (l * NP + i + 1))
                dve.wait_ge(ret.turned, made(1, u - 1))
                dve.wait_ge(ret.kf_ready, made(1, v))
                steps.wait()
                rope(steps, ret.x[:, b], ret.raw[:, b, 0:2 * GW], ret.rope_t[:, b], ret.tmp[:, :], 2 * HEADS
                     ).then_inc(ret.x_ready, 1)
                dve.wait_ge(ret.x_ready, made(1, u + 1))
                dve.wait_ge(ret.kv_done, made(1, v - 1))
                nc.vector.tensor_tensor(heads_of(ret.kd[:, b]), heads_of(ret.x[:, b, GW:2 * GW]),
                                        key_decay[:, 0].unsqueeze(2).broadcast_to([P, HEADS, HD]), ALU.mult
                                        ).then_inc(ret.kf_ready, 1)

            def rest_ret(i, b, c):
                u = l * NT + 2 * i + b
                v = ret.lay(l) * NT + 2 * i + b
                steps = Steps(dve, ret.f_step, u * 3)
                if b == 1:
                    scaled_ret(i, 0)
                elif not (isinstance(i, int) and i == 0):
                    scaled_ret(i - 1, 1)
                dve.wait_ge(ret.xT_ready, made(1, v + 1))
                dve.wait_ge(ret.o_done, made(1, u - 1))
                for d in range(2):
                    last = nc.vector.tensor_tensor(ret.qd[:, b, d], ret.xT[:, b, 0:2, :], row_decay[:, d], ALU.mult)
                last.then_inc(ret.qd_ready, 1)
                dve.wait_ge(ret.p_done, made(1, u + 1))
                nc.vector.tensor_tensor(ret.p[:, b].rearrange("p h g n -> p h (g n)"), ps[:, 2:4, 0:2 * P],
                                        dmat[:, :, :, :].rearrange("p h g n -> p h (g n)"), ALU.mult).then_inc(ret.p_ready, 1)
                dve.wait_ge(ret.o_done, made(1, u + 1))
                st = ret.st[:, b]
                o = ps[:, 4:6, 0:2 * HD].rearrange("p a (g n) -> p g a n", n=HD)

                def pairs(x):
                    return x.rearrange("p (g a) -> p g a", a=2)

                steps.mark(nc.vector.reduce_sum(pairs(st[:, 0]), o, AX_X))
                steps.wait()
                steps.mark(nc.vector.tensor_scalar(st[:, 0], st[:, 0], 1.0 / HD, None, ALU.mult))
                steps.wait()
                dve.wait_ge(ret.out_ready, made(1, v - 1))
                nc.vector.tensor_tensor(ret.o_c[:, b].rearrange("p (g a n) -> p g a n", g=2, a=2), o,
                                        pairs(st[:, 0]).unsqueeze(3).broadcast_to([P, 2, 2, HD]), ALU.subtract).then_inc(ret.ready, 1)
                forward_state(ret, u, v, c, lambda g: pair_decay[:, 0, g:g + 1])
                dve.wait_ge(ret.ready, made(1, v + 1))
                dve.wait_ge(ret.var_ready, made(1, v - 1))
                steps.mark(nc.vector.tensor_tensor(ret.o_sq[:, b], ret.o_c[:, b], ret.o_c[:, b], ALU.mult))
                steps.wait()
                nc.vector.reduce_sum(st[:, 1], heads_of(ret.o_sq[:, b]), AX_X).then_inc(ret.var_ready, 1)
                settled(dve)

            tiles(dve, rope_ret, rest_ret)
            scaled_ret(NP - 1, 1)
            gate(dve, l, RET)

            dve.wait_ge(hg.tab_in, 80 * (l + 1))
            begin_states(hg)

            def back_hg(i, b, c):
                u = l * NT + 2 * i + b
                v = hg.lay(l) * NT + 2 * i + b
                steps = Steps(dve, hg.b_step, l * NT * 7 + 2 * i + b)
                dve.wait_ge(hg.ready, made(1, v + 1))
                dve.wait_ge(hg.b_in[b], 48 * (l * NP + i + 1))
                dve.wait_ge(hg.bkv_done, made(1, v - 1))
                nc.vector.tensor_tensor(hg.kd[:, b], hg.ed[:, b, 0:GW], hg.braw[:, b, 2 * GW:3 * GW], ALU.mult
                                        ).then_inc(hg.bk_ready, 1)
                back_state(hg, steps, i, b, c, b, lambda g: hg.ed[:, b, GW + g:GW + g + 1])

            backward(dve, back_hg)

            def decays_hg(i, b, c):
                u = l * NT + 2 * i + b
                v = hg.lay(l) * NT + 2 * i + b
                dve.wait_ge(hg.raw_in[b], 32 * (l * NP + i + 1))
                dve.wait_ge(hg.f_exp, made(1, u + 1))
                dve.wait_ge(hg.kv_done, made(1, v - 1))
                nc.vector.tensor_tensor(hg.kd[:, b], hg.ed[:, b, 0:GW], hg.raw[:, b, 5 * GW:6 * GW], ALU.mult
                                        ).then_inc(hg.kf_ready, 1)
                dve.wait_ge(hg.xT_ready, made(1, v + 1))
                dve.wait_ge(hg.o_done, made(HEADS, u - 1))
                x = hg.xT[:, b]
                nc.vector.tensor_tensor(hg.ks[:, b], x[:, 2:4], x[:, 4:6], ALU.add)
                for d in range(2):
                    dve.wait_ge(hg.d_ready, made(8, u) + 4 * (d + 1))
                    decays = hg.d[:, d]
                    nc.vector.tensor_tensor(hg.qx[:, b, :, d], decays[:, :, LEVELS], x[:, 0:2], ALU.mult)
                    for lv in range(LEVELS):
                        for out, src, half in ((hg.q, x[:, 0:2], 1 - d), (hg.k, x[:, 2 + 2 * d:4 + 2 * d], d)):
                            def part(y):
                                return y.rearrange("p g (m f s) -> p g m f s", f=2, s=2 ** lv)[:, :, :, half, :]
                            last = nc.vector.tensor_tensor(part(out[:, b, :, lv]), part(decays[:, :, lv]), part(src), ALU.mult)
                last.then_inc(hg.qk_ready, 1)

            def scaled_hg(i, b):
                v = hg.lay(l) * NT + 2 * i + b
                dve.wait_ge(hg.r_ready, made(1, v + 1))
                dve.wait_ge(hg.stored[b], 16 * (hg.lay(l) * NP + i))
                nc.vector.tensor_tensor(heads_of(hg.out_t[:, b]), heads_of(hg.o_c[:, b]),
                                        hg.st[:, b, 3].unsqueeze(2).broadcast_to([P, HEADS, HD]), ALU.mult
                                        ).then_inc(hg.out_ready, 1)

            def rest_hg(i, b, c):
                u = l * NT + 2 * i + b
                v = hg.lay(l) * NT + 2 * i + b
                steps = Steps(dve, hg.f_step, l * NT * 7 + NT + (2 * i + b) * 6)
                if b == 1:
                    scaled_hg(i, 0)
                elif not (isinstance(i, int) and i == 0):
                    scaled_hg(i - 1, 1)
                for h in range(HEADS):
                    dve.wait_ge(hg.p_done, made(HEADS, u) + h + 1)
                    dve.wait_ge(hg.tc_ready, made(HEADS, u) + h)
                    n = SLOTS + 1
                    steps.mark(nc.vector.tensor_tensor(hg.w[:, :, :].rearrange("p s n -> p (s n)"), ps[:, 4 + h % 2, 0:n * 64],
                                                       keep[:, :, :].rearrange("p s n -> p (s n)"), ALU.mult))
                    steps.wait()
                    dve.wait_ge(hg.p_ready, made(HEADS, u) + h - 1)
                    nc.vector.tensor_reduce(hg.tc[:, h % 2, :], hg.w[:, :, :].rearrange("p s n -> p n s"), AX_X, ALU.add
                                            ).then_inc(hg.tc_ready, 1)
                forward_state(hg, u, v, c, lambda g: hg.ed[:, b, GW + g:GW + g + 1])
                dve.wait_ge(hg.out_ready, made(1, v - 1))
                dve.wait_ge(hg.var_ready, made(1, v - 1))
                o = ps[:, 7, 0:GW]
                steps.mark(nc.vector.tensor_copy(hg.o_sq[:, b], o))
                nc.vector.tensor_tensor(hg.o_c[:, b], o, hg.raw[:, b, 3 * GW:4 * GW], ALU.mult).then_inc(hg.gated, 1)
                steps.wait()
                steps.mark(nc.vector.tensor_tensor(hg.o_sq[:, b], hg.o_sq[:, b], hg.o_sq[:, b], ALU.mult))
                steps.wait()
                nc.vector.reduce_sum(hg.st[:, b, 1], heads_of(hg.o_sq[:, b]), AX_X).then_inc(hg.var_ready, 1)

            tiles(dve, decays_hg, rest_hg)
            scaled_hg(NP - 1, 1)
            gate(dve, l, HGRN)

            def turned(i, b, c):
                u = l * NT + 2 * i + b
                dve.wait_ge(mx_turned, made(1, u + 1))
                dve.wait_ge(y_done, made(1, u - 1))
                nc.vector.tensor_copy(mT[:, b, 4:8, :], ps[:, 2 * b + 1, :].rearrange("p (k n) -> p k n", n=P)
                                      ).then_inc(mT_dve, 1)

            def residual(i, b, c):
                u = l * NT + 2 * i + b
                steps = Steps(dve, dve_step, l * DVE_STEPS + MOD_STEPS + NT * EMIT_DVE + 2 * i + b)
                y = y_t[:, b].rearrange("p (k n) -> p k n", n=GRP)
                dve.wait_ge(yr_ready, made(1, u + 1))
                dve.wait_ge(xo_in[b], 16 * (l * NP + i + 1))
                steps.mark(nc.vector.scalar_tensor_tensor(
                    y, ps[:, 4 + 2 * b:6 + 2 * b, :], stat[:, b, 2:3], gp_sb[:, c].rearrange("p (k n) -> p k n", n=GRP),
                    ALU.mult, ALU.mult))
                steps.wait()
                nc.vector.tensor_tensor(y_t[:, b], y_t[:, b], xo_t[:, b], ALU.add).then_inc(y_ready, 1)

            dve.wait_ge(wo_in, 48 * (l + 1))
            tiles(dve, turned, residual)
            gate(dve, l, OUTPUT)

    arena.close()


ACT_GROUPS = (0, 2, 4)
TURN_AFTER = 3
EXP_COLS = {1: GW, 3: GW, 5: GRP, 6: GRP, 7: GW}
last_exp = {1: 7, 3: 1, 5: 3, 6: 5, 7: 6}
SETUP_LB, SETUP_DVE, MOD_STEPS = 3, 12, 2
EMIT_DVE = 12
DVE_STEPS = MOD_STEPS + NT * EMIT_DVE + NT


def kernel(**inputs):
    import numpy as _np
    import concourse.bacc as _bacc
    from concourse.bass_utils import run_bass_kernel_spmd as _run

    g = {k: _np.asarray(v) for k, v in inputs.items()}
    arrays = {
        "x_all": _np.concatenate([g["x_prompt"].reshape(CTX, D_MODEL), g["x_sample"].reshape(LAT, D_MODEL)]),
        "cond_in": _np.concatenate([g["c_ctx"].reshape(1, D_MODEL), g["c"].reshape(1, D_MODEL)]),
        "cache_win_k": g["cache_win_k"].reshape(DEPTH, PAST, 2 * HD),
        "cache_win_v": g["cache_win_v"].reshape(DEPTH, PAST, 2 * HD),
        "cache_na_k": g["cache_na_k"].reshape(DEPTH, PAST, GW),
        "cache_na_v": g["cache_na_v"].reshape(DEPTH, PAST, GW),
        "state_ret": g["state_ret"].reshape(DEPTH, 2, HEADS, HD, HD),
        "state_hgrn": g["state_hgrn"].reshape(DEPTH, 2, HEADS, HD, HD),
        "w_ada": g["w_ada"], "b_ada": g["b_ada"], "g_pre": g["g_pre"], "g_post": g["g_post"],
        "w_in": g["w_in"], "w_out": g["w_out"], "attn_sink": g["attn_sink"],
        "na_rpb": g["na_rpb"].reshape(DEPTH, HEADS * 15, 31),
        "ret_decay_logit": g["ret_decay_logit"].reshape(DEPTH, 2 * HEADS),
        "hgrn_lb_logit": g["hgrn_lb_logit"].reshape(DEPTH, 2 * GW),
        "table": TABLE, "rope": ROPE,
    }
    arrays = {k: _np.ascontiguousarray(v) for k, v in arrays.items()}
    nc = _bacc.Bacc("TRN2", target_bir_lowering=False, num_devices=1)
    ins = [nc.dram_tensor(f"in_{k}", v.shape, F32, kind="ExternalInput").ap() for k, v in arrays.items()]
    shapes = {"streams": (DEPTH + 1, NT * P, D_MODEL), "win_k": (DEPTH, CTX, 2 * HD), "win_v": (DEPTH, CTX, 2 * HD),
              "na_k": (DEPTH, CTX, GW), "na_v": (DEPTH, CTX, GW),
              "ret": (DEPTH, 2, HEADS, HD, HD), "hgrn": (DEPTH, 2, HEADS, HD, HD)}
    outs = [nc.dram_tensor(f"out_{k}", s, F32, kind="ExternalOutput").ap() for k, s in shapes.items()]
    build(nc, ins, outs)
    r = _run(nc, [{f"in_{k}": v for k, v in arrays.items()}], core_ids=[0]).results[0]
    y = r["out_streams"][DEPTH]
    return (y[:CTX].reshape(1, CTX, D_MODEL), y[CTX:].reshape(1, LAT, D_MODEL),
            r["out_win_k"].reshape(1, DEPTH, CTX, 2, HD), r["out_win_v"].reshape(1, DEPTH, CTX, 2, HD),
            r["out_na_k"].reshape(1, DEPTH, CTX, HEADS, HD), r["out_na_v"].reshape(1, DEPTH, CTX, HEADS, HD),
            r["out_ret"].reshape(1, DEPTH, 2, HEADS, HD, HD), r["out_hgrn"].reshape(1, DEPTH, 2, HEADS, HD, HD))
```
